# Optimizing a Trainium2 kernel written in Bass

```python
import jax, jax.numpy as jnp
from jax import lax
import numpy as np

D_MODEL = 1024
BATCH = 1
SEQ = 1024
DEPTH = 1
DEC_BATCH = 1
DEC_SEQ = 64
PAST_LEN = 512

CHUNK = 64
QBLOCK = 128
EPS = 1e-6
MLA_HEADS = 8
Q_LORA = 256
KV_LORA = 128
NOPE_DIM = 64
ROPE_DIM = 32
V_DIM = 64
QK_DIM = NOPE_DIM + ROPE_DIM
ATT_WIDTH = MLA_HEADS * V_DIM
ROPE_BASE = 10000.0
GM_HEADS = 8
GM_HEAD_DIM = 64
GM_WIDTH = GM_HEADS * GM_HEAD_DIM
GM_CHUNK = 128
MIX_WIDTH = ATT_WIDTH + GM_WIDTH
IN_COLS = Q_LORA + KV_LORA + ROPE_DIM + 2 * GM_WIDTH
N_GROUPS = 4
EXPERTS_PER_GROUP = 8
N_EXPERTS = N_GROUPS * EXPERTS_PER_GROUP
TOP_K = 2
D_EXPERT = 256
MOE_BLOCK = 128

kernel_name = "hymba_mla_gmlp_hmoe_stream_step"

def rms_norm(x, g):
    xf = x.astype(jnp.float32)
    y = xf * lax.rsqrt(jnp.mean(xf * xf, axis=-1, keepdims=True) + EPS)
    return (y * g.astype(jnp.float32)).astype(x.dtype)

def layer_norm(x, g, b):
    xf = x.astype(jnp.float32)
    mu = jnp.mean(xf, axis=-1, keepdims=True)
    xc = xf - mu
    var = jnp.mean(xc * xc, axis=-1, keepdims=True)
    return (xc * lax.rsqrt(var + EPS) * g.astype(jnp.float32) + b.astype(jnp.float32)).astype(x.dtype)

def rope(x, pos):
    half = ROPE_DIM // 2
    inv = 1.0 / (ROPE_BASE ** (jnp.arange(half, dtype=jnp.float32) / half))
    ang = pos.astype(jnp.float32)[:, None] * inv[None, :]
    cos = jnp.cos(ang)[None, :, None, :]
    sin = jnp.sin(ang)[None, :, None, :]
    xf = x.astype(jnp.float32)
    x1, x2 = xf[..., :half], xf[..., half:]
    return jnp.concatenate([x1 * cos - x2 * sin, x2 * cos + x1 * sin], axis=-1).astype(x.dtype)

def mla_queries(q_lat, pos, lw):
    B, S, _ = q_lat.shape
    q = (rms_norm(q_lat, lw["g_q_lat"]) @ lw["w_uq"]).reshape(B, S, MLA_HEADS, QK_DIM)
    q = rms_norm(q, lw["g_qnorm"])
    return jnp.concatenate([q[..., :NOPE_DIM], rope(q[..., NOPE_DIM:], pos)], axis=-1)

def mla_keys_values(ckv, krope, pos, lw):
    B, K, _ = ckv.shape
    kv = (rms_norm(ckv, lw["g_kv_lat"]) @ lw["w_ukv"]).reshape(B, K, MLA_HEADS, NOPE_DIM + V_DIM)
    k_nope, v = kv[..., :NOPE_DIM], kv[..., NOPE_DIM:]
    k = jnp.concatenate([k_nope, jnp.broadcast_to(krope[:, :, None, :], (B, K, MLA_HEADS, ROPE_DIM))], axis=-1)
    k = rms_norm(k, lw["g_knorm"])
    k = jnp.concatenate([k[..., :NOPE_DIM], rope(k[..., NOPE_DIM:], pos)], axis=-1)
    return k, v

def chunk_causal_attend(q, q_pos, k, v, k_pos):
    s = jnp.einsum("bqhd,bkhd->bhqk", q.astype(jnp.float32), k.astype(jnp.float32)) * (QK_DIM ** -0.5)
    mask = (k_pos[None, :] // CHUNK) <= (q_pos[:, None] // CHUNK)
    s = jnp.where(mask[None, None], s, -jnp.inf)
    p = jax.nn.softmax(s, axis=-1)
    return jnp.einsum("bhqk,bkhd->bqhd", p, v.astype(jnp.float32)).astype(v.dtype)

def mla_attend(q, q_pos, k, v, k_pos):
    B, Q = q.shape[:2]
    if Q <= QBLOCK:
        return chunk_causal_attend(q, q_pos, k, v, k_pos)
    nb = Q // QBLOCK
    qb = jnp.moveaxis(q.reshape(B, nb, QBLOCK, MLA_HEADS, QK_DIM), 1, 0)
    ob = lax.map(lambda a: chunk_causal_attend(a[0], a[1], k, v, k_pos), (qb, q_pos.reshape(nb, QBLOCK)))
    return jnp.moveaxis(ob, 0, 1).reshape(B, Q, MLA_HEADS, V_DIM)

def spatial_gating(u, v, lw):
    B, S, _ = v.shape
    L = min(S, GM_CHUNK)
    n = S // L
    t = jnp.arange(L)
    mask = (t[None, :] // CHUNK) <= (t[:, None] // CHUNK)
    w = jnp.where(mask[None], lw["w_spatial"][:, :L, :L], 0)
    vh = v.reshape(B, n, L, GM_HEADS, GM_HEAD_DIM)
    bias = jnp.transpose(lw["b_spatial"][:, :L])[None, None, :, :, None]
    mixed = jnp.einsum("hts,bnshd->bnthd", w, vh) + bias
    return u * mixed.reshape(B, S, GM_WIDTH)

def token_mixers(h, past_ckv, past_krope, q_pos, k_pos, lw):
    B, S, _ = h.shape
    proj = h @ lw["w_in"]
    o1 = Q_LORA
    o2 = o1 + KV_LORA
    o3 = o2 + ROPE_DIM
    o4 = o3 + GM_WIDTH
    q_lat, ckv_new, krope_new = proj[..., :o1], proj[..., o1:o2], proj[..., o2:o3]
    g_u, g_v = proj[..., o3:o4], proj[..., o4:]
    if past_ckv is None:
        ckv_all, krope_all = ckv_new, krope_new
    else:
        ckv_all = jnp.concatenate([past_ckv.astype(ckv_new.dtype), ckv_new], axis=1)
        krope_all = jnp.concatenate([past_krope.astype(krope_new.dtype), krope_new], axis=1)
    q = mla_queries(q_lat, q_pos, lw)
    k, v = mla_keys_values(ckv_all, krope_all, k_pos, lw)
    att = mla_attend(q, q_pos, k, v, k_pos).reshape(B, S, ATT_WIDTH)
    u = jax.nn.gelu(g_u)
    v_rows = layer_norm(jax.nn.gelu(g_v), lw["g_ln_v"], lw["b_ln_v"])
    gm = spatial_gating(u, v_rows, lw)
    merged = jnp.concatenate([rms_norm(att, lw["g_out_attn"]), rms_norm(gm, lw["g_out_gmlp"])], axis=-1)
    return merged @ lw["w_out"], ckv_new, krope_new, v_rows

def grouped_experts(t, slot_expert, slot_weight, w_gate, w_up, w_down):
    T, D = t.shape
    A = slot_expert.shape[0]
    order = jnp.argsort(slot_expert)
    sorted_e = slot_expert[order]
    counts = jnp.bincount(slot_expert, length=N_EXPERTS)
    padded = (counts + MOE_BLOCK - 1) // MOE_BLOCK * MOE_BLOCK
    pad_end = jnp.cumsum(padded)
    dest = (pad_end - padded)[sorted_e] + jnp.arange(A) - (jnp.cumsum(counts) - counts)[sorted_e]
    n_blocks = -(-A // MOE_BLOCK) + N_EXPERTS
    P = n_blocks * MOE_BLOCK
    row_token = jnp.zeros((P,), jnp.int32).at[dest].set((order // TOP_K).astype(jnp.int32))
    row_weight = jnp.zeros((P,), jnp.float32).at[dest].set(slot_weight[order])
    block_expert = jnp.minimum(jnp.searchsorted(pad_end, jnp.arange(n_blocks) * MOE_BLOCK, side="right"), N_EXPERTS - 1)
    xb = t[row_token].reshape(n_blocks, MOE_BLOCK, D)

    def expert_block(args):
        xblk, e = args
        hid = jax.nn.silu(xblk @ w_gate[e]) * (xblk @ w_up[e])
        return hid @ w_down[e]

    yb = lax.map(expert_block, (xb, block_expert)).reshape(P, D)
    y = jnp.zeros((T, D), jnp.float32).at[row_token].add(yb.astype(jnp.float32) * row_weight[:, None])
    return y.astype(t.dtype)

def hier_moe(h, lw):
    B, S, D = h.shape
    t = h.reshape(B * S, D)
    T = t.shape[0]
    p_group = jax.nn.softmax((t @ lw["w_router_group"] + lw["b_router_group"]).astype(jnp.float32), axis=-1)
    g_prob, g_idx = lax.top_k(p_group, 1)
    logit_e = (t @ lw["w_router_expert"] + lw["b_router_expert"]).astype(jnp.float32)
    logit_e = logit_e.reshape(T, N_GROUPS, EXPERTS_PER_GROUP)
    logit_e = jnp.take_along_axis(logit_e, g_idx[:, :, None], axis=1)[:, 0, :]
    e_prob, e_idx = lax.top_k(jax.nn.softmax(logit_e, axis=-1), TOP_K)
    weight = g_prob * e_prob / jnp.sum(e_prob, axis=-1, keepdims=True)
    expert_id = (g_idx * EXPERTS_PER_GROUP + e_idx).astype(jnp.int32)
    y = grouped_experts(t, expert_id.reshape(-1), weight.reshape(-1), lw["w_gate_e"], lw["w_up_e"], lw["w_down_e"])
    return y.reshape(B, S, D)

def layer(x, c, past_ckv, past_krope, q_pos, k_pos, lw):
    mod = jax.nn.silu(c) @ lw["w_ada"] + lw["b_ada"]
    sh_a, sc_a, gt_a, sh_m, sc_m, gt_m = jnp.split(mod[:, None, :], 6, axis=-1)
    h = rms_norm(x, lw["g_norm_mix"]) * (1 + sc_a) + sh_a
    mix, ckv_new, krope_new, v_rows = token_mixers(h, past_ckv, past_krope, q_pos, k_pos, lw)
    x = x + gt_a * mix
    h = rms_norm(x, lw["g_norm_ffn"]) * (1 + sc_m) + sh_m
    x = x + gt_m * hier_moe(h, lw)
    return x, ckv_new, krope_new, v_rows

def setup_inputs(seed: int = 0) -> dict:
    key = jax.random.key(seed)
    ks = iter(jax.random.split(key, 40))

    def nrm(shape, scale):
        return jax.random.normal(next(ks), shape, jnp.float32) * scale

    def gain(shape):
        return 1.0 + nrm(shape, 0.02)

    L, D = DEPTH, D_MODEL
    return {
        "x_prompt": nrm((BATCH, SEQ, D), 1.0),
        "x_sample": nrm((DEC_BATCH, DEC_SEQ, D), 1.0),
        "cache_ckv": nrm((L, DEC_BATCH, PAST_LEN, KV_LORA), 1.0),
        "cache_krope": nrm((L, DEC_BATCH, PAST_LEN, ROPE_DIM), 1.0),
        "c_prompt": nrm((BATCH, D), 1.0),
        "c_sample": nrm((DEC_BATCH, D), 1.0),
        "w_ada": nrm((L, D, 6 * D), 0.3 * D ** -0.5),
        "b_ada": nrm((L, 6 * D), 0.01),
        "g_norm_mix": gain((L, D)),
        "w_in": nrm((L, D, IN_COLS), D ** -0.5),
        "g_q_lat": gain((L, Q_LORA)),
        "w_uq": nrm((L, Q_LORA, MLA_HEADS * QK_DIM), Q_LORA ** -0.5),
        "g_kv_lat": gain((L, KV_LORA)),
        "w_ukv": nrm((L, KV_LORA, MLA_HEADS * (NOPE_DIM + V_DIM)), KV_LORA ** -0.5),
        "g_qnorm": gain((L, QK_DIM)),
        "g_knorm": gain((L, QK_DIM)),
        "g_ln_v": gain((L, GM_WIDTH)),
        "b_ln_v": nrm((L, GM_WIDTH), 0.02),
        "w_spatial": nrm((L, GM_HEADS, GM_CHUNK, GM_CHUNK), GM_CHUNK ** -0.5),
        "b_spatial": gain((L, GM_HEADS, GM_CHUNK)),
        "g_out_attn": gain((L, ATT_WIDTH)),
        "g_out_gmlp": gain((L, GM_WIDTH)),
        "w_out": nrm((L, MIX_WIDTH, D), MIX_WIDTH ** -0.5),
        "g_norm_ffn": gain((L, D)),
        "w_router_group": nrm((L, D, N_GROUPS), D ** -0.5),
        "b_router_group": nrm((L, N_GROUPS), 0.01),
        "w_router_expert": nrm((L, D, N_EXPERTS), D ** -0.5),
        "b_router_expert": nrm((L, N_EXPERTS), 0.01),
        "w_gate_e": nrm((L, N_EXPERTS, D, D_EXPERT), D ** -0.5),
        "w_up_e": nrm((L, N_EXPERTS, D, D_EXPERT), D ** -0.5),
        "w_down_e": nrm((L, N_EXPERTS, D_EXPERT, D), D_EXPERT ** -0.5),
    }

def reference(x_prompt, x_sample, cache_ckv, cache_krope, c_prompt, c_sample,
              w_ada, b_ada, g_norm_mix, w_in, g_q_lat, w_uq, g_kv_lat, w_ukv, g_qnorm, g_knorm,
              g_ln_v, b_ln_v, w_spatial, b_spatial, g_out_attn, g_out_gmlp, w_out, g_norm_ffn,
              w_router_group, b_router_group, w_router_expert, b_router_expert, w_gate_e, w_up_e, w_down_e):
    seq = x_prompt.shape[1]
    dec_seq = x_sample.shape[1]
    past = cache_ckv.shape[2]
    pos_prompt = jnp.arange(seq)
    pos_sample_q = past + jnp.arange(dec_seq)
    pos_sample_k = jnp.arange(past + dec_seq)

    y_p, y_s = x_prompt, x_sample
    ckv_p_list, krope_p_list, ckv_s_list, krope_s_list, v_s_list = [], [], [], [], []
    for l in range(DEPTH):
        lw = {
            "w_ada": w_ada[l], "b_ada": b_ada[l], "g_norm_mix": g_norm_mix[l], "w_in": w_in[l],
            "g_q_lat": g_q_lat[l], "w_uq": w_uq[l], "g_kv_lat": g_kv_lat[l], "w_ukv": w_ukv[l],
            "g_qnorm": g_qnorm[l], "g_knorm": g_knorm[l], "g_ln_v": g_ln_v[l], "b_ln_v": b_ln_v[l],
            "w_spatial": w_spatial[l], "b_spatial": b_spatial[l], "g_out_attn": g_out_attn[l],
            "g_out_gmlp": g_out_gmlp[l], "w_out": w_out[l], "g_norm_ffn": g_norm_ffn[l],
            "w_router_group": w_router_group[l], "b_router_group": b_router_group[l],
            "w_router_expert": w_router_expert[l], "b_router_expert": b_router_expert[l],
            "w_gate_e": w_gate_e[l], "w_up_e": w_up_e[l], "w_down_e": w_down_e[l],
        }
        y_p, ckv_p, krope_p, _ = layer(y_p, c_prompt, None, None, pos_prompt, pos_prompt, lw)
        y_s, ckv_s, krope_s, v_s = layer(y_s, c_sample, cache_ckv[l], cache_krope[l], pos_sample_q, pos_sample_k, lw)
        ckv_p_list.append(ckv_p)
        krope_p_list.append(krope_p)
        ckv_s_list.append(ckv_s)
        krope_s_list.append(krope_s)
        v_s_list.append(v_s)

    new_ckv_prompt = jnp.stack(ckv_p_list)
    new_krope_prompt = jnp.stack(krope_p_list)
    new_ckv_sample = jnp.stack(ckv_s_list)
    new_krope_sample = jnp.stack(krope_s_list)
    new_gmlp_v_sample = jnp.stack(v_s_list)
    return (y_p, y_s, new_ckv_prompt, new_krope_prompt, new_ckv_sample, new_krope_sample, new_gmlp_v_sample)


_drawn_inputs = setup_inputs


def setup_inputs(seed=0):
    import zlib

    import numpy as np

    out = dict(_drawn_inputs(seed))
    spreads = {}
    factors = {'b_ada': 3.529,
     'g_q_lat': 8.0,
     'g_kv_lat': 7.297,
     'g_qnorm': 8.0,
     'g_knorm': 8.0,
     'g_ln_v': 2.8,
     'b_ln_v': 2.97,
     'b_spatial': 8.0,
     'g_out_attn': 8.0,
     'g_out_gmlp': 8.0,
     'g_norm_ffn': 8.0,
     'b_router_group': 8.0,
     'b_router_expert': 8.0}
    for name, (base, spread) in spreads.items():
        noise = np.random.default_rng([zlib.crc32(name.encode()), seed]).standard_normal(out[name].shape)
        drawn = base * np.exp(spread * noise) if base else spread * noise
        out[name] = __import__('jax').numpy.asarray(drawn.astype(out[name].dtype))
    for name, factor in factors.items():
        out[name] = (out[name] * factor).astype(out[name].dtype)
    return out
```

```python
from contextlib import ExitStack

import numpy as np

import concourse.bass as bass
from concourse import mybir

F32 = mybir.dt.float32
BF16 = mybir.dt.bfloat16
I32 = mybir.dt.int32
U32 = mybir.dt.uint32
ALU = mybir.AluOpType
ACT = mybir.ActivationFunctionType
AXX = mybir.AxisListType.X

P = 128
D = 1024
KD = D // P
NT = 8
SEQ = NT * P
DEC = 64
TOK = SEQ + DEC
PAST = 512
NC_ = PAST // P
H = 8
QL, KVL, RD, ND, VD = 256, 128, 32, 64, 64
QK = ND + RD
LAT = QL + KVL + RD
GW = 512
EPS = 1e-6
NG, EG = 4, 8
NE = NG * EG
DE = 256
MAXOV = (2 * TOK) // P - 1
NB = NE + MAXOV
YROWS = NB * P
ADA_COLS = 256
ADA_CHUNKS = 6 * D // ADA_COLS
NEG = -1e30
ROWS = [P] * NT + [DEC]
SAMPLE = NT
KEYROW = [P * t for t in range(NT)] + [SEQ + PAST] + [SEQ + P * c for c in range(NC_)]
KEYROWS = SEQ + PAST + DEC


class Signal:

    def __init__(self, sem):
        self.sem, self.n = sem, 0


class Serial:

    def __init__(self, eng, step):
        self.eng, self.step = eng, step
        self.off = 0

    def __call__(self, ins, signal=None):
        s = signal or self.step
        s.n += 1
        ins.then_inc(s.sem, 1)
        self.eng.wait_ge(s.sem, s.n + (self.off if s is self.step else 0))


class Banks:

    def __init__(self, tiles, filled, freed, order):
        self.tiles, self.filled, self.freed = tiles, filled, freed
        self.at, total, uses = {}, [0] * len(tiles), [0] * len(tiles)
        for n, (tag, readers) in enumerate(order):
            b = n % len(tiles)
            assert tag not in self.at, tag
            self.at[tag] = (b, uses[b], total[b])
            uses[b] += 1
            total[b] += readers
        self.total = total

    def claim(self, pe, tag):
        b, _, before = self.at[tag]
        if before:
            pe.wait_ge(self.freed[b], before)
        return self.tiles[b]

    def full(self, ins, tag):
        ins.then_inc(self.filled[self.at[tag][0]], 1)

    def read(self, eng, tag):
        b, use, _ = self.at[tag]
        eng.wait_ge(self.filled[b], use + 1)
        return self.tiles[b]

    def free(self, tag):
        return self.freed[self.at[tag][0]]


def build(nc, a, o):
    with ExitStack() as ctx:
        build_in(nc, a, o, ctx)


def build_in(nc, a, o, ctx):
    def sem(name):
        return nc.alloc_semaphore(name)

    cursor = [(nc.sbuf_base + 63) // 64 * 64]

    def sb(name, shape, dt=F32):
        n = int(np.prod(shape[1:])) * (2 if dt == BF16 else 4)
        t = nc.alloc_sbuf_tensor_at(name, list(shape), dt, offset=cursor[0])
        cursor[0] += (n + 31) // 32 * 32
        assert cursor[0] <= nc.sbuf_usable_end, (name, cursor[0])
        return t

    w = {k: a[k] for k in a}
    x_rows = [w["x_prompt"][0, P * t:P * (t + 1), :] for t in range(NT)] + [w["x_sample"][0]]
    y_p, y_s, ckv_p, kr_p, ckv_s, kr_s, v_s = o
    y_rows = [y_p[0, P * t:P * (t + 1), :] for t in range(NT)] + [y_s[0]]
    ckv_rows = [ckv_p[0, 0, P * t:P * (t + 1), :] for t in range(NT)] + [ckv_s[0, 0]]
    kr_rows = [kr_p[0, 0, P * t:P * (t + 1), :] for t in range(NT)] + [kr_s[0, 0]]
    q_d = nc.dram_tensor("q_scratch", (TOK, H * QK), F32).ap()
    k_d = nc.dram_tensor("k_scratch", (KEYROWS, H * QK), F32).ap()
    v_d = nc.dram_tensor("v_scratch", (KEYROWS, H * VD), F32).ap()
    gm_d = nc.dram_tensor("gmlp_scratch", (TOK, GW), F32).ap()
    x2_d = nc.dram_tensor("residual_scratch", (TOK, D), F32).ap()
    h2_d = nc.dram_tensor("ffn_input_scratch", (TOK, D), F32).ap()
    yb_d = nc.dram_tensor("expert_rows_scratch", (YROWS, D), F32).ap()
    w_ada, w_in = w["w_ada"][0], w["w_in"][0]

    psum = [nc.alloc_psum_tensor(f"bank{i}", [P, 512], F32) for i in range(8)]

    ident = sb("ident", [P, P])
    vecs = sb("vecs", [P, P])
    vT = sb("vT", [P, P])
    modT = sb("modT", [P, 48, 2])
    logits = sb("logits", [P, NT + 1, NG + NE])
    iota_f = sb("iota_f", [P, P])
    tok_id = sb("tok_id", [P, NT + 1])
    rowtok_i = sb("rowtok_i", [P, NB], I32)
    roww = sb("roww", [P, NB])
    pos_i2 = sb("pos_i2", [P, 2, NT + 1], I32)
    ovf_i = sb("ovf_i", [P, MAXOV + 1], I32)
    tri = sb("tri", [P, P])
    ones = sb("ones", [P, P])
    mhalf = sb("mhalf", [P, H])
    stage_base = cursor[0]
    R_BADA, R_G1, R_G2, R_GQL, R_GKV, R_GOA, R_GOG, R_BSP, R_GQ, R_GK = 0, 48, 56, 64, 66, 67, 71, 75, 83, 84
    NVEC = 85

    W_in = sb("W_in", [P, KD, LAT + 2 * GW])
    W_out = sb("W_out", [P, KD, D])
    keep_out = cursor[0]
    W_uq = sb("W_uq", [P, 2, H * QK])
    W_ukv = sb("W_ukv", [P, H * (ND + VD)])
    c_in = sb("c_in", [P, 2, KD])
    c_act = sb("c_act", [P, KD, 2])
    A1 = sb("A1", [P, KD, 2])
    ada_w = sb("ada_w", [P, 3, KD, ADA_COLS])
    xbuf = sb("xbuf", [P, 2, D])
    xn = sb("xn", [P, D])
    hT = sb("hT", [P, 2, KD, P])
    lat = sb("lat", [P, 2, LAT])
    latn = sb("latn", [P, QL + KVL])
    latT = sb("latT", [P, 3, P])
    u_sb = sb("u_sb", [P, 2, GW])
    gv = sb("gv", [P, GW])
    vrows = sb("vrows", [P, GW])
    qh = sb("qh", [P, H, QK])
    kh = sb("kh", [P, H, QK])
    vh = sb("vh", [P, H, VD])
    gm = sb("gm", [P, GW])
    junk = sb("junk", [P, D])
    junk_v = sb("junk_v", [P, GW])
    zeros = sb("zeros", [P, D])
    cn = sb("cn", [P, NC_, P])
    latT_c = sb("latT_c", [P, NC_, P])
    sq_q = sb("sq_q", [P, H, QK])
    sq_k = sb("sq_k", [P, H, ND])
    rot = sb("rot", [P, H, RD])
    rot2 = sb("rot2", [P, H, RD])
    krot = sb("krot", [P, RD])
    ctmp = sb("ctmp", [P, RD])
    wsp = sb("wsp", [P, H, P])
    wspT = sb("wspT", [P, H, P])
    ln_g = sb("ln_g", [P, GW])
    ln_b = sb("ln_b", [P, GW])
    rope_q = sb("rope_q", [P, NT, 2 * RD])
    rope_k = sb("rope_k", [P, NT, 2 * RD])
    grope = sb("grope", [P, 2, 2 * RD])
    cck = sb("cck", [P, NC_, KVL + RD])
    st = sb("st", [P, 64])

    cursor[0] = keep_out
    kT = sb("kT", [QK, H, SEQ])
    vall = sb("vall", [P, NT, H * VD])
    qbuf = sb("qbuf", [P, 2, H, QK])
    kbuf = sb("kbuf", [P, 2, H, QK])
    qT = sb("qT", [QK, H, P])
    merged = sb("merged", [P, 2, D])
    x_att = sb("x_att", [P, 2, D])
    prob = sb("prob", [P, 2, SEQ])
    probT = sb("probT", [P, 2, NT, P])
    mT = sb("mT", [P, KD, P])
    attn = sb("attn", [P, GW])
    h2 = sb("h2", [P, D])
    h2T = sb("h2T", [P, KD, P])
    gate_a = sb("gate_a", [P, D])
    A2 = sb("A2", [P, D])
    B2 = sb("B2", [P, D])
    assert cursor[0] <= nc.sbuf_usable_end
    cursor[0] = stage_base
    tmp2 = sb("tmp2", [P, D])
    junk2 = sb("junk2", [P, D])
    junk_v2 = sb("junk_v2", [P, GW])
    bc_next = sb("bc_next", [P, 3, D])
    w_r = sb("w_r", [P, KD, NG + NE])
    b_r = sb("b_r", [P, NG + NE])
    st2 = sb("st2", [P, 64])
    gqk = sb("gqk", [P, 1])
    A2T = sb("A2T", [P, KD, 2])
    mask_l = sb("mask_l", [1, P], BF16)
    mask_r = sb("mask_r", [1, DEC], BF16)
    assert cursor[0] <= keep_out - 0, cursor[0]

    cursor[0] = stage_base
    SLOTS = 4
    WG = sb("WG", [P, SLOTS, KD, DE])
    WU = sb("WU", [P, SLOTS, KD, DE])
    WD = sb("WD", [P, SLOTS, 2, D])
    xg = sb("xg", [P, 2, D])
    xT = sb("xT", [P, KD, P])
    sg = sb("sg", [P, DE])
    hid = sb("hid", [P, DE])
    hidT = sb("hidT", [P, 2, P])
    yb = sb("yb", [P, 2, D])
    gi = sb("gi", [P, 2], I32)
    x2b = sb("x2b", [P, 2, D])
    y1b = sb("y1b", [P, 2, D])
    y2b = sb("y2b", [P, 2, D])
    yo = sb("yo", [P, 2, D])
    gate_m = sb("gate_m", [P, 2, D])

    E1 = sb("E1", [P, NT + 1, NE])
    E2 = sb("E2", [P, NT + 1, NE])
    E = sb("E", [P, NT + 1, NE])
    big = sb("big", [P, NT + 1, NE])
    big2 = sb("big2", [P, NT + 1, NE])
    base = sb("base", [P, NT + 1, NE])
    rt = sb("rt", [P, 24, NT + 1, EG])
    cnt = sb("cnt", [P, 8, NE])
    cmp_ = sb("cmp", [P, NE, MAXOV])
    onehot = sb("onehot", [P, 2, P])
    bhot = sb("bhot", [P, 2, 2, NB])
    thr = sb("thr", [P, MAXOV])
    ovf = sb("ovf", [P, MAXOV + 1])
    posf = sb("posf", [P, 2, NT + 1])
    ri = sb("ri", [P, 2, NT + 1], I32)
    bi = sb("bi", [P, 2, NT + 1], I32)
    rf = sb("rf", [P, 2, NT + 1])
    bf = sb("bf", [P, 2, NT + 1])

    s_params = sem("params_loaded")
    s_c = sem("c_loaded")
    s_ada = [sem(f"ada_chunk_loaded{i}") for i in range(3)]
    s_cache = sem("cache_loaded")
    s_wkv = sem("w_ukv_loaded")
    s_wlat = sem("w_in_lat_loaded")
    s_wgu = sem("w_in_gate_loaded")
    s_wgv = sem("w_in_value_loaded")
    s_wuq = sem("w_uq_loaded")
    s_wout = sem("w_out_loaded")
    s_x = [sem(f"x_loaded{i}") for i in range(2)]
    s_id = sem("identity_ready")
    s_vecs = sem("vector_rows_ready")
    s_cact = sem("silu_c_ready")
    s_setup2 = sem("constants_ready")
    s_vec = sem("vectors_loaded")
    s_css = sem("cache_square_sums_ready")
    s_cn = sem("cache_normed")
    s_cT = sem("cache_transposed")
    s_fold1 = sem("gains_folded")
    s_wsp = sem("spatial_weights_ready")
    s_lss = sem("latent_square_sums_ready")
    s_rx = sem("router_exponents_ready")
    s_ry = sem("router_exponentials_ready")
    s_A1 = sem("mix_scale_ready")
    s_adafree = sem("ada_chunk_used")
    s_ss = sem("x_square_sum_ready")
    s_xn = sem("x_normed")
    s_hTa = sem("hT_by_act")
    s_hTv = sem("hT_by_dve")
    s_lat = sem("latents_copied")
    s_latn = sem("latents_normed")
    s_latT = sem("latents_transposed")
    s_proj = sem("projection_done")
    s_sqk = sem("k_squares_ready")
    s_v = sem("v_copied")
    s_u = sem("u_ready")
    s_gv = sem("gelu_v_ready")
    s_vr = sem("v_rows_ready")
    s_sqq = sem("q_squares_ready")
    s_kh = sem("k_ready")
    s_qh = sem("q_ready")
    s_gm = sem("gmlp_ready")
    s_out1 = {k: sem(f"stored_{k}") for k in ("lat0", "lat1", "k", "v", "q", "gm", "vs")}
    f1 = [sem(f"bank_filled{i}") for i in range(8)]
    e1 = [sem(f"bank_freed{i}") for i in range(8)]
    s_end1 = sem("projected")

    s_ms = sem("mean_squares_ready")
    s_rs = sem("reciprocal_roots_ready")
    act_step, dve_step, pool_step = (Signal(sem(f"{n}_step")) for n in ("act", "dve", "pool"))

    order1 = [("vec", 1), ("wsp0", 1), ("wsp1", 1), ("cT", 1)]
    order1 += [(("ada", j), 1) for j in range(8)]
    order1 += [x for c in range(NC_) for x in ((("kv0", 9 + c), 3), (("kv1", 9 + c), 3))]
    order1 += [(("xT0", 0), 1), (("xT1", 0), 1)]
    for t in range(NT + 1):
        order1 += [(("lat", t), 1)]
        if t:
            order1 += [(("kv0", t - 1), 3), (("kv1", t - 1), 3)]
        order1 += [(("u", t), 1), (("latT", t), 1)]
        if t < NT:
            order1 += [(("xT0", t + 1), 1), (("xT1", t + 1), 1)]
        if t:
            order1 += [(("mix", t - 1), 1)]
        order1 += [(("gv", t), 1)]
        if t < NT:
            order1 += [(("ada", 8 + 2 * t), 1), (("ada", 9 + 2 * t), 1)]
        order1 += [(("q0", t), 2), (("q1", t), 2)]
    order1 += [(("kv0", NT), 3), (("kv1", NT), 3), (("mix", NT), 1)]
    b1 = Banks(psum, f1, e1, order1)

    s_ld2 = {k: [sem(f"{k}_reloaded{i}") for i in range(2)] for k in ("q", "k", "gm", "x")}
    s_vl = [sem(f"v_reloaded{i}") for i in range(2)]
    s_wr = sem("router_weights_loaded")
    s_qkT = sem("q_and_k_transposed")
    s_keys = sem("key_tile_consumed")
    s_qused = sem("q_tile_consumed")
    s_S = [sem(f"scores_ready{i}") for i in range(2)]
    s_nmax = sem("row_max_ready")
    s_prob = sem("probabilities_ready")
    s_PT = sem("probabilities_transposed")
    s_O = sem("attention_accumulated")
    s_Ofree = sem("attention_copied")
    s_mrg = sem("merged_ready")
    s_mT = sem("merged_transposed")
    s_y = sem("out_projection_done")
    s_x2 = sem("residual_ready")
    s_x2sq = sem("residual_square_sum_ready")
    s_yfree = sem("out_projection_read")
    s_h2 = sem("ffn_input_ready")
    s_h2T = sem("ffn_input_transposed")
    s_heads = sem("tile_heads_done")
    s_bc = sem("broadcast_rows_ready")
    s_fold = sem("attend_constants_ready")
    s_st2 = {k: sem(f"stored_{k}") for k in ("x2_0", "x2_1", "h2")}
    f2 = [sem(f"ring_filled{i}") for i in range(3)]
    e2 = [sem(f"ring_freed{i}") for i in range(3)]
    s_end2 = sem("attended")

    seq = [SAMPLE] + list(range(NT))
    key_tiles = {SAMPLE: [9 + c for c in range(NC_)] + [SAMPLE]} | {t: [t] for t in range(NT)}

    def kslot(t, kt):
        return t if t < NT else (kt - 9 if kt >= 9 else NC_)

    def nkeys(t):
        return PAST + DEC if t == SAMPLE else P * (t + 1)

    def blocks(t):
        n = nkeys(t)
        return [(b, min(P, n - P * b)) for b in range((n + P - 1) // P)]

    order2 = []
    for s, t in enumerate(seq):
        for kt in key_tiles[t]:
            order2 += [(("kT0", kt), 1), (("kT1", kt), 1)]
        order2 += [(("qT0", t), 1), (("qT1", t), 1)]
        if s < 2:
            order2 += [(("bc", s, j), 1) for j in range(6)]
        if s:
            order2 += [(("mT0", seq[s - 1]), 1), (("mT1", seq[s - 1]), 1)]
        for h in range(H):
            order2 += [(("PT", t, h, j), 1) for j in range((len(blocks(t)) + 3) // 4)]
            if h == 3 and s:
                order2 += [(("h2T0", seq[s - 1]), 1), (("h2T1", seq[s - 1]), 1)]
            if h == 5 and s:
                order2 += [(("rt", seq[s - 1]), 1)]
    last = seq[-1]
    order2 += [(("mT0", last), 1), (("mT1", last), 1), (("h2T0", last), 1), (("h2T1", last), 1), (("rt", last), 1)]
    b2 = Banks([psum[4], psum[5], psum[6]], f2, e2, order2)

    def scores(h):
        return 2 * ((h + 1) % 2)

    s_E = sem("expert_one_hots_ready")
    s_rank = sem("ranks_ready")
    s_hot = [sem(f"slot_one_hots_ready{i}") for i in range(2)]
    s_hotu = sem("slot_one_hots_used")
    s_tabp = sem("tables_summed")
    s_tab = sem("tables_ready")
    s_gmp = sem("gate_rows_filled")
    s_gmr = sem("gate_rows_read")
    s_wd = [sem(f"expert_weights_loaded{i}") for i in range(SLOTS)]
    s_zero = sem("zero_rows_ready")
    s_zst = sem("zero_rows_stored")
    s_idx = sem("gather_index_ready")
    s_xg = [sem(f"tokens_gathered{i}") for i in range(2)]
    s_xTp = sem("tokens_transposed")
    s_xTa = sem("xT_by_act")
    s_xTv = sem("xT_by_dve")
    s_gu = sem("gate_up_done")
    s_sg = sem("silu_ready")
    s_hid = sem("hidden_ready")
    s_hTp = sem("hidden_transposed")
    s_hTc = sem("hidT_ready")
    s_down = sem("down_done")
    s_ya = sem("y_by_act")
    s_yv = sem("y_by_dve")
    s_yst = [sem(f"expert_rows_stored{i}") for i in range(2)]
    s_end4 = sem("experts_done")
    s_x2l = [sem(f"residual_loaded{i}") for i in range(2)]
    s_g1 = [sem(f"slot_rows_gathered{i}") for i in range(2)]
    s_yo = sem("output_tile_ready")
    s_yout = [sem(f"output_stored{i}") for i in range(2)]

    ctx_block = nc.Block()
    block = ctx.enter_context(ctx_block)
    prompt_or_sample = lambda t: 1 if t == SAMPLE else 0

    def bcast(ap, shape):
        return ap.broadcast_to(list(shape))

    key_order = [9 + c for c in range(NC_)] + list(range(NT + 1))

    def store_tail(sp, s):
        t = seq[s]
        R = ROWS[t]
        sp.wait_ge(s_x2, s + 1)
        sp.dma_start(x2_d[P * t:P * t + R], x_att[:R, s % 2]).then_inc(s_st2[f"x2_{s % 2}"], 16)
        sp.wait_ge(s_h2, s + 1)
        sp.dma_start(h2_d[P * t:P * t + R], h2[:R]).then_inc(s_st2["h2"], 16)

    @block.sync
    def _(sp):
        rows = [(R_BADA, w["b_ada"][0].rearrange("(r n) -> r n", n=P), 48), (R_G1, w["g_norm_mix"][0].rearrange("(r n) -> r n", n=P), 8),
                (R_G2, w["g_norm_ffn"][0].rearrange("(r n) -> r n", n=P), 8), (R_GQL, w["g_q_lat"][0].rearrange("(r n) -> r n", n=P), 2),
                (R_GKV, w["g_kv_lat"], 1), (R_GOA, w["g_out_attn"][0].rearrange("(r n) -> r n", n=P), 4),
                (R_GOG, w["g_out_gmlp"][0].rearrange("(r n) -> r n", n=P), 4), (R_BSP, w["b_spatial"][0], 8)]
        sp.dma_start(c_in[:, 0, :], w["c_prompt"][0].rearrange("(p k) -> p k", k=KD)).then_inc(s_c, 16)
        sp.dma_start(c_in[:, 1, :], w["c_sample"][0].rearrange("(p k) -> p k", k=KD)).then_inc(s_c, 16)
        sp.wait_ge(s_vecs, 1)
        for r, src, k in rows:
            sp.dma_start(vecs[r:r + k, :], src).then_inc(s_vec, 16)
        for r, name in ((R_GQ, "g_qnorm"), (R_GK, "g_knorm")):
            sp.dma_start(vecs[r:r + 1, 0:QK], w[name]).then_inc(s_vec, 16)
        ada_src = w_ada.rearrange("(p k) n -> p k n", k=KD)

        def ada(j):
            if j >= 3:
                sp.wait_ge(s_adafree, j - 2)
            sp.dma_start(ada_w[:, j % 3], ada_src[:, :, j * ADA_COLS:(j + 1) * ADA_COLS]).then_inc(s_ada[j % 3], 16)

        for j in range(3):
            ada(j)
        sp.dma_start(W_ukv[:], w["w_ukv"][0]).then_inc(s_wkv, 16)
        sp.dma_start(cck[:, :, 0:KVL], w["cache_ckv"][0, 0].rearrange("(c p) n -> p c n", p=P)).then_inc(s_cache, 16)
        sp.dma_start(cck[:, :, KVL:KVL + RD], w["cache_krope"][0, 0].rearrange("(c p) n -> p c n", p=P)).then_inc(s_cache, 16)
        sp.dma_start(wsp[:], w["w_spatial"][0].rearrange("h t s -> t h s")).then_inc(s_params, 16)
        sp.dma_start(ln_g[:], bcast(w["g_ln_v"], [P, GW])).then_inc(s_params, 16)
        sp.dma_start(ln_b[:], bcast(w["b_ln_v"], [P, GW])).then_inc(s_params, 16)
        sp.dma_start(rope_q[:], w["rope_table"].rearrange("(t p) c -> p t c", p=P)).then_inc(s_params, 16)
        for i, name in enumerate(("g_qnorm", "g_knorm")):
            for to, frm, k in ((0, 0, RD), (RD, RD // 2, RD // 2), (RD + RD // 2, 0, RD // 2)):
                sp.dma_start(grope[:, i, to:to + k], bcast(w[name][:, ND + frm:ND + frm + k], [P, k])).then_inc(s_params, 16)
        for t in range(2):
            sp.dma_start(xbuf[:ROWS[t], t], x_rows[t]).then_inc(s_x[t], 16)
        for j in range(3, 8):
            ada(j)
        win = w_in.rearrange("(k p) n -> p k n", p=P)
        sp.dma_start(W_in[:, :, 0:LAT], win[:, :, 0:LAT]).then_inc(s_wlat, 16)
        sp.dma_start(W_in[:, :, LAT:LAT + GW], win[:, :, LAT:LAT + GW]).then_inc(s_wgu, 16)
        sp.dma_start(W_in[:, :, LAT + GW:], win[:, :, LAT + GW:]).then_inc(s_wgv, 16)
        sp.dma_start(W_uq[:], w["w_uq"][0].rearrange("(k p) n -> p k n", p=P)).then_inc(s_wuq, 16)

        sp.wait_ge(s_zero, 1)
        sp.dma_start(yb_d[NE * P:].rearrange("(j p) n -> p j n", p=P), zeros[:].unsqueeze(1).broadcast_to([P, MAXOV, D])).then_inc(s_zst, 16)

        def store_kv(kt):
            R = P if kt != SAMPLE else DEC
            order = key_order.index(kt) + 1
            sp.wait_ge(s_v, order)
            sp.dma_start(v_d[KEYROW[kt]:KEYROW[kt] + R], vh[:R].rearrange("p h n -> p (h n)")).then_inc(s_out1["v"], 16)
            sp.wait_ge(s_kh, order)
            sp.dma_start(k_d[KEYROW[kt]:KEYROW[kt] + R], kh[:R].rearrange("p h n -> p (h n)")).then_inc(s_out1["k"], 16)

        def store_gm(t):
            R = ROWS[t]
            if t == SAMPLE:
                sp.wait_ge(s_vr, t + 1)
                sp.dma_start(v_s[0, 0], vrows[:R]).then_inc(s_out1["vs"], 16)
            sp.wait_ge(s_gm, t + 1)
            sp.dma_start(gm_d[P * t:P * t + R], gm[:R]).then_inc(s_out1["gm"], 16)

        for c in range(NC_):
            store_kv(9 + c)
        for t in range(NT + 1):
            R = ROWS[t]
            sp.wait_ge(s_lat, t + 1)
            sp.dma_start(ckv_rows[t], lat[:R, t % 2, QL:QL + KVL]).then_inc(s_out1[f"lat{t % 2}"], 16)
            sp.dma_start(kr_rows[t], lat[:R, t % 2, QL + KVL:]).then_inc(s_out1[f"lat{t % 2}"], 16)
            if t < NT:
                ada(8 + 2 * t)
                ada(9 + 2 * t)
            if 1 <= t and t + 1 <= NT:
                sp.wait_ge(s_xn, t)
                sp.dma_start(xbuf[:ROWS[t + 1], (t + 1) % 2], x_rows[t + 1]).then_inc(s_x[(t + 1) % 2], 16)
            if t == 0:
                sp.dma_start(W_out[:], w["w_out"][0].rearrange("(k p) n -> p k n", p=P)).then_inc(s_wout, 16)
            if t:
                store_kv(t - 1)
                store_gm(t - 1)
            sp.wait_ge(s_qh, t + 1)
            sp.dma_start(q_d[P * t:P * t + R], qh[:R].rearrange("p h n -> p (h n)")).then_inc(s_out1["q"], 16)
        store_kv(NT)
        store_gm(NT)
        for k, m in (("lat0", 2 * (NT // 2 + 1)), ("lat1", 2 * (NT // 2)), ("k", NT + 1 + NC_), ("v", NT + 1 + NC_), ("q", NT + 1), ("gm", NT + 1), ("vs", 1)):
            sp.wait_ge(s_out1[k], 16 * m)
        sp.wait_ge(s_zst, 16)
        sp.sem_inc(s_end1, 1)
        sp.wait_ge(s_end1, 4)

        sp.dma_start(w_r[:, :, 0:NG], w["w_router_group"][0].rearrange("(p k) n -> p k n", k=KD)).then_inc(s_wr, 16)
        sp.dma_start(w_r[:, :, NG:], w["w_router_expert"][0].rearrange("(p k) n -> p k n", k=KD)).then_inc(s_wr, 16)
        sp.dma_start(b_r[:, 0:NG], bcast(w["b_router_group"], [P, NG])).then_inc(s_wr, 16)
        sp.dma_start(b_r[:, NG:], bcast(w["b_router_expert"], [P, NE])).then_inc(s_wr, 16)
        nk = 0
        for s, t in enumerate(seq):
            R = ROWS[t]
            for kt in key_tiles[t]:
                r = P if kt != SAMPLE else DEC
                if nk >= 2:
                    sp.wait_ge(s_keys, nk - 1)
                sp.dma_start(kbuf[:r, nk % 2].rearrange("p h n -> p (h n)"), k_d[KEYROW[kt]:KEYROW[kt] + r]).then_inc(s_ld2["k"][nk % 2], 16)
                if s:
                    sp.wait_ge(s_heads, max(1, s - 1))
                sp.dma_start(vall[:r, kslot(t, kt)], v_d[KEYROW[kt]:KEYROW[kt] + r]).then_inc(s_vl[s % 2], 16)
                nk += 1
            if s >= 2:
                sp.wait_ge(s_qused, s - 1)
            sp.dma_start(qbuf[:R, s % 2].rearrange("p h n -> p (h n)"), q_d[P * t:P * t + R]).then_inc(s_ld2["q"][s % 2], 16)
            if s >= 2:
                sp.wait_ge(s_h2, s - 1)
                sp.wait_ge(s_st2[f"x2_{s % 2}"], 16 * (s // 2))
            sp.dma_start(merged[:R, s % 2, GW:], gm_d[P * t:P * t + R]).then_inc(s_ld2["gm"][s % 2], 16)
            sp.dma_start(x_att[:R, s % 2], x_rows[t]).then_inc(s_ld2["x"][s % 2], 16)
            if s >= 1:
                store_tail(sp, s - 1)
        store_tail(sp, len(seq) - 1)
        for i in range(2):
            sp.wait_ge(s_st2[f"x2_{i}"], 16 * len(range(i, len(seq), 2)))
        sp.wait_ge(s_st2["h2"], 16 * len(seq))
        sp.sem_inc(s_end2, 1)
        sp.wait_ge(s_end2, 4)

        def load_expert(e, slot):
            sp.dma_start(WG[:, slot], w["w_gate_e"][0, e].rearrange("(p k) n -> p k n", k=KD)).then_inc(s_wd[slot], 16)
            sp.dma_start(WU[:, slot], w["w_up_e"][0, e].rearrange("(p k) n -> p k n", k=KD)).then_inc(s_wd[slot], 16)
            sp.dma_start(WD[:, slot], w["w_down_e"][0, e].rearrange("(p k) n -> p k n", k=2)).then_inc(s_wd[slot], 16)

        def load_expert_dyn(e, slot):
            sp.dma_start(WG[:, slot], w["w_gate_e"][0, bass.ds(e, 1)].rearrange("o (p k) n -> (o p) k n", k=KD)).then_inc(s_wd[slot], 16)
            sp.dma_start(WU[:, slot], w["w_up_e"][0, bass.ds(e, 1)].rearrange("o (p k) n -> (o p) k n", k=KD)).then_inc(s_wd[slot], 16)
            sp.dma_start(WD[:, slot], w["w_down_e"][0, bass.ds(e, 1)].rearrange("o (p k) n -> (o p) k n", k=2)).then_inc(s_wd[slot], 16)

        def store_y(b, par):
            sp.wait_ge(s_ya, b + 1)
            sp.wait_ge(s_yv, b + 1)
            sp.dma_start(yb_d[bass.ds(b * P, P)] if not isinstance(b, int) else yb_d[b * P:(b + 1) * P], yb[:, par]).then_inc(s_yst[par], 16)

        for e in range(SLOTS):
            load_expert(e, e)
        with sp.Fori(0, (NE - SLOTS) // SLOTS) as i:
            for u in range(SLOTS):
                store_y(i * SLOTS + u, u % 2)
                sp.wait_ge(s_down, i * SLOTS + u + 1)
                load_expert_dyn(i * SLOTS + (SLOTS + u), u)
        for b in range(NE - SLOTS, NE):
            store_y(b, b % 2)
        sp.wait_ge(s_down, NE)
        sp.wait_ge(s_tab, 1)
        n_ov = sp.value_load(ovf_i[0:1, MAXOV:MAXOV + 1], min_val=0, max_val=MAXOV)
        with sp.Fori(0, MAXOV) as j:
            with sp.If(j < n_ov):
                e = sp.value_load(ovf_i[0:1, bass.ds(j, 1)], min_val=0, max_val=NE - 1)
                sp.wait_ge(s_yst[0], j * 16 + NE // 2 * 16)
                load_expert_dyn(e, 0)
                sp.wait_ge(s_ya, j + (NE + 1))
                sp.wait_ge(s_yv, j + (NE + 1))
                sp.dma_start(yb_d[bass.ds(j * P + NE * P, P)], yb[:, 0]).then_inc(s_yst[0], 16)
            with sp.Else():
                sp.nop()
        sp.wait_ge(s_yst[0], n_ov * 16 + NE // 2 * 16)
        sp.wait_ge(s_yst[1], NE // 2 * 16)
        sp.sem_inc(s_end4, 1)

        for t in range(NT + 1):
            R = ROWS[t]
            if t >= 2:
                sp.wait_ge(s_yo, t - 1)
            sp.dma_start(x2b[:R, t % 2], x2_d[P * t:P * t + R]).then_inc(s_x2l[t % 2], 16)
            if t >= 1:
                sp.wait_ge(s_yo, t)
                sp.dma_start(y_rows[t - 1], yo[:ROWS[t - 1], (t - 1) % 2]).then_inc(s_yout[(t - 1) % 2], 16)
        sp.wait_ge(s_yo, NT + 1)
        sp.dma_start(y_rows[NT], yo[:DEC, NT % 2]).then_inc(s_yout[NT % 2], 16)
        for i in range(2):
            sp.wait_ge(s_yout[i], 16 * len(range(i, NT + 1, 2)))

    @block.gpsimd
    def _(g):
        do = Serial(g, pool_step)
        do(g.memset(vecs[:], 0.0))
        g.sem_inc(s_vecs, 1)
        do(g.memset(ident[:], 0.0))
        do(g.affine_select(out=ident[:], in_=ident[:], compare_op=ALU.not_equal, fill=1.0, base=0, pattern=[[-1, P]], channel_multiplier=1))
        g.sem_inc(s_id, 1)
        do(g.iota(iota_f[:], [[1, P]], base=0, channel_multiplier=0, allow_small_or_imprecise_dtypes=True))
        do(g.iota(tok_id[:], [[P, NT + 1]], base=0, channel_multiplier=1, allow_small_or_imprecise_dtypes=True))
        do(g.memset(logits[:], 0.0))
        do(g.memset(tri[:], 1.0))
        do(g.affine_select(out=tri[:], in_=tri[:], compare_op=ALU.is_gt, fill=0.0, base=0, pattern=[[1, P]], channel_multiplier=-1))
        do(g.memset(ones[:], 1.0))
        do(g.memset(mhalf[:], -0.5))
        do(g.memset(zeros[:], 0.0))
        g.sem_inc(s_zero, 1)
        n_roots = 0

        def rstd(dst, src):
            nonlocal n_roots
            n_roots += 1
            g.wait_ge(s_ms, n_roots)
            do(g.tensor_scalar(dst, src, EPS, None, ALU.add))
            g.tensor_tensor(dst, dst, mhalf[:dst.shape[0], 0:dst.shape[1]], ALU.pow).then_inc(s_rs, 1)

        rstd(st[:, 16:20], st[:, 8:12])
        rstd(st[:, 2:3], st[:, 0:1])
        for c in range(NC_):
            rstd(st[:, 32:40], st[:, 32:40])
        for t in range(NT + 1):
            R = ROWS[t]
            rstd(st[:R, 14:16], st[:R, 12:14])
            if t < NT:
                r = ROWS[t + 1]
                n = (t + 1) % 2
                rstd(st[:r, 2 + n:3 + n], st[:r, n:n + 1])
            if t:
                rstd(st[:P, 32:40], st[:P, 32:40])
            if t:
                rstd(st[:P, 41:42], st[:P, 41:42])
            rstd(st[:R, 50:51], st[:R, 49:50])
            rstd(st[:R, 52:60], st[:R, 52:60])
        rstd(st[:DEC, 32:40], st[:DEC, 32:40])
        rstd(st[:DEC, 41:42], st[:DEC, 41:42])
        g.sem_inc(s_end1, 1)
        g.wait_ge(s_end1, 4)
        do(g.memset(mask_l[0:1, :], 0.0))
        do(g.memset(mask_l[0:1, 0:DEC], 1.0))
        do(g.memset(mask_r[0:1, :], NEG))
        g.sem_inc(s_setup2, 1)
        for s, t in enumerate(seq):
            if s:
                r = ROWS[seq[s - 1]]
                rstd(st2[:r, 41:42], st2[:r, 40:41])
            rstd(st2[:ROWS[t], 42:43], st2[:ROWS[t], 42:43])
        rstd(st2[:, 41:42], st2[:, 40:41])
        g.wait_ge(s_tab, 1)

        def gather(b, par, start):
            idx = rowtok_i[:, b:b + 1] if isinstance(b, int) else rowtok_i[:, bass.ds(b, 1)]
            if not start:
                g.wait_ge(s_xTp, b - 1)
            do(g.tensor_copy(gi[:, par:par + 1], idx))
            g.sem_inc(s_idx, 1)
            g.indirect_dma_start(xg[:, par], None, h2_d, bass.IndirectOffsetOnAxis(gi[:, par:par + 1].bitcast(U32), 0)).then_inc(s_xg[par], 16)

        gather(0, 0, True)
        gather(1, 1, True)
        with g.Fori(0, (NE - 2) // 2) as i:
            do.off = i * 2
            for u in range(2):
                gather(i * 2 + (2 + u), u, False)
        do.off = 0
        pool_step.n += (NE - 2) // 2 * 2 - 2
        n_ov = g.value_load(ovf_i[0:1, MAXOV:MAXOV + 1], min_val=0, max_val=MAXOV)
        n0 = pool_step.n
        with g.Fori(0, MAXOV) as j:
            with g.If(j < n_ov):
                g.wait_ge(s_xTp, j + NE)
                g.wait_ge(s_xg[0], j * 16 + 16 * (NE // 2))
                g.tensor_copy(gi[:, 0:1], rowtok_i[:, bass.ds(j + NE, 1)]).then_inc(pool_step.sem, 1)
                g.wait_ge(pool_step.sem, j + (n0 + 1))
                g.sem_inc(s_idx, 1)
                g.indirect_dma_start(xg[:, 0], None, h2_d, bass.IndirectOffsetOnAxis(gi[:, 0:1].bitcast(U32), 0)).then_inc(s_xg[0], 16)
            with g.Else():
                g.nop()
        g.wait_ge(s_end4, 1)
        for t in range(NT + 1):
            R = ROWS[t]
            if t >= 2:
                g.wait_ge(s_yo, t - 1)
            for k, dst in enumerate((y1b, y2b)):
                g.indirect_dma_start(dst[:R, t % 2], None, yb_d, bass.IndirectOffsetOnAxis(pos_i2[:R, k, t:t + 1].bitcast(U32), 0)).then_inc(s_g1[t % 2], 16)

    @block.tensor
    def _(pe):
        mm = nc.tensor.matmul
        tr = lambda out, in_, r: nc.tensor.transpose(out, in_, ident[:r, :r])
        pe.wait_ge(s_id, 1)
        pe.wait_ge(s_vec, 16 * 10)
        ps = b1.claim(pe, "vec")
        b1.full(tr(ps[:, 0:NVEC], vecs[0:NVEC, :], NVEC), "vec")
        pe.wait_ge(s_params, 16 * 10)
        for half in range(2):
            ps = b1.claim(pe, f"wsp{half}")
            for j in range(4):
                ins = tr(ps[:, j * P:(j + 1) * P], wsp[:, 4 * half + j, :], P)
            b1.full(ins, f"wsp{half}")
        pe.wait_ge(s_cn, 1)
        ps = b1.claim(pe, "cT")
        for c in range(NC_):
            ins = tr(ps[:, c * P:(c + 1) * P], cn[:, c, :], P)
        b1.full(ins, "cT")

        def ada(j):
            pe.wait_ge(s_ada[j % 3], 16 * (j // 3 + 1))
            if j == 0:
                pe.wait_ge(s_cact, 1)
            ps = b1.claim(pe, ("ada", j))
            for n in range(ADA_COLS // P):
                for k in range(KD):
                    ins = mm(ps[:, 2 * n:2 * n + 2], ada_w[:, j % 3, k, n * P:(n + 1) * P], c_act[:, k, :], start=(k == 0), stop=(k == KD - 1))
            b1.full(ins, ("ada", j))

        for j in range(8):
            ada(j)

        def kv(kt):
            R = P if kt != SAMPLE else DEC
            lhs = latT_c[:, kt - 9, :] if kt >= 9 else latT[:, 2, :R]
            for half in range(2):
                ps = b1.claim(pe, (f"kv{half}", kt))
                ins = mm(ps[:R, :], lhs, W_ukv[:, half * 512:(half + 1) * 512], start=True, stop=True)
                b1.full(ins, (f"kv{half}", kt))

        pe.wait_ge(s_cT, 1)
        pe.wait_ge(s_fold1, 1)
        for c in range(NC_):
            kv(9 + c)

        def xT_(t):
            R = ROWS[t]
            pe.wait_ge(s_xn, t + 1)
            for half in range(2):
                ps = b1.claim(pe, (f"xT{half}", t))
                for j in range(4):
                    k = 4 * half + j
                    ins = tr(ps[:, j * P:j * P + R], xn[:R, k * P:(k + 1) * P], R)
                b1.full(ins, (f"xT{half}", t))

        def proj(t, name, c0, n):
            R = ROWS[t]
            ps = b1.claim(pe, (name, t))
            for k in range(KD):
                ins = mm(ps[:R, 0:n], hT[:, t % 2, k, :R], W_in[:, k, c0:c0 + n], start=(k == 0), stop=(k == KD - 1))
            b1.full(ins, (name, t))

        def mix(t):
            R = ROWS[t]
            pe.wait_ge(s_vr, t + 1)
            if t == 0:
                pe.wait_ge(s_wsp, 2)
            ps = b1.claim(pe, ("mix", t))
            for h in range(H):
                ins = mm(ps[:R, h * 64:(h + 1) * 64], wspT[:R, h, :R], vrows[:R, h * 64:(h + 1) * 64], start=True, stop=True)
            b1.full(ins, ("mix", t))

        xT_(0)
        for t in range(NT + 1):
            R = ROWS[t]
            pe.wait_ge(s_hTa, t + 1)
            pe.wait_ge(s_hTv, t + 1)
            if t == 0:
                pe.wait_ge(s_wlat, 16)
            proj(t, "lat", 0, LAT)
            if t:
                kv(t - 1)
            if t == 0:
                pe.wait_ge(s_wgu, 16)
            proj(t, "u", LAT, GW)
            pe.wait_ge(s_latn, t + 1)
            ps = b1.claim(pe, ("latT", t))
            for j in range(3):
                ins = tr(ps[:, j * P:j * P + R], latn[:R, j * P:(j + 1) * P], R)
            b1.full(ins, ("latT", t))
            if t < NT:
                xT_(t + 1)
            if t:
                mix(t - 1)
            if t == 0:
                pe.wait_ge(s_wgv, 16)
            proj(t, "gv", LAT + GW, GW)
            if t < NT:
                ada(8 + 2 * t)
                ada(9 + 2 * t)
            pe.wait_ge(s_latT, t + 1)
            if t == 0:
                pe.wait_ge(s_fold1, 2)
            for half in range(2):
                ps = b1.claim(pe, (f"q{half}", t))
                n = H * QK // 2
                for k in range(2):
                    ins = mm(ps[:R, 0:n], latT[:, k, :R], W_uq[:, k, half * n:(half + 1) * n], start=(k == 0), stop=(k == 1))
                b1.full(ins, (f"q{half}", t))
        kv(NT)
        mix(NT)
        pe.wait_ge(s_end1, 4)

        pe.wait_ge(s_fold, 1)
        pe.wait_ge(s_setup2, 1)
        nk, nv = 0, [0, 0]

        def heads(s, t):
            R = ROWS[t]
            n = nkeys(t)
            bl = blocks(t)

            def S(h):
                u = s * H + h
                bank = scores(h)
                if u >= 2:
                    pe.wait_ge(s_prob, u - 1)
                if h == 1 and s:
                    pe.wait_ge(s_x2, s)
                for c0 in range(0, n, 512):
                    m = min(512, n - c0)
                    out = psum[bank + c0 // 512]
                    final = c0 + m == n
                    masked = final and t != SAMPLE
                    ins = mm(out[:R, 0:m], qT[:, h, :R], kT[:, h, c0:c0 + m], start=True, stop=not masked)
                    if masked:
                        ins = mm(out[:R, m - DEC:m], mask_l[0:1, :R], mask_r[0:1, :], start=False, stop=True)
                ins.then_inc(s_S[h % 2], 1)

            def PT(h):
                u = s * H + h
                pe.wait_ge(s_prob, u + 1)
                for j in range((len(bl) + 3) // 4):
                    ps = b2.claim(pe, ("PT", t, h, j))
                    for b, r in bl[4 * j:4 * j + 4]:
                        ins = tr(ps[:r, (b % 4) * P:(b % 4) * P + R], prob[:R, u % 2, b * P:b * P + r], R)
                    b2.full(ins, ("PT", t, h, j))

            def O(h):
                u = s * H + h
                pe.wait_ge(s_PT, u + 1)
                if h == 0 and s:
                    pe.wait_ge(s_Ofree, s)
                for b, r in bl:
                    ins = mm(psum[7][:R, h * VD:(h + 1) * VD], probT[:r, u % 2, b, :R], vall[:r, b, h * VD:(h + 1) * VD],
                             start=(b == 0), stop=(b == len(bl) - 1))
                if h == H - 1:
                    ins.then_inc(s_heads, 1)

            S(0)
            S(1)
            for h in range(H):
                PT(h)
                if h + 2 < H:
                    S(h + 2)
                if h == 3 and s:
                    h2T_(s - 1)
                if h == 5 and s:
                    router(s - 1)
                O(h)

        def mT_(s):
            t = seq[s]
            R = ROWS[t]
            pe.wait_ge(s_mrg, s + 1)
            for half in range(2):
                ps = b2.claim(pe, (f"mT{half}", t))
                for j in range(4):
                    ins = tr(ps[:, j * P:j * P + R], merged[:R, s % 2, (4 * half + j) * P:(4 * half + j + 1) * P], R)
                b2.full(ins, (f"mT{half}", t))

        def out_(s):
            t = seq[s]
            R = ROWS[t]
            pe.wait_ge(s_mT, s + 1)
            pe.wait_ge(s_prob, (s + 1) * H)
            for half in range(2):
                for k in range(KD):
                    ins = mm(psum[half][:R, :], mT[:, k, :R], W_out[:, k, half * 512:(half + 1) * 512], start=(k == 0), stop=(k == KD - 1))
            ins.then_inc(s_y, 1)

        def h2T_(s):
            t = seq[s]
            R = ROWS[t]
            pe.wait_ge(s_h2, s + 1)
            for half in range(2):
                ps = b2.claim(pe, (f"h2T{half}", t))
                for j in range(4):
                    ins = tr(ps[:, j * P:j * P + R], h2[:R, (4 * half + j) * P:(4 * half + j + 1) * P], R)
                b2.full(ins, (f"h2T{half}", t))

        def router(s):
            t = seq[s]
            R = ROWS[t]
            pe.wait_ge(s_h2T, s + 1)
            if s == 0:
                pe.wait_ge(s_wr, 64)
            ps = b2.claim(pe, ("rt", t))
            for k in range(KD):
                ins = mm(ps[:R, 0:NG + NE], h2T[:, k, :R], w_r[:, k, :], start=(k == 0), stop=(k == KD - 1))
            b2.full(ins, ("rt", t))

        for s, t in enumerate(seq):
            R = ROWS[t]
            for kt in key_tiles[t]:
                r = P if kt != SAMPLE else DEC
                pe.wait_ge(s_ld2["k"][nk % 2], 16 * (nk // 2 + 1))
                for half in range(2):
                    ps = b2.claim(pe, (f"kT{half}", kt))
                    for j in range(4):
                        ins = tr(ps[:QK, j * P:j * P + r], kbuf[:r, nk % 2, 4 * half + j, :], r)
                    b2.full(ins, (f"kT{half}", kt))
                nk += 1
            pe.wait_ge(s_ld2["q"][s % 2], 16 * (s // 2 + 1))
            for half in range(2):
                ps = b2.claim(pe, (f"qT{half}", t))
                for j in range(4):
                    ins = tr(ps[:QK, j * P:j * P + R], qbuf[:R, s % 2, 4 * half + j, :], R)
                b2.full(ins, (f"qT{half}", t))
            if s < 2:
                for j in range(6):
                    which, half = j // 2, j % 2
                    ps = b2.claim(pe, ("bc", s, j))
                    for i in range(4):
                        k = 4 * half + i
                        src = (modT[:, 16 + k, 1 - s:2 - s], A2T[:, k, 1 - s:2 - s], modT[:, 24 + k, 1 - s:2 - s])[which]
                        ins = tr(ps[:, i * P:(i + 1) * P], src.broadcast_to([P, P]), P)
                    b2.full(ins, ("bc", s, j))
            if s:
                mT_(s - 1)
                out_(s - 1)
            pe.wait_ge(s_qkT, s + 1)
            nv[s % 2] += len(key_tiles[t])
            pe.wait_ge(s_vl[s % 2], 16 * nv[s % 2])
            heads(s, t)
        s = len(seq) - 1
        mT_(s)
        out_(s)
        h2T_(s)
        router(s)

        pe.wait_ge(s_E, 1)
        flat = E[:].rearrange("p t e -> p (t e)")
        mm(psum[0][:, 0:(NT + 1) * NE], tri[:], flat, start=True, stop=True)
        mm(psum[1][:, 0:(NT + 1) * NE], ones[:], flat, start=True, stop=True).then_inc(s_rank, 1)
        n = 0
        for t in range(NT + 1):
            R = ROWS[t]
            for k in range(2):
                pe.wait_ge(s_hot[n % 2], n // 2 + 1)
                mm(psum[2][:, 0:2 * NB], onehot[:R, n % 2, :], bhot[:R, n % 2].rearrange("p a b -> p (a b)"),
                   start=(n == 0), stop=(n == 2 * NT + 1)).then_inc(s_hotu, 1)
                n += 1
        for v in range(2):
            if v:
                pe.wait_ge(s_gmr, v)
            for half in range(2):
                for i in range(4):
                    k = 4 * half + i
                    ins = tr(psum[4 + half][:, i * P:(i + 1) * P], modT[:, 40 + k, v:v + 1].broadcast_to([P, P]), P)
            ins.then_inc(s_gmp, 1)

        pe.wait_ge(s_gmr, 2)
        pe.wait_ge(s_tab, 1)

        def xT4(b, par, nth):
            pe.wait_ge(s_xg[par], nth)
            for half in range(2):
                for j in range(4):
                    k = 4 * half + j
                    ins = tr(psum[half][:, j * P:(j + 1) * P], xg[:, par, k * P:(k + 1) * P], P)
            ins.then_inc(s_xTp, 1)

        def gu(b, slot, nth):
            pe.wait_ge(s_xTa, b + 1)
            pe.wait_ge(s_xTv, b + 1)
            pe.wait_ge(s_wd[slot], nth)
            for k in range(KD):
                mm(psum[2][:, 0:DE], xT[:, k, :], WG[:, slot, k, :], start=(k == 0), stop=(k == KD - 1))
            for k in range(KD):
                ins = mm(psum[3][:, 0:DE], xT[:, k, :], WU[:, slot, k, :], start=(k == 0), stop=(k == KD - 1))
            ins.then_inc(s_gu, 1)

        def hT4(b):
            pe.wait_ge(s_hid, b + 1)
            for k in range(2):
                ins = tr(psum[4][:, k * P:(k + 1) * P], hid[:, k * P:(k + 1) * P], P)
            ins.then_inc(s_hTp, 1)

        def down(b, slot):
            pe.wait_ge(s_hTc, b + 1)
            if not isinstance(b, int) or b >= 1:
                pe.wait_ge(s_ya, b)
                pe.wait_ge(s_yv, b)
            for half in range(2):
                for k in range(2):
                    ins = mm(psum[5 + half][:], hidT[:, k, :], WD[:, slot, k, half * 512:(half + 1) * 512], start=(k == 0), stop=(k == 1))
            ins.then_inc(s_down, 1)

        xT4(0, 0, 16)
        gu(0, 0, 48)
        xT4(1, 1, 16)
        with pe.Fori(0, (NE - SLOTS) // SLOTS) as i:
            for u in range(SLOTS):
                b = i * SLOTS + u
                hT4(b)
                gu(b + 1, (u + 1) % SLOTS, i * 48 + (48 if u + 1 < SLOTS else 96))
                xT4(b + 2, u % 2, i * 32 + 16 * ((u + 2) // 2 + 1))
                down(b, u)
        for b in range(NE - SLOTS, NE):
            hT4(b)
            if b + 1 < NE:
                gu(b + 1, (b + 1) % SLOTS, 48 * ((b + 1) // SLOTS + 1))
            if b + 2 < NE:
                xT4(b + 2, b % 2, 16 * ((b + 2) // 2 + 1))
            down(b, b % SLOTS)
        n_ov = pe.value_load(ovf_i[0:1, MAXOV:MAXOV + 1], min_val=0, max_val=MAXOV)
        with pe.Fori(0, MAXOV) as j:
            with pe.If(j < n_ov):
                xT4(j + NE, 0, j * 16 + 16 * (NE // 2 + 1))
                gu(j + NE, 0, j * 48 + 48 * (NE // SLOTS + 1))
                hT4(j + NE)
                down(j + NE, 0)
            with pe.Else():
                nc.tensor.nop()

    def x2_squares(act, s, do, sig):
        R = ROWS[seq[s]]
        act.wait_ge(s_x2, s + 1)
        do(nc.scalar.activation(junk2[:R], x_att[:R, s % 2], ACT.Square, scale=D ** -0.5, accum_out=st2[:R, 40:41]), sig[id(s_x2sq)])

    @block.scalar
    def _(act):
        do = Serial(act, act_step)
        A = nc.scalar.activation
        sig = {id(x): Signal(x) for x in (s_ss, s_hTa, s_lat, s_sqk, s_v, s_u, s_gv, s_sqq, s_prob, s_x2sq)}
        act.wait_ge(s_c, 32)
        do(A(c_act[:].rearrange("p k v -> p v k"), c_in[:], ACT.Silu), Signal(s_cact))
        freed = {}

        def done(ins, sem):
            ins.then_inc(sem, 1)

        def kv(kt):
            R = P if kt != SAMPLE else DEC
            n = key_order.index(kt)
            for half in range(2):
                ps = b1.read(act, (f"kv{half}", kt))
                v = ps[:R].rearrange("p (h n) -> p h n", n=ND + VD)
                if n >= 1 and half == 0:
                    act.wait_ge(s_kh, n)
                    act.wait_ge(s_out1["v"], 16 * n)
                done(A(sq_k[:R, 4 * half:4 * half + 4], v[:, :, 0:ND], ACT.Square), b1.free((f"kv{half}", kt)))
                done(A(vh[:R, 4 * half:4 * half + 4], v[:, :, ND:], ACT.Copy), b1.free((f"kv{half}", kt)))
            act.wait_ge(b1.free(("kv1", kt)), b1.at[("kv1", kt)][2] + 2)
            act.wait_ge(b1.free(("kv0", kt)), b1.at[("kv0", kt)][2] + 2)
            act.sem_inc(s_sqk, 1)
            act.sem_inc(s_v, 1)

        def x_squares(t):
            R = ROWS[t]
            act.wait_ge(s_x[t % 2], 16 * (t // 2 + 1))
            do(A(junk[:R], xbuf[:R, t % 2], ACT.Square, scale=D ** -0.5, accum_out=st[:R, t % 2:t % 2 + 1]), sig[id(s_ss)])

        def hT_half(t):
            R = ROWS[t]
            v = prompt_or_sample(t)
            if t == 0:
                act.wait_ge(s_A1, 1)
            ps = b1.read(act, ("xT1", t))
            for j in range(4):
                k = 4 + j
                ins = A(hT[:, t % 2, k, :R], ps[:, j * P:j * P + R], ACT.Identity, bias=modT[:, k, v:v + 1], scale=A1[:, k, v:v + 1])
                if j < 3:
                    do(ins)
                else:
                    ins.then_inc(b1.free(("xT1", t)), 1)
            act.wait_ge(b1.free(("xT1", t)), b1.at[("xT1", t)][2] + 1)
            act.sem_inc(s_hTa, 1)

        act.wait_ge(s_cache, 32)
        for c in range(NC_):
            do(A(junk[:, 0:KVL], cck[:, c, 0:KVL], ACT.Square, scale=KVL ** -0.5, accum_out=st[:, 8 + c:9 + c]))
        act.sem_inc(s_css, 1)
        x_squares(0)
        for c in range(NC_):
            kv(9 + c)
        hT_half(0)
        for t in range(NT + 1):
            R = ROWS[t]
            ps = b1.read(act, ("lat", t))
            if t >= 2:
                act.wait_ge(s_out1[f"lat{t % 2}"], 32 * (t // 2))
                act.wait_ge(s_kh, NC_ + t - 1)
            done(A(lat[:R, t % 2], ps[:R, 0:LAT], ACT.Copy), b1.free(("lat", t)))
            act.wait_ge(b1.free(("lat", t)), b1.at[("lat", t)][2] + 1)
            act.sem_inc(s_lat, 1)
            if t:
                act.wait_ge(s_latn, t)
            do(A(junk[:R, 0:QL], lat[:R, t % 2, 0:QL], ACT.Square, scale=QL ** -0.5, accum_out=st[:R, 12:13]))
            do(A(junk[:R, 0:KVL], lat[:R, t % 2, QL:QL + KVL], ACT.Square, scale=KVL ** -0.5, accum_out=st[:R, 13:14]))
            act.sem_inc(s_lss, 1)
            if t < NT:
                x_squares(t + 1)
            if t:
                kv(t - 1)
            ps = b1.read(act, ("u", t))
            if t >= 2:
                act.wait_ge(s_gm, t - 1)
            done(A(u_sb[:R, t % 2], ps[:R, :], ACT.Gelu_apprx_tanh), b1.free(("u", t)))
            act.wait_ge(b1.free(("u", t)), b1.at[("u", t)][2] + 1)
            act.sem_inc(s_u, 1)
            if t < NT:
                hT_half(t + 1)
            ps = b1.read(act, ("gv", t))
            if t:
                act.wait_ge(s_vr, t)
            done(A(gv[:R], ps[:R, :], ACT.Gelu_apprx_tanh), b1.free(("gv", t)))
            act.wait_ge(b1.free(("gv", t)), b1.at[("gv", t)][2] + 1)
            act.sem_inc(s_gv, 1)
            if t:
                act.wait_ge(s_qh, t)
            for half in range(2):
                ps = b1.read(act, (f"q{half}", t))
                done(A(sq_q[:R, 4 * half:4 * half + 4], ps[:R, 0:384].rearrange("p (h n) -> p h n", n=QK), ACT.Square), b1.free((f"q{half}", t)))
            for half in range(2):
                act.wait_ge(b1.free((f"q{half}", t)), b1.at[(f"q{half}", t)][2] + 1)
            act.sem_inc(s_sqq, 1)
        kv(NT)
        act.sem_inc(s_end1, 1)
        act.wait_ge(s_end1, 4)

        nk = 0

        def turn(tag, half, dst, r):
            ps = b2.read(act, tag)
            src = ps[:QK, :].rearrange("p (h n) -> p h n", n=P)[:, :, :r]
            if dst is None:
                ins = A(qT[:, 4 * half:4 * half + 4, :r], src, ACT.Copy, scale=gqk[0:QK, 0:1])
            else:
                ins = A(kT[:, 4 * half:4 * half + 4, dst:dst + r], src, ACT.Copy)
            ins.then_inc(b2.free(tag), 1)
            act.wait_ge(b2.free(tag), b2.at[tag][2] + 1)

        act.wait_ge(s_fold, 1)
        for s, t in enumerate(seq):
            R = ROWS[t]
            for kt in key_tiles[t]:
                r = P if kt != SAMPLE else DEC
                if s == 1:
                    act.wait_ge(s_heads, 1)
                turn(("kT0", kt), 0, kslot(t, kt) * P, r)
                turn(("kT1", kt), 1, kslot(t, kt) * P, r)
                act.sem_inc(s_keys, 1)
            if s:
                act.wait_ge(s_heads, s)
            turn(("qT0", t), 0, None, R)
            turn(("qT1", t), 1, None, R)
            act.sem_inc(s_qused, 1)
            act.sem_inc(s_qkT, 1)
            if s:
                x2_squares(act, s - 1, do, sig)
            n = nkeys(t)
            for h in range(H):
                u = s * H + h
                act.wait_ge(s_nmax, u + 1)
                if u >= 2:
                    act.wait_ge(s_PT, u - 1)
                bank = scores(h)
                if n > 512:
                    do(A(prob[:R, u % 2, 0:512], psum[bank][:R, :], ACT.Exp, bias=st2[:R, h:h + 1], accum_out=st2[:R, 16 + h:17 + h]))
                    do(A(prob[:R, u % 2, 512:n], psum[bank + 1][:R, 0:n - 512], ACT.Exp, bias=st2[:R, h:h + 1], accum_out=st2[:R, 24 + h:25 + h]), sig[id(s_prob)])
                else:
                    do(A(prob[:R, u % 2, 0:n], psum[bank][:R, 0:n], ACT.Exp, bias=st2[:R, h:h + 1], accum_out=st2[:R, 16 + h:17 + h]), sig[id(s_prob)])
        x2_squares(act, len(seq) - 1, do, sig)
        act.sem_inc(s_end2, 1)
        act.wait_ge(s_end2, 4)

        act.wait_ge(s_rx, 1)
        do(A(rt[:, 1, :, 0:NG], rt[:, 0, :, 0:NG], ACT.Exp))
        do(A(rt[:, 3, :, 0:1], rt[:, 2, :, 0:1], ACT.Exp))
        act.sem_inc(s_ry, 1)
        act.wait_ge(s_tab, 1)

        def xT_half(b):
            act.wait_ge(s_xTp, b + 1)
            A(xT[:, 4:8, :], psum[1][:].rearrange("p (k n) -> p k n", n=P), ACT.Copy).then_inc(s_xTa, 1)
            act.wait_ge(s_xTa, b + 1)

        def silu(b):
            act.wait_ge(s_gu, b + 1)
            if not isinstance(b, int) or b >= 1:
                act.wait_ge(s_hid, b)
            A(sg[:], psum[2][:, 0:DE], ACT.Silu).then_inc(s_sg, 1)
            act.wait_ge(s_sg, b + 1)

        def y_half(b, par, nth):
            act.wait_ge(s_down, b + 1)
            if nth is not None:
                act.wait_ge(s_yst[par], nth)
            ww = roww[:, b:b + 1] if isinstance(b, int) else roww[:, bass.ds(b, 1)]
            A(yb[:, par, 0:512], psum[5][:], ACT.Copy, scale=ww).then_inc(s_ya, 1)

        xT_half(0)
        silu(0)
        xT_half(1)
        for b in range(2):
            silu(b + 1)
            xT_half(b + 2)
            y_half(b, b % 2, None)
        with act.Fori(0, (NE - SLOTS) // 2) as i:
            for u in range(2):
                b = i * 2 + (2 + u)
                silu(b + 1)
                xT_half(b + 2)
                y_half(b, u, i * 16 + 16)
        for b in range(NE - 2, NE):
            if b + 1 < NE:
                silu(b + 1)
            y_half(b, b % 2, 16 * (b // 2))
        n_ov = act.value_load(ovf_i[0:1, MAXOV:MAXOV + 1], min_val=0, max_val=MAXOV)
        with act.Fori(0, MAXOV) as j:
            with act.If(j < n_ov):
                b = j + NE
                xT_half(b)
                silu(b)
                y_half(b, 0, j * 16 + 16 * (NE // 2))
            with act.Else():
                act.nop()

    @block.vector
    def _(dve):
        do = Serial(dve, dve_step)
        V = nc.vector
        mark = {}

        def signal(s):
            dve.sem_inc(s, 1)

        def rstd(n=[0]):
            n[0] += 1
            dve.sem_inc(s_ms, 1)
            dve.wait_ge(s_rs, n[0])

        def last_read(ins, tag, banks=b1):
            ins.then_inc(banks.free(tag), 1)
            b, _, before = banks.at[tag]
            nread[tag] = nread.get(tag, 0) + 1
            dve.wait_ge(banks.free(tag), before + nread[tag] + (others.get(tag[0] if isinstance(tag, tuple) else tag, 0)))

        nread = {}
        others = {"kv0": 2, "kv1": 2, "q0": 1, "q1": 1}

        def lat_norm(R, lat_ap, dst_q, dst_c, sq, sc):
            do(V.tensor_scalar(dst_q, lat_ap[:, 0:QL], sq, None, ALU.mult))
            do(V.tensor_scalar(dst_c, lat_ap[:, QL:QL + KVL], sc, None, ALU.mult))

        ps = b1.read(dve, "vec")
        last_read(V.tensor_copy(vT[:, 0:NVEC], ps[:, 0:NVEC]), "vec")
        dve.wait_ge(s_css, 1)
        rstd()
        for c in range(NC_):
            do(V.tensor_scalar(cn[:, c, :], cck[:, c, 0:KVL], st[:, 16 + c:17 + c], None, ALU.mult))
        signal(s_cn)
        dve.wait_ge(s_params, 16 * 10)
        for half in range(2):
            ps = b1.read(dve, f"wsp{half}")
            last_read(V.tensor_copy(wspT[:, 4 * half:4 * half + 4, :], ps[:].rearrange("p (h n) -> p h n", n=P)), f"wsp{half}")
        do(V.memset(wspT[DEC:P, :, 0:DEC], 0.0))
        signal(s_wsp)
        signal(s_wsp)
        do(V.tensor_tensor(rope_k[:], rope_q[:], bcast(grope[:, 1:2, :], [P, NT, 2 * RD]), ALU.mult))
        do(V.tensor_tensor(rope_q[:], rope_q[:], bcast(grope[:, 0:1, :], [P, NT, 2 * RD]), ALU.mult))
        dve.wait_ge(s_wkv, 16)
        do(V.tensor_scalar(W_ukv[:], W_ukv[:], vT[:, R_GKV:R_GKV + 1], None, ALU.mult))
        signal(s_fold1)
        ps = b1.read(dve, "cT")
        last_read(V.tensor_copy(latT_c[:], ps[:].rearrange("p (h n) -> p h n", n=P)), "cT")
        signal(s_cT)

        def ada(j):
            ps = b1.read(dve, ("ada", j))
            last_read(V.tensor_tensor(modT[:, 2 * j:2 * j + 2, :], ps[:, 0:4].rearrange("p (n v) -> p n v", v=2),
                                      bcast(vT[:, R_BADA + 2 * j:R_BADA + 2 * j + 2].unsqueeze(2), [P, 2, 2]), ALU.add), ("ada", j))
            signal(s_adafree)

        for j in range(8):
            ada(j)
        do(V.tensor_scalar(A1[:], modT[:, 8:16, :], 1.0, None, ALU.add))
        do(V.tensor_tensor(A1[:], A1[:], bcast(vT[:, R_G1:R_G1 + 8].unsqueeze(2), [P, KD, 2]), ALU.mult))
        signal(s_A1)

        def x_norm(t):
            R = ROWS[t]
            dve.wait_ge(s_ss, t + 1)
            rstd()
            do(V.tensor_scalar(xn[:R], xbuf[:R, t % 2], st[:R, 2 + t % 2:3 + t % 2], None, ALU.mult))
            signal(s_xn)

        def hT_half(t):
            R = ROWS[t]
            v = prompt_or_sample(t)
            ps = b1.read(dve, ("xT0", t))
            for k in range(4):
                ins = V.tensor_scalar(hT[:, t % 2, k, :R], ps[:, k * P:k * P + R], A1[:, k, v:v + 1], modT[:, k, v:v + 1], ALU.mult, ALU.add)
                if k < 3:
                    do(ins)
                else:
                    last_read(ins, ("xT0", t))
            signal(s_hTv)

        def turn(dst, src, table, pt, R, n):
            C = bcast(table[:R, pt:pt + 1, 0:RD], [R, n, RD])
            half = RD // 2
            do(V.tensor_tensor(rot[:R, 0:n], src, C, ALU.mult))
            for i in range(2):
                Sn = bcast(table[:R, pt:pt + 1, RD + half * i:RD + half * (i + 1)], [R, n, half])
                do(V.tensor_tensor(rot2[:R, 0:n, half * i:half * (i + 1)], src[:, :, half * (1 - i):half * (2 - i)], Sn, ALU.mult))
            do(V.tensor_tensor(dst, rot[:R, 0:n], rot2[:R, 0:n], ALU.add))

        def kv(kt):
            R = P if kt != SAMPLE else DEC
            n = key_order.index(kt)
            if kt >= 9:
                kr = cck[:R, kt - 9:kt - 8, KVL:KVL + RD]
                pt = kt - 9
            else:
                kr = lat[:R, kt % 2:kt % 2 + 1, QL + KVL:LAT]
                pt = kt if kt < NT else NC_
            turn(krot[:R].unsqueeze(1), kr, rope_k, pt, R, 1)
            do(V.tensor_tensor_reduce(ctmp[:R], kr[:, 0, :], kr[:, 0, :], 1.0, 0.0, ALU.mult, ALU.add, st[:R, 30:31]))
            dve.wait_ge(s_sqk, n + 1)
            do(V.tensor_reduce(st[:R, 32:40], sq_k[:R], AXX, ALU.add))
            do(V.tensor_scalar(st[:R, 32:40], st[:R, 32:40], st[:R, 30:31], 1.0 / QK, ALU.add, ALU.mult))
            rstd()
            if n:
                dve.wait_ge(s_out1["k"], 16 * n)
            for half in range(2):
                ps = b1.read(dve, (f"kv{half}", kt))
                v = ps[:R].rearrange("p (h n) -> p h n", n=ND + VD)[:, :, 0:ND]
                last_read(V.tensor_tensor(kh[:R, 4 * half:4 * half + 4, 0:ND], v,
                                          bcast(st[:R, 32 + 4 * half:36 + 4 * half].unsqueeze(2), [R, 4, ND]), ALU.mult), (f"kv{half}", kt))
            do(V.tensor_tensor(kh[:R, :, ND:], bcast(krot[:R].unsqueeze(1), [R, H, RD]), bcast(st[:R, 32:40].unsqueeze(2), [R, H, RD]), ALU.mult))
            signal(s_kh)

        x_norm(0)
        for c in range(NC_):
            kv(9 + c)
        dve.wait_ge(s_wuq, 16)
        for k in range(2):
            do(V.tensor_scalar(W_uq[:, k], W_uq[:, k], vT[:, R_GQL + k:R_GQL + k + 1], None, ALU.mult))
        signal(s_fold1)
        hT_half(0)

        def mix(t):
            R = ROWS[t]
            ps = b1.read(dve, ("mix", t))
            if t:
                dve.wait_ge(s_out1["gm"], 16 * t)
            last_read(V.tensor_tensor(gm[:R].rearrange("p (h n) -> p h n", n=64), ps[:R].rearrange("p (h n) -> p h n", n=64),
                                      bcast(vT[:R, R_BSP:R_BSP + 8].unsqueeze(2), [R, H, 64]), ALU.add), ("mix", t))
            do(V.tensor_tensor(gm[:R], gm[:R], u_sb[:R, t % 2], ALU.mult))
            do(V.tensor_tensor_reduce(junk_v[:R], gm[:R], gm[:R], 1.0 / GW, 0.0, ALU.mult, ALU.add, st[:R, 41:42]))
            rstd()
            do(V.tensor_scalar(gm[:R], gm[:R], st[:R, 41:42], None, ALU.mult))
            signal(s_gm)

        for t in range(NT + 1):
            R = ROWS[t]
            dve.wait_ge(s_lss, t + 1)
            rstd()
            lat_norm(R, lat[:R, t % 2], latn[:R, 0:QL], latn[:R, QL:], st[:R, 14:15], st[:R, 15:16])
            signal(s_latn)
            if t < NT:
                x_norm(t + 1)
            if t:
                kv(t - 1)
            ps = b1.read(dve, ("latT", t))
            last_read(V.tensor_copy(latT[:, :, :R], ps[:, 0:3 * P].rearrange("p (k n) -> p k n", n=P)[:, :, :R]), ("latT", t))
            signal(s_latT)
            if t < NT:
                hT_half(t + 1)
            if t:
                mix(t - 1)
            dve.wait_ge(s_gv, t + 1)
            do(V.bn_stats(st[:R, 42:48], gv[:R]))
            do(V.bn_aggr(st[:R, 48:50], st[:R, 42:48]))
            rstd()
            do(V.tensor_scalar(gv[:R], gv[:R], st[:R, 48:49], st[:R, 50:51], ALU.subtract, ALU.mult))
            do(V.tensor_tensor(vrows[:R], gv[:R], ln_g[:R], ALU.mult))
            do(V.tensor_tensor(vrows[:R], vrows[:R], ln_b[:R], ALU.add))
            signal(s_vr)
            if t < NT:
                ada(8 + 2 * t)
                ada(9 + 2 * t)
            dve.wait_ge(s_sqq, t + 1)
            do(V.tensor_reduce(st[:R, 52:60], sq_q[:R], AXX, ALU.add))
            do(V.tensor_scalar(st[:R, 52:60], st[:R, 52:60], 1.0 / QK, None, ALU.mult))
            rstd()
            if t:
                dve.wait_ge(s_out1["q"], 16 * t)
            for half in range(2):
                ps = b1.read(dve, (f"q{half}", t))
                last_read(V.tensor_tensor(qh[:R, 4 * half:4 * half + 4], ps[:R, 0:384].rearrange("p (h n) -> p h n", n=QK),
                                          bcast(st[:R, 52 + 4 * half:56 + 4 * half].unsqueeze(2), [R, 4, QK]), ALU.mult), (f"q{half}", t))
            turn(qh[:R, :, ND:], qh[:R, :, ND:], rope_q, t if t < NT else NC_, R, H)
            signal(s_qh)
        kv(NT)
        mix(NT)
        signal(s_end1)
        dve.wait_ge(s_end1, 4)

        do(V.tensor_tensor(gqk[0:ND], vT[0:ND, R_GQ:R_GQ + 1], vT[0:ND, R_GK:R_GK + 1], ALU.mult))
        do(V.memset(gqk[ND:QK], 1.0))
        do(V.tensor_scalar(gqk[0:QK], gqk[0:QK], QK ** -0.5, None, ALU.mult))
        do(V.tensor_scalar(A2T[:], modT[:, 32:40, :], 1.0, None, ALU.add))
        do(V.tensor_tensor(A2T[:], A2T[:], bcast(vT[:, R_G2:R_G2 + 8].unsqueeze(2), [P, KD, 2]), ALU.mult))
        signal(s_fold)
        dve.wait_ge(s_wout, 16)
        for k in range(KD):
            do(V.tensor_scalar(W_out[:, k], W_out[:, k], vT[:, R_GOA + k:R_GOA + k + 1], None, ALU.mult))
        perm = lambda ap: ap.rearrange("p (k q) -> p q k", q=P)

        def tail(s):
            t = seq[s]
            R = ROWS[t]
            dve.wait_ge(s_y, s + 1)
            dve.wait_ge(s_ld2["x"][s % 2], 16 * (s // 2 + 1))
            for half in range(2):
                do(V.tensor_tensor(tmp2[:R, half * 512:(half + 1) * 512], psum[half][:R], gate_a[:R, half * 512:(half + 1) * 512], ALU.mult))
            do(V.tensor_tensor(x_att[:R, s % 2], x_att[:R, s % 2], tmp2[:R], ALU.add))
            signal(s_x2)
            dve.wait_ge(s_x2sq, s + 1)
            rstd()
            do(V.scalar_tensor_tensor(tmp2[:R], x_att[:R, s % 2], st2[:R, 41:42], A2[:R], ALU.mult, ALU.mult))
            if s:
                dve.wait_ge(s_st2["h2"], 16 * s)
            do(V.tensor_tensor(perm(h2[:R]), tmp2[:R].rearrange("p (q k) -> p q k", k=KD), B2[:R].rearrange("p (q k) -> p q k", k=KD), ALU.add))
            signal(s_h2)

        def h2T_(s):
            t = seq[s]
            R = ROWS[t]
            for half in range(2):
                tag = (f"h2T{half}", t)
                ps = b2.read(dve, tag)
                last_read(V.tensor_copy(h2T[:, 4 * half:4 * half + 4, :R], ps[:].rearrange("p (k n) -> p k n", n=P)[:, :, :R]), tag, b2)
            signal(s_h2T)

        def router(s):
            t = seq[s]
            R = ROWS[t]
            if s == 0:
                dve.wait_ge(s_wr, 64)
            ps = b2.read(dve, ("rt", t))
            last_read(V.tensor_tensor(logits[:R, t, :], ps[:R, 0:NG + NE], b_r[:R], ALU.add), ("rt", t), b2)

        def mT_(s):
            t = seq[s]
            R = ROWS[t]
            for half in range(2):
                tag = (f"mT{half}", t)
                ps = b2.read(dve, tag)
                last_read(V.tensor_copy(mT[:, 4 * half:4 * half + 4, :R], ps[:].rearrange("p (k n) -> p k n", n=P)[:, :, :R]), tag, b2)
            signal(s_mT)

        for s, t in enumerate(seq):
            R = ROWS[t]
            if s == 0:
                for j in range(6):
                    dst = (gate_a, A2, B2)[j // 2]
                    ps = b2.read(dve, ("bc", s, j))
                    last_read(V.tensor_copy(dst[:, (j % 2) * 512:(j % 2 + 1) * 512], ps[:]), ("bc", s, j), b2)
            if s == 1:
                for j in range(6):
                    dst = bc_next[:, j // 2]
                    ps = b2.read(dve, ("bc", s, j))
                    last_read(V.tensor_copy(dst[:, (j % 2) * 512:(j % 2 + 1) * 512], ps[:]), ("bc", s, j), b2)
            if s:
                mT_(s - 1)
                tail(s - 1)
            if s == 1:
                for j, dst in enumerate((gate_a, A2, B2)):
                    do(V.tensor_copy(dst[:], bc_next[:, j]))
            n = nkeys(t)
            nb = (len(blocks(t)) + 3) // 4

            def row_max(h):
                u = s * H + h
                bank = scores(h)
                dve.wait_ge(s_S[h % 2], s * (H // 2) + h // 2 + 1)
                if n > 512:
                    do(V.tensor_reduce(st2[:R, 8:9], psum[bank][:R, :], AXX, ALU.max))
                    do(V.tensor_reduce(st2[:R, 9:10], psum[bank + 1][:R, 0:n - 512], AXX, ALU.max))
                    do(V.tensor_scalar(st2[:R, h:h + 1], st2[:R, 8:9], st2[:R, 9:10], -1.0, ALU.max, ALU.mult))
                else:
                    do(V.tensor_reduce(st2[:R, 8:9], psum[bank][:R, 0:n], AXX, ALU.max))
                    do(V.tensor_scalar(st2[:R, h:h + 1], st2[:R, 8:9], -1.0, None, ALU.mult))
                signal(s_nmax)

            row_max(0)
            row_max(1)
            for h in range(H):
                u = s * H + h
                for j in range(nb):
                    tag = ("PT", t, h, j)
                    ps = b2.read(dve, tag)
                    bl = blocks(t)[4 * j:4 * j + 4]
                    full = [b for b in bl if b[1] == P]
                    part = [b for b in bl if b[1] < P]
                    src = ps[:].rearrange("p (k n) -> p k n", n=P)
                    ops = []
                    if full:
                        ops.append(V.tensor_copy(probT[:, u % 2, 4 * j:4 * j + len(full), :R], src[:, 0:len(full), :R]))
                        if part:
                            do(ops.pop())
                    for b, r in part:
                        ops.append(V.tensor_copy(probT[:r, u % 2, b, :R], src[:r, b % 4, :R]))
                    last_read(ops[-1], tag, b2)
                signal(s_PT)
                if h + 2 < H:
                    row_max(h + 2)
                if h == 3 and s:
                    h2T_(s - 1)
                if h == 5 and s:
                    router(s - 1)
            if n > 512:
                do(V.tensor_tensor(st2[:R, 16:24], st2[:R, 16:24], st2[:R, 24:32], ALU.add))
            do(V.reciprocal(st2[:R, 16:24], st2[:R, 16:24]))
            dve.wait_ge(s_heads, s + 1)
            do(V.tensor_tensor(attn[:R].rearrange("p (h n) -> p h n", n=VD), psum[7][:R].rearrange("p (h n) -> p h n", n=VD),
                               bcast(st2[:R, 16:24].unsqueeze(2), [R, H, VD]), ALU.mult))
            signal(s_Ofree)
            do(V.tensor_tensor_reduce(junk_v2[:R], attn[:R], attn[:R], 1.0 / GW, 0.0, ALU.mult, ALU.add, st2[:R, 42:43]))
            rstd()
            do(V.tensor_scalar(merged[:R, s % 2, 0:GW], attn[:R], st2[:R, 42:43], None, ALU.mult))
            dve.wait_ge(s_ld2["gm"][s % 2], 16 * (s // 2 + 1))
            signal(s_mrg)
        s = len(seq) - 1
        mT_(s)
        tail(s)
        h2T_(s)
        router(s)
        dve.sem_inc(s_end2, 2)
        dve.wait_ge(s_end2, 4)

        NTT = NT + 1
        T = lambda i, n=EG: rt[:, i, :, 0:n]
        col = lambda i: rt[:, i, :, 0:1]
        TT, TS = V.tensor_tensor, V.tensor_scalar

        def first_max(dst, vals, m, n, desc):
            do(V.tensor_reduce(m, vals, AXX, ALU.max))
            do(TT(T(20, n), vals, bcast(m, [P, NTT, n]), ALU.is_equal))
            do(TT(T(20, n), T(20, n), desc, ALU.mult))
            do(V.tensor_reduce(col(21), T(20, n), AXX, ALU.max))
            do(TT(dst, T(20, n), bcast(col(21), [P, NTT, n]), ALU.is_equal))

        do(TS(rt[:, 19, 0, :], iota_f[:, 0:EG], -1.0, float(EG), ALU.mult, ALU.add))
        desc = lambda n: bcast(rt[:, 19, 0:1, 0:n], [P, NTT, n])
        lg = logits[:, :, 0:NG]
        first_max(T(4, NG), lg, col(5), NG, desc(NG))
        do(TT(T(0, NG), lg, bcast(col(5), [P, NTT, NG]), ALU.subtract))
        le = logits[:, :, NG:].rearrange("p t (g e) -> p t g e", e=EG)
        do(TT(big[:].rearrange("p t (e g) -> p t g e", g=NG), le, bcast(T(4, NG).unsqueeze(3), [P, NTT, NG, EG]), ALU.mult))
        do(V.tensor_reduce(T(6), big[:].rearrange("p t (e g) -> p t e g", g=NG), AXX, ALU.add))
        first_max(T(7), T(6), col(8), EG, desc(EG))
        do(TS(T(9), T(7), NEG, None, ALU.mult))
        do(TT(T(9), T(9), T(6), ALU.add))
        first_max(T(10), T(9), col(11), EG, desc(EG))
        do(TT(col(2), col(11), col(8), ALU.subtract))
        signal(s_rx)
        g4 = bcast(T(4, NG).unsqueeze(3), [P, NTT, NG, EG])
        for dst, src in ((E1, 7), (E2, 10)):
            do(TT(dst[:].rearrange("p t (g e) -> p t g e", e=EG), g4, bcast(T(src).unsqueeze(2), [P, NTT, NG, EG]), ALU.mult))
            do(V.memset(dst[DEC:P, NT, :], 0.0))
        do(TT(E[:], E1[:], E2[:], ALU.add))
        signal(s_E)
        dve.wait_ge(s_ry, 1)
        do(V.tensor_reduce(col(12), T(1, NG), AXX, ALU.add))
        do(TS(col(13), col(3), 1.0, None, ALU.add))
        do(TT(col(13), col(13), col(12), ALU.mult))
        do(V.reciprocal(col(14), col(13)))
        do(TT(col(15), col(14), col(3), ALU.mult))
        dve.wait_ge(s_rank, 1)
        do(V.tensor_copy(big2[:], psum[1][:, 0:NTT * NE].rearrange("p (t e) -> p t e", e=NE)))
        do(V.memset(base[:, 0, :], 0.0))
        for t in range(1, NTT):
            do(TT(base[:, t, :], base[:, t - 1, :], big2[:, t - 1, :], ALU.add))
        do(TT(cnt[:, 0, :], base[:, NT, :], big2[:, NT, :], ALU.add))
        do(TT(base[:], base[:], psum[0][:, 0:NTT * NE].rearrange("p (t e) -> p t e", e=NE), ALU.add))
        do(TS(cmp_[:, 0, 0:MAXOV], iota_f[:, 0:MAXOV], float(P), float(P), ALU.mult, ALU.add))
        do(V.tensor_copy(thr[:], cmp_[:, 0, 0:MAXOV]))
        do(TT(cmp_[:], bcast(cnt[:, 0, :].unsqueeze(2), [P, NE, MAXOV]), bcast(thr[:].unsqueeze(1), [P, NE, MAXOV]), ALU.is_gt))
        do(V.tensor_reduce(cnt[:, 1, :], cmp_[:], AXX, ALU.add))
        src, dst = 1, 2
        k = 1
        do(V.tensor_copy(cnt[:, 2, :], cnt[:, 1, :]))
        src, dst = 2, 3
        while k < NE:
            do(V.tensor_copy(cnt[:, dst, 0:k], cnt[:, src, 0:k]))
            do(TT(cnt[:, dst, k:], cnt[:, src, k:], cnt[:, src, 0:NE - k], ALU.add))
            src, dst = dst, src
            k *= 2
        incl = src
        do(TT(cnt[:, 4, :], cnt[:, incl, :], cnt[:, 1, :], ALU.subtract))
        do(TT(cmp_[:].rearrange("p e j -> p j e"), bcast(cnt[:, incl, :].unsqueeze(1), [P, MAXOV, NE]),
              bcast(iota_f[:, 0:MAXOV].unsqueeze(2), [P, MAXOV, NE]), ALU.is_le))
        do(V.tensor_reduce(ovf[:, 0:MAXOV], cmp_[:].rearrange("p e j -> p j e"), AXX, ALU.add))
        do(V.tensor_copy(ovf[:, MAXOV:MAXOV + 1], cnt[:, incl, NE - 1:NE]))
        do(V.tensor_copy(ovf_i[:], ovf[:]))
        do(TS(cnt[:, 5, :], iota_f[:, 0:NE], float(P), None, ALU.mult))
        do(TS(cnt[:, 6, :], cnt[:, 4, :], float(NE - 1), float(P), ALU.add, ALU.mult))
        do(TT(cnt[:, 6, :], cnt[:, 6, :], cnt[:, 5, :], ALU.subtract))
        do(TS(big[:], base[:], float(P), None, ALU.is_ge))
        do(TT(big[:], big[:], bcast(cnt[:, 6:7, :], [P, NTT, NE]), ALU.mult))
        do(TT(big[:], big[:], base[:], ALU.add))
        do(TT(big[:], big[:], bcast(cnt[:, 5:6, :], [P, NTT, NE]), ALU.add))
        for kk, Ek in enumerate((E1, E2)):
            do(TT(big2[:], big[:], Ek[:], ALU.mult))
            do(V.tensor_reduce(posf[:, kk, :], big2[:], AXX, ALU.add))
        do(V.tensor_copy(pos_i2[:], posf[:]))
        do(TS(ri[:], pos_i2[:], P - 1, None, ALU.bitwise_and))
        do(TS(bi[:], pos_i2[:], 7, None, ALU.logical_shift_right))
        do(V.tensor_copy(rf[:], ri[:]))
        do(V.tensor_copy(bf[:], bi[:]))
        n = 0
        for t in range(NTT):
            for kk in range(2):
                if n >= 2:
                    dve.wait_ge(s_hotu, n - 1)
                do(TS(onehot[:, n % 2, :], iota_f[:], rf[:, kk, t:t + 1], None, ALU.is_equal))
                do(TS(bhot[:, n % 2, 0, :], iota_f[:, 0:NB], bf[:, kk, t:t + 1], tok_id[:, t:t + 1], ALU.is_equal, ALU.mult))
                do(TS(bhot[:, n % 2, 1, :], iota_f[:, 0:NB], bf[:, kk, t:t + 1], rt[:, 14 + kk, t, 0:1], ALU.is_equal, ALU.mult))
                signal(s_hot[n % 2])
                n += 1
        dve.wait_ge(s_hotu, n)
        do(V.tensor_copy(rowtok_i[:], psum[2][:, 0:NB]))
        do(V.tensor_copy(roww[:], psum[2][:, NB:2 * NB]))
        signal(s_tab)
        for v in range(2):
            dve.wait_ge(s_gmp, v + 1)
            for half in range(2):
                do(V.tensor_copy(gate_m[:, v, half * 512:(half + 1) * 512], psum[4 + half][:]))
            signal(s_gmr)

        def xT_half(b):
            dve.wait_ge(s_xTp, b + 1)
            V.tensor_copy(xT[:, 0:4, :], psum[0][:].rearrange("p (k n) -> p k n", n=P)).then_inc(s_xTv, 1)
            dve.wait_ge(s_xTv, b + 1)

        def hidden(b):
            dve.wait_ge(s_sg, b + 1)
            if not isinstance(b, int) or b >= 1:
                dve.wait_ge(s_hTp, b)
            V.tensor_tensor(hid[:].rearrange("p (k q) -> p q k", q=P), sg[:].rearrange("p (q k) -> p q k", k=2),
                            psum[3][:, 0:DE].rearrange("p (q k) -> p q k", k=2), ALU.mult).then_inc(s_hid, 1)
            dve.wait_ge(s_hid, b + 1)

        def hidT_(b):
            dve.wait_ge(s_hTp, b + 1)
            if not isinstance(b, int) or b >= 1:
                dve.wait_ge(s_down, b)
            V.tensor_copy(hidT[:], psum[4][:, 0:DE].rearrange("p (k n) -> p k n", n=P)).then_inc(s_hTc, 1)
            dve.wait_ge(s_hTc, b + 1)

        def y_half(b, par, nth):
            dve.wait_ge(s_down, b + 1)
            if nth is not None:
                dve.wait_ge(s_yst[par], nth)
            ww = roww[:, b:b + 1] if isinstance(b, int) else roww[:, bass.ds(b, 1)]
            V.tensor_scalar(yb[:, par, 512:], psum[6][:], ww, None, ALU.mult).then_inc(s_yv, 1)

        xT_half(0)
        hidden(0)
        xT_half(1)
        for b in range(2):
            hidT_(b)
            hidden(b + 1)
            xT_half(b + 2)
            y_half(b, b % 2, None)
        with dve.Fori(0, (NE - SLOTS) // 2) as i:
            for u in range(2):
                b = i * 2 + (2 + u)
                hidT_(b)
                hidden(b + 1)
                xT_half(b + 2)
                y_half(b, u, i * 16 + 16)
        for b in range(NE - 2, NE):
            hidT_(b)
            if b + 1 < NE:
                hidden(b + 1)
            y_half(b, b % 2, 16 * (b // 2))
        n_ov = dve.value_load(ovf_i[0:1, MAXOV:MAXOV + 1], min_val=0, max_val=MAXOV)
        with dve.Fori(0, MAXOV) as j:
            with dve.If(j < n_ov):
                b = j + NE
                xT_half(b)
                hidden(b)
                hidT_(b)
                y_half(b, 0, j * 16 + 16 * (NE // 2))
            with dve.Else():
                dve.nop()
        for t in range(NT + 1):
            R = ROWS[t]
            v = prompt_or_sample(t)
            p = t % 2
            dve.wait_ge(s_g1[p], 32 * (t // 2 + 1))
            do(V.tensor_tensor(y1b[:R, p], y1b[:R, p], y2b[:R, p], ALU.add))
            do(V.tensor_tensor(y1b[:R, p], y1b[:R, p], gate_m[:R, v], ALU.mult))
            dve.wait_ge(s_x2l[p], 16 * (t // 2 + 1))
            if t >= 2:
                dve.wait_ge(s_yout[p], 16 * (t // 2))
            do(V.tensor_tensor(yo[:R, p], y1b[:R, p], x2b[:R, p], ALU.add))
            signal(s_yo)



_INS = ["x_prompt", "x_sample", "cache_ckv", "cache_krope", "c_prompt", "c_sample", "w_ada", "b_ada", "g_norm_mix", "w_in",
        "g_q_lat", "w_uq", "g_kv_lat", "w_ukv", "g_qnorm", "g_knorm", "g_ln_v", "b_ln_v", "w_spatial", "b_spatial",
        "g_out_attn", "g_out_gmlp", "w_out", "g_norm_ffn", "w_router_group", "b_router_group", "w_router_expert",
        "b_router_expert", "w_gate_e", "w_up_e", "w_down_e"]
_OUTS = [(1, SEQ, D), (1, DEC, D), (1, 1, SEQ, KVL), (1, 1, SEQ, RD), (1, 1, DEC, KVL), (1, 1, DEC, RD), (1, 1, DEC, GW)]


def rope_table():
    half = RD // 2
    inv = (np.float32(1.0) / (np.float32(10000.0) ** (np.arange(half, dtype=np.float32) / np.float32(half)))).astype(np.float32)
    ang = np.arange(SEQ, dtype=np.float32)[:, None] * inv[None, :]
    c, s = np.cos(ang).astype(np.float32), np.sin(ang).astype(np.float32)
    return np.concatenate([c, c, -s, s], axis=1)


def kernel(**inputs):
    import concourse.bacc as bacc
    from concourse.bass_utils import run_bass_kernel_spmd

    nc = bacc.Bacc("TRN2", target_bir_lowering=False, num_devices=1)
    arrays, aps = {}, {}
    for name in _INS:
        x = np.ascontiguousarray(inputs[name])
        arrays[f"in_{name}"] = x
        aps[name] = nc.dram_tensor(f"in_{name}", x.shape, F32, kind="ExternalInput").ap()
    arrays["rope_table"] = rope_table()
    aps["rope_table"] = nc.dram_tensor("rope_table", (SEQ, 2 * RD), F32, kind="ExternalInput").ap()
    outs = [nc.dram_tensor(f"out_{i}", shape, F32, kind="ExternalOutput").ap() for i, shape in enumerate(_OUTS)]
    build(nc, aps, outs)
    r = run_bass_kernel_spmd(nc, [arrays], core_ids=[0])
    return tuple(r.results[0][f"out_{i}"] for i in range(len(_OUTS)))
```

```python
from contextlib import ExitStack

import numpy as np

import concourse.bass as bass
from concourse import mybir

F32 = mybir.dt.float32
BF16 = mybir.dt.bfloat16
I32 = mybir.dt.int32
U32 = mybir.dt.uint32
ALU = mybir.AluOpType
ACT = mybir.ActivationFunctionType
AXX = mybir.AxisListType.X

P = 128
D = 1024
KD = D // P
NT = 8
SEQ = NT * P
DEC = 64
TOK = SEQ + DEC
PAST = 512
NC_ = PAST // P
H = 8
QL, KVL, RD, ND, VD = 256, 128, 32, 64, 64
QK = ND + RD
LAT = QL + KVL + RD
GW = 512
EPS = 1e-6
NG, EG = 4, 8
NE = NG * EG
DE = 256
MAXOV = (2 * TOK) // P - 1
NB = NE + MAXOV
YROWS = NB * P
ZROWS = MAXOV * P // NT
assert ZROWS * NT == MAXOV * P and ZROWS % P == 0
ADA_COLS = 256
ADA_CHUNKS = 6 * D // ADA_COLS
NEG = -1e30
ROWS = [P] * NT + [DEC]
SAMPLE = NT
KEYROW = [P * t for t in range(NT)] + [SEQ + PAST] + [SEQ + P * c for c in range(NC_)]
KEYROWS = SEQ + PAST + DEC


class Signal:

    def __init__(self, sem):
        self.sem, self.n = sem, 0


class Serial:

    def __init__(self, eng, step):
        self.eng, self.step = eng, step
        self.off = 0

    def __call__(self, ins, signal=None):
        s = signal or self.step
        s.n += 1
        ins.then_inc(s.sem, 1)
        self.eng.wait_ge(s.sem, s.n + (self.off if s is self.step else 0))


class Banks:

    def __init__(self, tiles, filled, freed, order):
        self.tiles, self.filled, self.freed = tiles, filled, freed
        self.at, total, uses = {}, [0] * len(tiles), [0] * len(tiles)
        for n, (tag, readers) in enumerate(order):
            b = n % len(tiles)
            assert tag not in self.at, tag
            self.at[tag] = (b, uses[b], total[b])
            uses[b] += 1
            total[b] += readers
        self.total = total

    def claim(self, pe, tag):
        b, _, before = self.at[tag]
        if before:
            pe.wait_ge(self.freed[b], before)
        return self.tiles[b]

    def full(self, ins, tag):
        ins.then_inc(self.filled[self.at[tag][0]], 1)

    def read(self, eng, tag):
        b, use, _ = self.at[tag]
        eng.wait_ge(self.filled[b], use + 1)
        return self.tiles[b]

    def free(self, tag):
        return self.freed[self.at[tag][0]]


def overflow_blocks(eng, n_ov, block):
    with eng.If(n_ov > 0):
        block(0)
    with eng.Else():
        eng.nop()
    with eng.If(n_ov > 1):
        with eng.Fori(0, MAXOV - 1) as i:
            with eng.If(i + 1 < n_ov):
                block(i + 1)
            with eng.Else():
                eng.nop()
    with eng.Else():
        eng.nop()


def build(nc, a, o):
    with ExitStack() as ctx:
        build_in(nc, a, o, ctx)


def build_in(nc, a, o, ctx):
    def sem(name):
        return nc.alloc_semaphore(name)

    cursor = [(nc.sbuf_base + 63) // 64 * 64]

    def sb(name, shape, dt=F32):
        n = int(np.prod(shape[1:])) * (2 if dt == BF16 else 4)
        t = nc.alloc_sbuf_tensor_at(name, list(shape), dt, offset=cursor[0])
        cursor[0] += (n + 31) // 32 * 32
        assert cursor[0] <= nc.sbuf_usable_end, (name, cursor[0])
        return t

    w = {k: a[k] for k in a}
    x_rows = [w["x_prompt"][0, P * t:P * (t + 1), :] for t in range(NT)] + [w["x_sample"][0]]
    y_p, y_s, ckv_p, kr_p, ckv_s, kr_s, v_s = o
    y_rows = [y_p[0, P * t:P * (t + 1), :] for t in range(NT)] + [y_s[0]]
    ckv_rows = [ckv_p[0, 0, P * t:P * (t + 1), :] for t in range(NT)] + [ckv_s[0, 0]]
    kr_rows = [kr_p[0, 0, P * t:P * (t + 1), :] for t in range(NT)] + [kr_s[0, 0]]
    q_d = nc.dram_tensor("q_scratch", (TOK, H * QK), F32).ap()
    k_d = nc.dram_tensor("k_scratch", (KEYROWS, H * QK), F32).ap()
    v_d = nc.dram_tensor("v_scratch", (KEYROWS, H * VD), F32).ap()
    gm_d = nc.dram_tensor("gmlp_scratch", (TOK, GW), F32).ap()
    x2_d = nc.dram_tensor("residual_scratch", (TOK, D), F32).ap()
    h2_d = nc.dram_tensor("ffn_input_scratch", (TOK, D), F32).ap()
    yb_d = nc.dram_tensor("expert_rows_scratch", (YROWS, D), F32).ap()
    w_ada, w_in = w["w_ada"][0], w["w_in"][0]

    psum = [nc.alloc_psum_tensor(f"bank{i}", [P, 512], F32) for i in range(8)]

    ident = sb("ident", [P, P])
    vecs = sb("vecs", [P, P])
    vT = sb("vT", [P, P])
    modT = sb("modT", [P, 48, 2])
    logits = sb("logits", [P, NT + 1, NG + NE])
    iota_f = sb("iota_f", [P, P])
    tok_id = sb("tok_id", [P, NT + 1])
    rowtok_i = sb("rowtok_i", [P, NB], I32)
    roww = sb("roww", [P, NB])
    pos_i2 = sb("pos_i2", [P, 2, NT + 1], I32)
    ovf_i = sb("ovf_i", [P, MAXOV + 1], I32)
    tri = sb("tri", [P, P])
    ones = sb("ones", [P, P])
    mhalf = sb("mhalf", [P, H])
    stage_base = cursor[0]
    R_BADA, R_G1, R_G2, R_GQL, R_GKV, R_GOA, R_GOG, R_BSP, R_GQ, R_GK = 0, 48, 56, 64, 66, 67, 71, 75, 83, 84
    NVEC = 85

    W_in = sb("W_in", [P, KD, LAT + 2 * GW])
    W_out = sb("W_out", [P, KD, D])
    keep_out = cursor[0]
    W_uq = sb("W_uq", [P, 2, H * QK])
    W_ukv = sb("W_ukv", [P, H * (ND + VD)])
    c_in = sb("c_in", [P, 2, KD])
    c_act = sb("c_act", [P, KD, 2])
    A1 = sb("A1", [P, KD, 2])
    ada_w = sb("ada_w", [P, 3, KD, ADA_COLS])
    ada_row = sb("ada_row", [2, 2, ADA_COLS])
    xbuf = sb("xbuf", [P, 2, D])
    xn = sb("xn", [P, D])
    hT = sb("hT", [P, 2, KD, P])
    lat = sb("lat", [P, 2, LAT])
    latn = sb("latn", [P, QL + KVL])
    latT = sb("latT", [P, 3, P])
    u_sb = sb("u_sb", [P, 2, GW])
    gv = sb("gv", [P, GW])
    vrows = sb("vrows", [P, GW])
    qh = sb("qh", [P, H, QK])
    kh = sb("kh", [P, 2, H, QK])
    vh = sb("vh", [P, 2, H, VD])
    gm = sb("gm", [P, GW])
    junk = sb("junk", [P, D])
    ada_acc = sb("ada_acc", [P, 2, ADA_COLS])
    zeros = sb("zeros", [P, D // 2])
    cn = sb("cn", [P, NC_, P])
    latT_c = sb("latT_c", [P, NC_, P])
    sq_q = sb("sq_q", [P, H, QK])
    sq_k = sb("sq_k", [P, H, ND])
    rot = sb("rot", [P, H, RD])
    rot2 = sb("rot2", [P, H, RD])
    krot = sb("krot", [P, RD])
    ctmp = sb("ctmp", [P, RD])
    wsp = sb("wsp", [P, H, P])
    wspT = sb("wspT", [P, H, P])
    ln_g = sb("ln_g", [P, GW])
    ln_b = sb("ln_b", [P, GW])
    rope_q = sb("rope_q", [P, NT, 2 * RD])
    rope_k = sb("rope_k", [P, NT, 2 * RD])
    grope = sb("grope", [P, 2, 2 * RD])
    cck = sb("cck", [P, NC_, KVL + RD])
    st = sb("st", [P, 64])

    cursor[0] = keep_out
    kT = sb("kT", [QK, H, SEQ])
    vall = sb("vall", [P, NT, H * VD])
    qbuf = sb("qbuf", [P, 2, H, QK])
    merged = sb("merged", [P, 2, D])
    x_att = sb("x_att", [P, 2, D])
    prob = sb("prob", [P, 2, SEQ])
    probT = sb("probT", [P, 2, NT, P])
    mT = sb("mT", [P, KD, P])
    attn = sb("attn", [P, GW])
    h2 = sb("h2", [P, D])
    h2T = sb("h2T", [P, KD, P])
    gate_a = sb("gate_a", [P, D])
    A2 = sb("A2", [P, D])
    B2 = sb("B2", [P, D])
    assert cursor[0] <= nc.sbuf_usable_end
    cursor[0] = stage_base
    tmp2 = sb("tmp2", [P, D])
    junk2 = sb("junk2", [P, D])
    junk_v2 = sb("junk_v2", [P, GW])
    bc_next = sb("bc_next", [P, 3, D])
    w_r = sb("w_r", [P, KD, NG + NE])
    qT = sb("qT", [QK, 2, H, P])
    KBUF = 4
    kbuf = sb("kbuf", [P, KBUF, H, QK])
    b_r = sb("b_r", [P, NG + NE])
    st2 = sb("st2", [P, 80])
    gqk = sb("gqk", [P, 1])
    A2T = sb("A2T", [P, KD, 2])
    mask_l = sb("mask_l", [1, P], BF16)
    mask_r = sb("mask_r", [1, DEC], BF16)
    assert cursor[0] <= keep_out, cursor[0]

    cursor[0] = stage_base
    SLOTS = 4
    WG = sb("WG", [P, SLOTS, KD, DE])
    WU = sb("WU", [P, SLOTS, KD, DE])
    WD = sb("WD", [P, SLOTS, 2, D])
    xg = sb("xg", [P, 2, D])
    xT = sb("xT", [P, KD, P])
    sg = sb("sg", [P, DE])
    hid = sb("hid", [P, DE])
    hidT = sb("hidT", [P, 2, P])
    yb = sb("yb", [P, 2, D])
    gi = sb("gi", [P, 2], I32)
    YBUF = 3
    y1b = sb("y1b", [P, YBUF, D])
    y2b = sb("y2b", [P, YBUF, D])
    gate_m = sb("gate_m", [P, 2, D])
    route_base = cursor[0]
    x2_all = sb("x2_all", [P, NT + 1, D])

    cursor[0] = route_base
    E1 = sb("E1", [P, NT + 1, NE])
    E2 = sb("E2", [P, NT + 1, NE])
    E = sb("E", [P, NT + 1, NE])
    big = sb("big", [P, NT + 1, NE])
    big2 = sb("big2", [P, NT + 1, NE])
    base = sb("base", [P, NT + 1, NE])
    rt = sb("rt", [P, 24, NT + 1, EG])
    cnt = sb("cnt", [P, 8, NE])
    cmp_ = sb("cmp", [P, NE, MAXOV])
    onehot = sb("onehot", [P, 2, NT + 1, P])
    bhot = sb("bhot", [P, 2, NT + 1, 2, NB])
    thr = sb("thr", [P, MAXOV])
    ovf = sb("ovf", [P, MAXOV + 1])
    posf = sb("posf", [P, 2, NT + 1])
    ri = sb("ri", [P, 2, NT + 1], I32)
    bi = sb("bi", [P, 2, NT + 1], I32)
    rf = sb("rf", [P, 2, NT + 1])
    bf = sb("bf", [P, 2, NT + 1])

    s_params = sem("params_loaded")
    s_c = sem("c_loaded")
    s_ada = [sem(f"ada_chunk_loaded{i}") for i in range(3)]
    s_cache = sem("cache_loaded")
    s_wkv = sem("w_ukv_loaded")
    s_wlat = sem("w_in_lat_loaded")
    s_wgu = sem("w_in_gate_loaded")
    s_wgv = sem("w_in_value_loaded")
    s_wuq = sem("w_uq_loaded")
    s_wout = sem("w_out_loaded")
    s_x = [sem(f"x_loaded{i}") for i in range(2)]
    s_const = sem("pool_constants_ready")
    s_cact = sem("silu_c_ready")
    s_setup2 = sem("constants_ready")
    s_vec = sem("vectors_loaded")
    s_css = sem("cache_square_sums_ready")
    s_cn = sem("cache_normed")
    s_cT = sem("cache_transposed")
    s_fold1 = sem("gains_folded")
    s_wsp = sem("spatial_weights_ready")
    s_lss = sem("latent_square_sums_ready")
    s_rx = sem("router_exponents_ready")
    s_ry = sem("router_exponentials_ready")
    s_A1 = sem("mix_scale_ready")
    s_aused = [sem(f"ada_chunk_used{i}") for i in range(3)]
    s_modT = sem("ada_columns_ready")
    s_rope = sem("rotary_tables_loaded")
    s_ss = sem("x_square_sum_ready")
    s_xn = sem("x_normed")
    s_hTa = sem("hT_by_act")
    s_hTv = sem("hT_by_dve")
    s_lat = sem("latents_copied")
    s_latn = sem("latents_normed")
    s_latT = sem("latents_transposed")
    s_sqk = sem("k_squares_and_v_ready")
    s_u = sem("u_ready")
    s_gv = sem("gelu_v_ready")
    s_vr = sem("v_rows_ready")
    s_sqq = sem("q_squares_ready")
    s_kh = sem("k_ready")
    s_qh = sem("q_ready")
    s_gm = sem("gmlp_ready")
    s_out1 = {k: sem(f"stored_{k}") for k in ("lat0", "lat1", "k0", "k1", "v0", "v1", "q", "gm", "vs")}
    f1 = [sem(f"bank_filled{i}") for i in range(8)]
    e1 = [sem(f"bank_freed{i}") for i in range(8)]
    s_end1 = sem("projected")

    s_ms = sem("mean_squares_ready")
    s_rs = sem("reciprocal_roots_ready")
    act_step, dve_step, pool_step = (Signal(sem(f"{n}_step")) for n in ("act", "dve", "pool"))

    SETUP_ADA = 8
    def loop_ada(t):
        return [SETUP_ADA + 2 * t, SETUP_ADA + 2 * t + 1] if t < NT // 2 else [SETUP_ADA + NT // 2 + t]

    DVE_ADA = [loop_ada(t)[-1] for t in range(NT)]
    END_ADA = list(range(SETUP_ADA + NT + NT // 2, ADA_CHUNKS))

    def kvs(t):
        return ([9 + t] if t < NC_ else []) + ([t - 1] if t else [])

    key_order = [kt for t in range(NT + 1) for kt in kvs(t)] + [NT]
    kv_use = lambda kt: [(("kv0", kt), 3), (("kv1", kt), 3)]
    order1 = [(("ada", 0), 1), (("ada", 1), 1), ("vec", 1), (("adaT", 0), 1)]
    for j in range(2, SETUP_ADA):
        order1 += [(("ada", j), 1), (("adaT", j - 1), 1)]
    order1 += [(("adaT", SETUP_ADA - 1), 1), (("xT0", 0), 1), (("xT1", 0), 1), ("cT", 1), ("wsp0", 1), ("wsp1", 1)]
    for t in range(NT + 1):
        order1 += [(("lat", t), 1)]
        for kt in kvs(t):
            order1 += kv_use(kt)
        order1 += [(("u", t), 1), (("latT", t), 1)]
        if t < NT:
            order1 += [(("xT0", t + 1), 1), (("xT1", t + 1), 1)]
        if t:
            order1 += [(("mix", t - 1), 1), (("adaT", loop_ada(t - 1)[0]), 1)]
        order1 += [(("gv", t), 1)]
        if t < NT:
            order1 += [(("ada", j), 1) for j in loop_ada(t)[:-1]]
        order1 += [(("q0", t), 2), (("q1", t), 2)]
    order1 += [(("ada", j), 1) for j in END_ADA[:2]] + kv_use(NT) + [(("mix", NT), 1)]
    order1 += [(("ada", j), 1) for j in END_ADA[2:]] + [(("adaT", END_ADA[0]), 1)]
    b1 = Banks(psum, f1, e1, order1)

    s_ld2 = {k: [sem(f"{k}_reloaded{i}") for i in range(4 if k == "k" else 2)] for k in ("q", "k", "gm", "x")}
    s_vl = [sem(f"v_reloaded{i}") for i in range(2)]
    s_wr = sem("router_weights_loaded")
    s_qkT = sem("q_and_k_transposed")
    s_keys = sem("key_tile_consumed")
    s_S = [sem(f"scores_ready{i}") for i in range(2)]
    s_nmax = sem("row_max_ready")
    s_prob = sem("probabilities_ready")
    s_PT = sem("probabilities_transposed")
    s_Ofree = sem("attention_copied")
    s_mrg = sem("merged_ready")
    s_mT = sem("merged_transposed")
    s_y = sem("out_projection_done")
    s_x2 = sem("residual_ready")
    s_x2sq = sem("residual_square_sum_ready")
    s_yfree = sem("out_projection_read")
    s_h2 = sem("ffn_input_ready")
    s_h2T = sem("ffn_input_transposed")
    s_heads = sem("tile_heads_done")
    s_fold = sem("attend_constants_ready")
    s_st2 = {k: sem(f"stored_{k}") for k in ("x2_0", "x2_1", "h2")}
    f2 = [sem(f"ring_filled{i}") for i in range(2)]
    e2 = [sem(f"ring_freed{i}") for i in range(2)]
    s_end2 = sem("attended")

    seq = [SAMPLE] + list(range(NT))
    key_tiles = {SAMPLE: [9 + c for c in range(NC_)] + [SAMPLE]} | {t: [t] for t in range(NT)}

    def slot0(t):
        return NT - NC_ - 1 if t == SAMPLE else 0

    def kslot(t, kt):
        return t if t < NT else slot0(t) + (kt - 9 if kt >= 9 else NC_)

    def nkeys(t):
        return PAST + DEC if t == SAMPLE else P * (t + 1)

    def blocks(t):
        n = nkeys(t)
        return [(b, min(P, n - P * b)) for b in range((n + P - 1) // P)]

    OUT_PARTS = [(0, 0, 3), (0, 3, 6), (0, 6, KD), (1, 0, 2), (1, 2, 4), (1, 4, 6), (1, 6, KD)]
    sums = lambda s: 16 if s % 2 == 0 else 64
    LAST = len(seq) - 1

    def beside(s, h):
        work = []
        if s == 0 and h in (2, 3):
            work += [("vectors", h - 2, 0)]
        if s >= 2 and h < 3:
            work += [("W_out", s - 2, 4 + h)]
        if s and h == 3:
            work += [("mT", s - 1, 0)]
        if s and h >= 4:
            work += [("W_out", s - 1, h - 4)]
        if s >= 2 and h == 6:
            work += [("h2T", s - 2, 0)]
        if s >= 2 and h == 7:
            work += [("router", s - 2, 0)]
        if s < LAST and h == 5:
            work += [("prep", s + 1, 0)]
        return work

    closing = [("W_out", LAST - 1, i) for i in range(4, 7)] + [("mT", LAST, 0)] + [("W_out", LAST, i) for i in range(3)] + [("h2T", LAST - 1, 0)]
    closing += [("W_out", LAST, i) for i in range(3, 7)] + [("router", LAST - 1, 0), ("h2T", LAST, 0), ("router", LAST, 0)]

    def uses(work, s, _):
        t = seq[s]
        if work == "prep":
            return [((f"kT{half}", kt), 1) for kt in key_tiles[t] for half in range(2)] + [((f"qT{half}", t), 1) for half in range(2)]
        if work == "vectors":
            return [(("bc", s, j), 1) for j in range(6)]
        if work in ("mT", "h2T"):
            return [((f"{work}{half}", t), 1) for half in range(2)]
        return [(("rt", t), 1)] if work == "router" else []

    order2 = uses("prep", 0, 0)
    for s, t in enumerate(seq):
        for h in range(H):
            order2 += [(("PT", t, h, j), 1) for j in range((len(blocks(t)) + 3) // 4)]
            for work in beside(s, h):
                order2 += uses(*work)
    for work in closing:
        order2 += uses(*work)
    b2 = Banks([psum[4], psum[5]], f2, e2, order2)

    def scores(u):
        return 2 * (u % 2)

    s_E = sem("expert_one_hots_ready")
    s_rank = sem("ranks_ready")
    s_hot = sem("slot_one_hots_ready")
    s_tabp = sem("tables_summed")
    s_tab = sem("tables_ready")
    s_gmp = sem("gate_rows_filled")
    s_gmr = sem("gate_rows_read")
    s_wd = [sem(f"expert_weights_loaded{i}") for i in range(SLOTS)]
    s_zst = sem("zero_rows_stored")
    s_idx = sem("gather_index_ready")
    s_xg = [sem(f"tokens_gathered{i}") for i in range(2)]
    s_xTp = sem("tokens_transposed")
    s_xTa = sem("xT_by_act")
    s_xTv = sem("xT_by_dve")
    s_gu = sem("gate_up_done")
    s_sg = sem("silu_ready")
    s_hid = sem("hidden_ready")
    s_hTp = sem("hidden_transposed")
    s_hTc = sem("hidT_ready")
    s_down = sem("down_done")
    s_ya = sem("y_by_act")
    s_yv = sem("y_by_dve")
    s_yst = [sem(f"expert_rows_stored{i}") for i in range(2)]
    s_end4 = sem("experts_done")
    s_x2l = sem("residual_loaded")
    s_g1 = [sem(f"slot_rows_gathered{i}") for i in range(YBUF)]
    s_yo = sem("output_tile_ready")
    s_yout = sem("output_stored")

    ctx_block = nc.Block()
    block = ctx.enter_context(ctx_block)
    prompt_or_sample = lambda t: 1 if t == SAMPLE else 0

    def bcast(ap, shape):
        return ap.broadcast_to(list(shape))

    def ada_rows(j):
        if j in END_ADA:
            c = (j - END_ADA[0]) * ADA_COLS
            return xn[0:2, c:c + ADA_COLS]
        return ada_row[0:2, j % 2, :]

    def store_tail(sp, s):
        t = seq[s]
        R = ROWS[t]
        sp.wait_ge(s_x2, s + 1)
        sp.dma_start(x2_d[P * t:P * t + R], x_att[:R, s % 2]).then_inc(s_st2[f"x2_{s % 2}"], 16)
        sp.wait_ge(s_h2, s + 1)
        sp.dma_start(h2_d[P * t:P * t + R], h2[:R]).then_inc(s_st2["h2"], 16)

    @block.sync
    def _(sp):
        sp.dma_start(c_in[:, 0, :], w["c_prompt"][0].rearrange("(p k) -> p k", k=KD)).then_inc(s_c, 16)
        sp.dma_start(c_in[:, 1, :], w["c_sample"][0].rearrange("(p k) -> p k", k=KD)).then_inc(s_c, 16)
        ada_src = w_ada.rearrange("(p k) n -> p k n", k=KD)

        def ada(j):
            if j >= 3:
                sp.wait_ge(s_aused[j % 3], j // 3)
            sp.dma_start(ada_w[:, j % 3], ada_src[:, :, j * ADA_COLS:(j + 1) * ADA_COLS]).then_inc(s_ada[j % 3], 16)

        def x_load(t):
            sp.dma_start(xbuf[:ROWS[t], t % 2], x_rows[t]).then_inc(s_x[t % 2], 16)

        win = w_in.rearrange("(k p) n -> p k n", p=P)
        ada(0)
        sp.dma_start(cck[:, :, 0:KVL], w["cache_ckv"][0, 0].rearrange("(c p) n -> p c n", p=P)).then_inc(s_cache, 16)
        sp.dma_start(cck[:, :, KVL:KVL + RD], w["cache_krope"][0, 0].rearrange("(c p) n -> p c n", p=P)).then_inc(s_cache, 16)
        ada(1)
        sp.dma_start(W_ukv[:], w["w_ukv"][0]).then_inc(s_wkv, 16)
        ada(2)
        x_load(0)
        for j in range(3, SETUP_ADA):
            ada(j)
        x_load(1)
        sp.dma_start(W_in[:, :, 0:LAT], win[:, :, 0:LAT]).then_inc(s_wlat, 16)
        sp.dma_start(W_in[:, :, LAT:LAT + GW], win[:, :, LAT:LAT + GW]).then_inc(s_wgu, 16)
        sp.dma_start(W_uq[:], w["w_uq"][0].rearrange("(k p) n -> p k n", p=P)).then_inc(s_wuq, 16)
        sp.dma_start(W_in[:, :, LAT + GW:], win[:, :, LAT + GW:]).then_inc(s_wgv, 16)

        def store_kv(kt):
            R = P if kt != SAMPLE else DEC
            order = key_order.index(kt) + 1
            sp.wait_ge(s_sqk, order)
            i = (order - 1) % 2
            sp.dma_start(v_d[KEYROW[kt]:KEYROW[kt] + R], vh[:R, i].rearrange("p h n -> p (h n)")).then_inc(s_out1[f"v{i}"], 16)
            sp.wait_ge(s_kh, order)
            sp.dma_start(k_d[KEYROW[kt]:KEYROW[kt] + R], kh[:R, i].rearrange("p h n -> p (h n)")).then_inc(s_out1[f"k{i}"], 16)

        def store_gm(t):
            R = ROWS[t]
            if t == SAMPLE:
                sp.wait_ge(s_vr, t + 1)
                sp.dma_start(v_s[0, 0], vrows[:R]).then_inc(s_out1["vs"], 16)
            sp.wait_ge(s_gm, t + 1)
            sp.dma_start(gm_d[P * t:P * t + R], gm[:R]).then_inc(s_out1["gm"], 16)

        for t in range(NT + 1):
            R = ROWS[t]
            sp.wait_ge(s_lat, t + 1)
            sp.dma_start(ckv_rows[t], lat[:R, t % 2, QL:QL + KVL]).then_inc(s_out1[f"lat{t % 2}"], 16)
            sp.dma_start(kr_rows[t], lat[:R, t % 2, QL + KVL:]).then_inc(s_out1[f"lat{t % 2}"], 16)
            if t + 2 <= NT:
                sp.wait_ge(s_xn, t + 1)
                x_load(t + 2)
            if t < NT:
                for j in loop_ada(t):
                    ada(j)
                if t == 0:
                    sp.wait_ge(s_const, 3)
                z = NE * P + t * ZROWS
                sp.dma_start(yb_d[z:z + ZROWS].rearrange("(p j) (a n) -> p (j a) n", p=P, a=2),
                             zeros[:].unsqueeze(1).broadcast_to([P, 2 * ZROWS // P, D // 2])).then_inc(s_zst, 16)
            if t == 0:
                sp.dma_start(W_out[:], w["w_out"][0].rearrange("(k p) n -> p k n", p=P)).then_inc(s_wout, 16)
            for kt in kvs(t):
                store_kv(kt)
            if t:
                store_gm(t - 1)
            if t == NT:
                for j in END_ADA[:3]:
                    ada(j)
            sp.wait_ge(s_qh, t + 1)
            sp.dma_start(q_d[P * t:P * t + R], qh[:R].rearrange("p h n -> p (h n)")).then_inc(s_out1["q"], 16)
        for j in END_ADA[3:]:
            ada(j)
        store_kv(NT)
        store_gm(NT)
        for k, m in (("lat0", 2 * (NT // 2 + 1)), ("lat1", 2 * (NT // 2)), ("k0", (NT + 2 + NC_) // 2), ("k1", (NT + 1 + NC_) // 2), ("v0", (NT + 2 + NC_) // 2), ("v1", (NT + 1 + NC_) // 2), ("q", NT + 1), ("gm", NT + 1), ("vs", 1)):
            sp.wait_ge(s_out1[k], 16 * m)
        sp.wait_ge(s_zst, 16 * NT)
        sp.sem_inc(s_end1, 1)
        sp.wait_ge(s_end1, 4)

        nk = 0

        def new_keys(s):
            nonlocal nk
            t = seq[s]
            for i, kt in enumerate(key_tiles[t]):
                r = P if kt != SAMPLE else DEC
                if nk >= KBUF:
                    sp.wait_ge(s_keys, nk - KBUF + 1)
                sp.dma_start(kbuf[:r, nk % KBUF].rearrange("p h n -> p (h n)"), k_d[KEYROW[kt]:KEYROW[kt] + r]).then_inc(s_ld2["k"][nk % KBUF], 16)
                nk += 1
            if s >= 2:
                sp.wait_ge(s_qkT, s - 1)
            sp.dma_start(qbuf[:ROWS[t], s % 2].rearrange("p h n -> p (h n)"), q_d[P * t:P * t + ROWS[t]]).then_inc(s_ld2["q"][s % 2], 16)
            if s >= 2:
                sp.wait_ge(s_heads, s - 1)
            for kt in key_tiles[t]:
                r = P if kt != SAMPLE else DEC
                sp.dma_start(vall[:r, kslot(t, kt)], v_d[KEYROW[kt]:KEYROW[kt] + r]).then_inc(s_vl[s % 2], 16)

        new_keys(0)
        sp.dma_start(w_r[:, :, 0:NG], w["w_router_group"][0].rearrange("(p k) n -> p k n", k=KD)).then_inc(s_wr, 16)
        sp.dma_start(w_r[:, :, NG:], w["w_router_expert"][0].rearrange("(p k) n -> p k n", k=KD)).then_inc(s_wr, 16)
        sp.dma_start(b_r[:, 0:NG], bcast(w["b_router_group"], [P, NG])).then_inc(s_wr, 16)
        sp.dma_start(b_r[:, NG:], bcast(w["b_router_expert"], [P, NE])).then_inc(s_wr, 16)
        for s, t in enumerate(seq):
            R = ROWS[t]
            if s < LAST:
                new_keys(s + 1)
            if s >= 2:
                sp.wait_ge(s_mT, s - 1)
            sp.dma_start(merged[:R, s % 2, GW:], gm_d[P * t:P * t + R]).then_inc(s_ld2["gm"][s % 2], 16)
            if s >= 2:
                store_tail(sp, s - 2)
                sp.wait_ge(s_st2[f"x2_{s % 2}"], 16 * (s // 2))
            sp.dma_start(x_att[:R, s % 2], x_rows[t]).then_inc(s_ld2["x"][s % 2], 16)
        store_tail(sp, LAST - 1)
        store_tail(sp, LAST)
        for i in range(2):
            sp.wait_ge(s_st2[f"x2_{i}"], 16 * len(range(i, len(seq), 2)))
        sp.wait_ge(s_st2["h2"], 16 * len(seq))
        sp.sem_inc(s_end2, 1)
        sp.wait_ge(s_end2, 4)

        def load_expert(e, slot):
            sp.dma_start(WG[:, slot], w["w_gate_e"][0, e].rearrange("(p k) n -> p k n", k=KD)).then_inc(s_wd[slot], 16)
            sp.dma_start(WU[:, slot], w["w_up_e"][0, e].rearrange("(p k) n -> p k n", k=KD)).then_inc(s_wd[slot], 16)
            sp.dma_start(WD[:, slot], w["w_down_e"][0, e].rearrange("(p k) n -> p k n", k=2)).then_inc(s_wd[slot], 16)

        def load_expert_dyn(e, slot):
            sp.dma_start(WG[:, slot], w["w_gate_e"][0, bass.ds(e, 1)].rearrange("o (p k) n -> (o p) k n", k=KD)).then_inc(s_wd[slot], 16)
            sp.dma_start(WU[:, slot], w["w_up_e"][0, bass.ds(e, 1)].rearrange("o (p k) n -> (o p) k n", k=KD)).then_inc(s_wd[slot], 16)
            sp.dma_start(WD[:, slot], w["w_down_e"][0, bass.ds(e, 1)].rearrange("o (p k) n -> (o p) k n", k=2)).then_inc(s_wd[slot], 16)

        def store_y(b, par):
            sp.wait_ge(s_ya, b + 1)
            sp.wait_ge(s_yv, b + 1)
            sp.dma_start(yb_d[bass.ds(b * P, P)] if not isinstance(b, int) else yb_d[b * P:(b + 1) * P], yb[:, par]).then_inc(s_yst[par], 16)

        for e in range(SLOTS):
            load_expert(e, e)
        sp.wait_ge(s_tab, 1)
        with sp.Fori(0, (NE - SLOTS) // SLOTS) as i:
            for u in range(SLOTS):
                store_y(i * SLOTS + u, u % 2)
                sp.wait_ge(s_down, i * SLOTS + u + 1)
                load_expert_dyn(i * SLOTS + (SLOTS + u), u)
        n_ov = sp.value_load(ovf_i[0:1, MAXOV:MAXOV + 1], min_val=0, max_val=MAXOV)
        for b in range(NE - SLOTS, NE):
            store_y(b, b % 2)
            if b == NE - SLOTS:
                sp.wait_ge(s_down, b + 1)
                with sp.If(n_ov > 0):
                    e = sp.value_load(ovf_i[0:1, 0:1], min_val=0, max_val=NE - 1)
                    load_expert_dyn(e, 0)
                with sp.Else():
                    sp.nop()
            i = b - (NE - SLOTS)
            for t in range(i * 2, i * 2 + 2 if i < SLOTS - 1 else NT + 1):
                sp.dma_start(x2_all[:ROWS[t], t], x2_d[P * t:P * t + ROWS[t]]).then_inc(s_x2l, 16)
        def overflow(j):
            sp.wait_ge(s_ya, j + (NE + 1))
            sp.wait_ge(s_yv, j + (NE + 1))
            sp.dma_start(yb_d[bass.ds(j * P + NE * P, P)], yb[:, 0]).then_inc(s_yst[0], 16)
            with sp.If(j + 1 < n_ov):
                e = sp.value_load(ovf_i[0:1, bass.ds(j + 1, 1)], min_val=0, max_val=NE - 1)
                load_expert_dyn(e, 0)
            with sp.Else():
                sp.nop()

        overflow_blocks(sp, n_ov, overflow)
        sp.wait_ge(s_yst[0], n_ov * 16 + NE // 2 * 16)
        sp.wait_ge(s_yst[1], NE // 2 * 16)
        sp.sem_inc(s_end4, 1)

        for t in range(NT + 1):
            sp.wait_ge(s_yo, t + 1)
            sp.dma_start(y_rows[t], x2_all[:ROWS[t], t]).then_inc(s_yout, 16)
        sp.wait_ge(s_yout, 16 * (NT + 1))

    @block.gpsimd
    def _(g):
        do = Serial(g, pool_step)
        do(g.memset(vecs[:], 0.0))
        g.sem_inc(s_const, 1)
        do(g.memset(ident[:], 0.0))
        do(g.affine_select(out=ident[:], in_=ident[:], compare_op=ALU.not_equal, fill=1.0, base=0, pattern=[[-1, P]], channel_multiplier=1))
        g.sem_inc(s_const, 1)
        do(g.iota(iota_f[:], [[1, P]], base=0, channel_multiplier=0, allow_small_or_imprecise_dtypes=True))
        do(g.iota(tok_id[:], [[P, NT + 1]], base=0, channel_multiplier=1, allow_small_or_imprecise_dtypes=True))
        do(g.memset(logits[:], 0.0))
        do(g.memset(tri[:], 1.0))
        do(g.affine_select(out=tri[:], in_=tri[:], compare_op=ALU.is_gt, fill=0.0, base=0, pattern=[[1, P]], channel_multiplier=-1))
        do(g.memset(ones[:], 1.0))
        do(g.memset(mhalf[:], -0.5))
        do(g.memset(zeros[:], 0.0))
        g.sem_inc(s_const, 1)
        n_roots = 0

        def rstd(dst, src):
            nonlocal n_roots
            n_roots += 1
            g.wait_ge(s_ms, n_roots)
            do(g.tensor_scalar(dst, src, EPS, None, ALU.add))
            g.tensor_tensor(dst, dst, mhalf[:dst.shape[0], 0:dst.shape[1]], ALU.pow).then_inc(s_rs, 1)

        rstd(st[:, 16:20], st[:, 8:12])
        rstd(st[:, 2:3], st[:, 0:1])
        for t in range(NT + 1):
            R = ROWS[t]
            rstd(st[:R, 14:16], st[:R, 12:14])
            if t < NT:
                r = ROWS[t + 1]
                n = (t + 1) % 2
                rstd(st[:r, 2 + n:3 + n], st[:r, n:n + 1])
            for _ in kvs(t):
                rstd(st[:P, 32:40], st[:P, 32:40])
            if t:
                rstd(st[:P, 41:42], st[:P, 41:42])
            rstd(st[:R, 50:51], st[:R, 49:50])
            rstd(st[:R, 52:60], st[:R, 52:60])
        rstd(st[:DEC, 32:40], st[:DEC, 32:40])
        rstd(st[:DEC, 41:42], st[:DEC, 41:42])
        g.sem_inc(s_end1, 1)
        g.wait_ge(s_end1, 4)
        do(g.memset(mask_l[0:1, :], 0.0))
        do(g.memset(mask_l[0:1, 0:DEC], 1.0))
        do(g.memset(mask_r[0:1, :], NEG))
        g.sem_inc(s_setup2, 1)
        for s, t in enumerate(seq):
            if s:
                r = ROWS[seq[s - 1]]
                rstd(st2[:r, 42:43], st2[:r, 42:43])
            if s >= 2:
                r = ROWS[seq[s - 2]]
                rstd(st2[:r, 41:42], st2[:r, 40:41])
        rstd(st2[:, 42:43], st2[:, 42:43])
        for s in (LAST - 1, LAST):
            rstd(st2[:ROWS[seq[s]], 41:42], st2[:ROWS[seq[s]], 40:41])
        g.wait_ge(s_tab, 1)

        def gather(b, par, start):
            idx = rowtok_i[:, b:b + 1] if isinstance(b, int) else rowtok_i[:, bass.ds(b, 1)]
            if not start:
                g.wait_ge(s_xTp, b - 1)
            do(g.tensor_copy(gi[:, par:par + 1], idx))
            g.sem_inc(s_idx, 1)
            g.indirect_dma_start(xg[:, par], None, h2_d, bass.IndirectOffsetOnAxis(gi[:, par:par + 1].bitcast(U32), 0)).then_inc(s_xg[par], 16)

        gather(0, 0, True)
        gather(1, 1, True)
        with g.Fori(0, (NE - 2) // 2) as i:
            do.off = i * 2
            for u in range(2):
                gather(i * 2 + (2 + u), u, False)
        do.off = 0
        pool_step.n += (NE - 2) // 2 * 2 - 2
        n_ov = g.value_load(ovf_i[0:1, MAXOV:MAXOV + 1], min_val=0, max_val=MAXOV)
        n0 = pool_step.n
        def overflow(j):
            g.wait_ge(s_xTp, NE - 1 if isinstance(j, int) else j + NE)
            g.wait_ge(s_xg[0], j * 16 + 16 * (NE // 2))
            g.tensor_copy(gi[:, 0:1], rowtok_i[:, bass.ds(j + NE, 1)]).then_inc(pool_step.sem, 1)
            g.wait_ge(pool_step.sem, j + (n0 + 1))
            g.sem_inc(s_idx, 1)
            g.indirect_dma_start(xg[:, 0], None, h2_d, bass.IndirectOffsetOnAxis(gi[:, 0:1].bitcast(U32), 0)).then_inc(s_xg[0], 16)

        overflow_blocks(g, n_ov, overflow)
        g.wait_ge(s_end4, 1)
        for t in range(NT + 1):
            R = ROWS[t]
            if t >= YBUF:
                g.wait_ge(s_yo, t - YBUF + 1)
            for k, dst in enumerate((y1b, y2b)):
                g.indirect_dma_start(dst[:R, t % YBUF], None, yb_d, bass.IndirectOffsetOnAxis(pos_i2[:R, k, t:t + 1].bitcast(U32), 0)).then_inc(s_g1[t % YBUF], 16)

    @block.tensor
    def _(pe):
        mm = nc.tensor.matmul
        tr = lambda out, in_, r: nc.tensor.transpose(out, in_, ident[:r, :r])

        def ada(j):
            pe.wait_ge(s_ada[j % 3], 16 * (j // 3 + 1))
            if j == 0:
                pe.wait_ge(s_cact, 1)
            ps = b1.claim(pe, ("ada", j))
            for k in range(KD):
                ins = mm(ps[0:2, 0:ADA_COLS], c_act[:, k, :], ada_w[:, j % 3, k, :], start=(k == 0), stop=(k == KD - 1))
            b1.full(ins, ("ada", j))

        def adaT(js):
            for j in js:
                pe.wait_ge(s_aused[j % 3], j // 3 + 1)
            ps = b1.claim(pe, ("adaT", js[0]))
            for i, j in enumerate(js):
                for n in range(ADA_COLS // P):
                    c = 2 * (2 * i + n)
                    if j in DVE_ADA:
                        for v in range(2):
                            ins = mm(ps[:, c + v:c + v + 1], ada_acc[:, v, n * P:(n + 1) * P], ones[:, 0:1], start=True, stop=True)
                        continue
                    ins = tr(ps[:, c:c + 2], ada_rows(j)[:, n * P:(n + 1) * P], 2)
            b1.full(ins, ("adaT", js[0]))

        def kv(kt):
            R = P if kt != SAMPLE else DEC
            lhs = latT_c[:, kt - 9, :] if kt >= 9 else latT[:, 2, :R]
            for half in range(2):
                ps = b1.claim(pe, (f"kv{half}", kt))
                ins = mm(ps[:R, :], lhs, W_ukv[:, half * 512:(half + 1) * 512], start=True, stop=True)
                b1.full(ins, (f"kv{half}", kt))

        def xT_(t):
            R = ROWS[t]
            pe.wait_ge(s_xn, t + 1)
            for half in range(2):
                ps = b1.claim(pe, (f"xT{half}", t))
                for j in range(4):
                    k = 4 * half + j
                    ins = tr(ps[:, j * P:j * P + R], xn[:R, k * P:(k + 1) * P], R)
                b1.full(ins, (f"xT{half}", t))

        def proj(t, name, c0, n):
            R = ROWS[t]
            ps = b1.claim(pe, (name, t))
            for k in range(KD):
                ins = mm(ps[:R, 0:n], hT[:, t % 2, k, :R], W_in[:, k, c0:c0 + n], start=(k == 0), stop=(k == KD - 1))
            b1.full(ins, (name, t))

        def mix(t):
            R = ROWS[t]
            pe.wait_ge(s_vr, t + 1)
            if t == 0:
                pe.wait_ge(s_wsp, 1)
            ps = b1.claim(pe, ("mix", t))
            for h in range(H):
                ins = mm(ps[:R, h * 64:(h + 1) * 64], wspT[:R, h, :R], vrows[:R, h * 64:(h + 1) * 64], start=True, stop=True)
            b1.full(ins, ("mix", t))

        for j in range(SETUP_ADA):
            ada(j)
            if j == 1:
                pe.wait_ge(s_const, 2)
                pe.wait_ge(s_vec, 16 * 10)
                ps = b1.claim(pe, "vec")
                b1.full(tr(ps[:, 0:NVEC], vecs[0:NVEC, :], NVEC), "vec")
            if j:
                adaT([j - 1])
        adaT([SETUP_ADA - 1])
        xT_(0)
        pe.wait_ge(s_cn, 1)
        ps = b1.claim(pe, "cT")
        for c in range(NC_):
            ins = tr(ps[:, c * P:(c + 1) * P], cn[:, c, :], P)
        b1.full(ins, "cT")
        pe.wait_ge(s_params, 16 * 3)
        for half in range(2):
            ps = b1.claim(pe, f"wsp{half}")
            for j in range(4):
                ins = tr(ps[:, j * P:(j + 1) * P], wsp[:, 4 * half + j, :], P)
            b1.full(ins, f"wsp{half}")
        for t in range(NT + 1):
            R = ROWS[t]
            pe.wait_ge(s_hTa, t + 1)
            pe.wait_ge(s_hTv, t + 1)
            if t == 0:
                pe.wait_ge(s_wlat, 16)
            proj(t, "lat", 0, LAT)
            if t == 0:
                pe.wait_ge(s_cT, 1)
                pe.wait_ge(s_fold1, 1)
            for kt in kvs(t):
                kv(kt)
            if t == 0:
                pe.wait_ge(s_wgu, 16)
            proj(t, "u", LAT, GW)
            pe.wait_ge(s_latn, t + 1)
            ps = b1.claim(pe, ("latT", t))
            for j in range(3):
                ins = tr(ps[:, j * P:j * P + R], latn[:R, j * P:(j + 1) * P], R)
            b1.full(ins, ("latT", t))
            if t < NT:
                xT_(t + 1)
            if t:
                mix(t - 1)
                if t == 1:
                    pe.wait_ge(s_const, 3)
                adaT(loop_ada(t - 1))
            if t == 0:
                pe.wait_ge(s_wgv, 16)
            proj(t, "gv", LAT + GW, GW)
            if t < NT:
                for j in loop_ada(t)[:-1]:
                    ada(j)
            pe.wait_ge(s_latT, t + 1)
            if t == 0:
                pe.wait_ge(s_fold1, 2)
            for half in range(2):
                ps = b1.claim(pe, (f"q{half}", t))
                n = H * QK // 2
                for k in range(2):
                    ins = mm(ps[:R, 0:n], latT[:, k, :R], W_uq[:, k, half * n:(half + 1) * n], start=(k == 0), stop=(k == 1))
                b1.full(ins, (f"q{half}", t))
        for j in END_ADA[:2]:
            ada(j)
        kv(NT)
        mix(NT)
        for j in END_ADA[2:]:
            ada(j)
        adaT(END_ADA)
        pe.wait_ge(s_end1, 4)

        pe.wait_ge(s_fold, 1)
        pe.wait_ge(s_setup2, 1)
        nk, nv = 0, [0, 0]

        def S(s, h):
            t = seq[s]
            R, n = ROWS[t], nkeys(t)
            u = s * H + h
            bank = scores(u)
            k0 = slot0(t) * P
            if h == 0:
                pe.wait_ge(s_qkT, s + 1)
            if u >= 2:
                pe.wait_ge(s_prob, u - 1)
            for c0 in range(0, n, 512):
                m = min(512, n - c0)
                out = psum[bank + c0 // 512]
                final = c0 + m == n
                masked = final and t != SAMPLE
                ins = mm(out[:R, 0:m], qT[:, s % 2, h, :R], kT[:, h, k0 + c0:k0 + c0 + m], start=True, stop=not masked)
                if masked:
                    ins = mm(out[:R, m - DEC:m], mask_l[0:1, :R], mask_r[0:1, :], start=False, stop=True)
            ins.then_inc(s_S[u % 2], 1)

        def PT(s, h):
            t = seq[s]
            R, bl = ROWS[t], blocks(t)
            u = s * H + h
            pe.wait_ge(s_prob, u + 1)
            for j in range((len(bl) + 3) // 4):
                ps = b2.claim(pe, ("PT", t, h, j))
                for b, r in bl[4 * j:4 * j + 4]:
                    ins = tr(ps[:r, (b % 4) * P:(b % 4) * P + R], prob[:R, u % 2, b * P:b * P + r], R)
                b2.full(ins, ("PT", t, h, j))

        def O(s, h):
            t = seq[s]
            R, bl = ROWS[t], blocks(t)
            u = s * H + h
            pe.wait_ge(s_PT, u + 1)
            if h == 0:
                nv[s % 2] += len(key_tiles[t])
                pe.wait_ge(s_vl[s % 2], 16 * nv[s % 2])
            if h == 0 and s:
                pe.wait_ge(s_Ofree, s)
            for b, r in bl:
                ins = mm(psum[7][:R, h * VD:(h + 1) * VD], probT[:r, u % 2, b, :R], vall[:r, slot0(t) + b, h * VD:(h + 1) * VD],
                         start=(b == 0), stop=(b == len(bl) - 1))
            if h == H - 1:
                ins.then_inc(s_heads, 1)

        def mT_(s):
            t = seq[s]
            R = ROWS[t]
            pe.wait_ge(s_mrg, s + 1)
            for half in range(2):
                ps = b2.claim(pe, (f"mT{half}", t))
                for j in range(4):
                    ins = tr(ps[:, j * P:j * P + R], merged[:R, s % 2, (4 * half + j) * P:(4 * half + j + 1) * P], R)
                b2.full(ins, (f"mT{half}", t))

        def out_(s, part):
            R = ROWS[seq[s]]
            half, first, end = OUT_PARTS[part]
            if part == 0:
                pe.wait_ge(s_mT, s + 1)
            if first == 0 and (s or half):
                pe.wait_ge(s_yfree, 2 * s + half)
            for k in range(first, end):
                ins = mm(psum[6][:R, :], mT[:, k, :R], W_out[:, k, half * 512:(half + 1) * 512], start=(k == 0), stop=(k == KD - 1))
            if end == KD:
                ins.then_inc(s_y, 1)

        def h2T_(s):
            t = seq[s]
            R = ROWS[t]
            pe.wait_ge(s_h2, s + 1)
            for half in range(2):
                ps = b2.claim(pe, (f"h2T{half}", t))
                for j in range(4):
                    ins = tr(ps[:, j * P:j * P + R], h2[:R, (4 * half + j) * P:(4 * half + j + 1) * P], R)
                b2.full(ins, (f"h2T{half}", t))

        def router(s):
            t = seq[s]
            R = ROWS[t]
            pe.wait_ge(s_h2T, s + 1)
            if s == 0:
                pe.wait_ge(s_wr, 64)
            ps = b2.claim(pe, ("rt", t))
            for k in range(KD):
                ins = mm(ps[:R, 0:NG + NE], h2T[:, k, :R], w_r[:, k, :], start=(k == 0), stop=(k == KD - 1))
            b2.full(ins, ("rt", t))

        def prep(s):
            nonlocal nk
            t = seq[s]
            R = ROWS[t]
            for kt in key_tiles[t]:
                r = P if kt != SAMPLE else DEC
                pe.wait_ge(s_ld2["k"][nk % KBUF], 16 * (nk // KBUF + 1))
                for half in range(2):
                    ps = b2.claim(pe, (f"kT{half}", kt))
                    for j in range(4):
                        ins = tr(ps[:QK, j * P:j * P + r], kbuf[:r, nk % KBUF, 4 * half + j, :], r)
                    b2.full(ins, (f"kT{half}", kt))
                nk += 1
            pe.wait_ge(s_ld2["q"][s % 2], 16 * (s // 2 + 1))
            for half in range(2):
                ps = b2.claim(pe, (f"qT{half}", t))
                for j in range(4):
                    ins = tr(ps[:QK, j * P:j * P + R], qbuf[:R, s % 2, 4 * half + j, :], R)
                b2.full(ins, (f"qT{half}", t))

        def rows_of_vectors(s):
            for j in range(6):
                which, half = j // 2, j % 2
                ps = b2.claim(pe, ("bc", s, j))
                for i in range(4):
                    k = 4 * half + i
                    src = (modT[:, 16 + k, 1 - s:2 - s], A2T[:, k, 1 - s:2 - s], modT[:, 24 + k, 1 - s:2 - s])[which]
                    ins = tr(ps[:, i * P:(i + 1) * P], src.broadcast_to([P, P]), P)
                b2.full(ins, ("bc", s, j))

        work_of = {"prep": lambda s, i: prep(s), "vectors": lambda s, i: rows_of_vectors(s), "mT": lambda s, i: mT_(s),
                   "W_out": out_, "h2T": lambda s, i: h2T_(s), "router": lambda s, i: router(s)}
        prep(0)
        S(0, 0)
        S(0, 1)
        for s in range(len(seq)):
            for h in range(H):
                PT(s, h)
                if s * H + h + 2 < len(seq) * H:
                    S(s + (h + 2) // H, (h + 2) % H)
                for name, of, part in beside(s, h):
                    work_of[name](of, part)
                if s or h:
                    O(s - (h == 0), (h - 1) % H)
        O(LAST, H - 1)
        for name, of, part in closing:
            work_of[name](of, part)

        pe.wait_ge(s_end2, 4)
        for v in range(2):
            if v:
                pe.wait_ge(s_gmr, v)
            for half in range(2):
                for i in range(4):
                    k = 4 * half + i
                    ins = tr(psum[4 + half][:, i * P:(i + 1) * P], modT[:, 40 + k, v:v + 1].broadcast_to([P, P]), P)
            ins.then_inc(s_gmp, 1)
        pe.wait_ge(s_E, 1)
        flat = E[:].rearrange("p t e -> p (t e)")
        mm(psum[0][:, 0:(NT + 1) * NE], tri[:], flat, start=True, stop=True)
        mm(psum[1][:, 0:(NT + 1) * NE], ones[:], flat, start=True, stop=True).then_inc(s_rank, 1)
        for k in range(2):
            pe.wait_ge(s_hot, k + 1)
            for t in range(NT + 1):
                R = ROWS[t]
                ins = mm(psum[2][:, 0:2 * NB], onehot[:R, k, t, :], bhot[:R, k, t].rearrange("p a b -> p (a b)"),
                         start=(t == 0 and k == 0), stop=(t == NT and k == 1))
        ins.then_inc(s_tabp, 1)
        pe.wait_ge(s_gmr, 2)
        pe.wait_ge(s_tab, 1)

        def xT4(b, par, nth):
            pe.wait_ge(s_xg[par], nth)
            for half in range(2):
                for j in range(4):
                    k = 4 * half + j
                    ins = tr(psum[half][:, j * P:(j + 1) * P], xg[:, par, k * P:(k + 1) * P], P)
            ins.then_inc(s_xTp, 1)

        def gu(b, slot, nth):
            pe.wait_ge(s_xTa, b + 1)
            pe.wait_ge(s_xTv, b + 1)
            pe.wait_ge(s_wd[slot], nth)
            for k in range(KD):
                mm(psum[2][:, 0:DE], xT[:, k, :], WG[:, slot, k, :], start=(k == 0), stop=(k == KD - 1))
            for k in range(KD):
                ins = mm(psum[3][:, 0:DE], xT[:, k, :], WU[:, slot, k, :], start=(k == 0), stop=(k == KD - 1))
            ins.then_inc(s_gu, 1)

        def hT4(b):
            pe.wait_ge(s_hid, b + 1)
            for k in range(2):
                ins = tr(psum[4][:, k * P:(k + 1) * P], hid[:, k * P:(k + 1) * P], P)
            ins.then_inc(s_hTp, 1)

        def down(b, slot):
            pe.wait_ge(s_hTc, b + 1)
            if not isinstance(b, int) or b >= 1:
                pe.wait_ge(s_ya, b)
                pe.wait_ge(s_yv, b)
            for half in range(2):
                for k in range(2):
                    ins = mm(psum[5 + half][:], hidT[:, k, :], WD[:, slot, k, half * 512:(half + 1) * 512], start=(k == 0), stop=(k == 1))
            ins.then_inc(s_down, 1)

        xT4(0, 0, 16)
        gu(0, 0, 48)
        xT4(1, 1, 16)
        with pe.Fori(0, (NE - SLOTS) // SLOTS) as i:
            for u in range(SLOTS):
                b = i * SLOTS + u
                hT4(b)
                gu(b + 1, (u + 1) % SLOTS, i * 48 + (48 if u + 1 < SLOTS else 96))
                xT4(b + 2, u % 2, i * 32 + 16 * ((u + 2) // 2 + 1))
                down(b, u)
        for b in range(NE - SLOTS, NE):
            hT4(b)
            if b + 1 < NE:
                gu(b + 1, (b + 1) % SLOTS, 48 * ((b + 1) // SLOTS + 1))
            if b + 2 < NE:
                xT4(b + 2, b % 2, 16 * ((b + 2) // 2 + 1))
            down(b, b % SLOTS)
        n_ov = pe.value_load(ovf_i[0:1, MAXOV:MAXOV + 1], min_val=0, max_val=MAXOV)
        def overflow(j):
            xT4(j + NE, 0, j * 16 + 16 * (NE // 2 + 1))
            gu(j + NE, 0, j * 48 + 48 * (NE // SLOTS + 1))
            hT4(j + NE)
            down(j + NE, 0)

        overflow_blocks(pe, n_ov, overflow)

    def x2_squares(act, s, do, sig):
        R = ROWS[seq[s]]
        act.wait_ge(s_x2, s + 1)
        do(nc.scalar.activation(junk2[:R], x_att[:R, s % 2], ACT.Square, scale=D ** -0.5, accum_out=st2[:R, 40:41]), sig[id(s_x2sq)])

    @block.scalar
    def _(act):
        do = Serial(act, act_step)
        A = nc.scalar.activation
        sig = {id(x): Signal(x) for x in (s_ss, s_hTa, s_lat, s_sqk, s_u, s_gv, s_sqq, s_prob, s_x2sq)}
        rows = [(R_BADA, w["b_ada"][0].rearrange("(r n) -> r n", n=P), 48), (R_G1, w["g_norm_mix"][0].rearrange("(r n) -> r n", n=P), 8),
                (R_G2, w["g_norm_ffn"][0].rearrange("(r n) -> r n", n=P), 8), (R_GQL, w["g_q_lat"][0].rearrange("(r n) -> r n", n=P), 2),
                (R_GKV, w["g_kv_lat"], 1), (R_GOA, w["g_out_attn"][0].rearrange("(r n) -> r n", n=P), 4),
                (R_GOG, w["g_out_gmlp"][0].rearrange("(r n) -> r n", n=P), 4), (R_BSP, w["b_spatial"][0], 8)]
        act.wait_ge(s_const, 1)
        for r, src, k in rows:
            act.dma_start(vecs[r:r + k, :], src).then_inc(s_vec, 16)
        for r, name in ((R_GQ, "g_qnorm"), (R_GK, "g_knorm")):
            act.dma_start(vecs[r:r + 1, 0:QK], w[name]).then_inc(s_vec, 16)
        act.wait_ge(s_c, 32)
        do(A(c_act[:].rearrange("p k v -> p v k"), c_in[:], ACT.Silu), Signal(s_cact))
        act.dma_start(rope_q[:], w["rope_table"].rearrange("(t p) c -> p t c", p=P)).then_inc(s_rope, 16)
        for i, name in enumerate(("g_qnorm", "g_knorm")):
            for to, frm, k in ((0, 0, RD), (RD, RD // 2, RD // 2), (RD + RD // 2, 0, RD // 2)):
                act.dma_start(grope[:, i, to:to + k], bcast(w[name][:, ND + frm:ND + frm + k], [P, k])).then_inc(s_rope, 16)
        act.dma_start(wsp[:], w["w_spatial"][0].rearrange("h t s -> t h s")).then_inc(s_params, 16)
        act.dma_start(ln_g[:], bcast(w["g_ln_v"], [P, GW])).then_inc(s_params, 16)
        act.dma_start(ln_b[:], bcast(w["b_ln_v"], [P, GW])).then_inc(s_params, 16)

        def done(ins, sem):
            ins.then_inc(sem, 1)

        def kv(kt):
            R = P if kt != SAMPLE else DEC
            n = key_order.index(kt)
            for half in range(2):
                ps = b1.read(act, (f"kv{half}", kt))
                v = ps[:R].rearrange("p (h n) -> p h n", n=ND + VD)
                if n >= 1 and half == 0:
                    act.wait_ge(s_kh, n)
                if n >= 2 and half == 0:
                    act.wait_ge(s_out1[f"v{n % 2}"], 16 * (n // 2))
                done(A(sq_k[:R, 4 * half:4 * half + 4], v[:, :, 0:ND], ACT.Square), b1.free((f"kv{half}", kt)))
                done(A(vh[:R, n % 2, 4 * half:4 * half + 4], v[:, :, ND:], ACT.Copy), b1.free((f"kv{half}", kt)))
            act.wait_ge(b1.free(("kv1", kt)), b1.at[("kv1", kt)][2] + 2)
            act.wait_ge(b1.free(("kv0", kt)), b1.at[("kv0", kt)][2] + 2)
            act.sem_inc(s_sqk, 1)

        def x_squares(t):
            R = ROWS[t]
            act.wait_ge(s_x[t % 2], 16 * (t // 2 + 1))
            do(A(junk[:R], xbuf[:R, t % 2], ACT.Square, scale=D ** -0.5, accum_out=st[:R, t % 2:t % 2 + 1]), sig[id(s_ss)])

        def hT_half(t):
            R = ROWS[t]
            v = prompt_or_sample(t)
            if t == 0:
                act.wait_ge(s_A1, 1)
            ps = b1.read(act, ("xT1", t))
            for j in range(4):
                k = 4 + j
                ins = A(hT[:, t % 2, k, :R], ps[:, j * P:j * P + R], ACT.Identity, bias=modT[:, k, v:v + 1], scale=A1[:, k, v:v + 1])
                if j < 3:
                    do(ins)
                else:
                    ins.then_inc(b1.free(("xT1", t)), 1)
            act.wait_ge(b1.free(("xT1", t)), b1.at[("xT1", t)][2] + 1)
            act.sem_inc(s_hTa, 1)


        def ada(j):
            ps = b1.read(act, ("ada", j))
            if j >= 2 and j not in END_ADA:
                act.wait_ge(s_modT, j - 1)
            ins = A(ada_rows(j), ps[0:2, 0:ADA_COLS], ACT.Copy)
            done(ins, b1.free(("ada", j)))
            act.wait_ge(b1.free(("ada", j)), b1.at[("ada", j)][2] + 1)
            act.sem_inc(s_aused[j % 3], 1)

        for j in range(SETUP_ADA):
            ada(j)
            if j == 1:
                act.wait_ge(s_cache, 32)
                for c in range(NC_):
                    do(A(junk[:, 0:KVL], cck[:, c, 0:KVL], ACT.Square, scale=KVL ** -0.5, accum_out=st[:, 8 + c:9 + c]))
                act.sem_inc(s_css, 1)
            if j == 3:
                x_squares(0)
        hT_half(0)
        for t in range(NT + 1):
            R = ROWS[t]
            ps = b1.read(act, ("lat", t))
            if t >= 2:
                act.wait_ge(s_out1[f"lat{t % 2}"], 32 * (t // 2))
                act.wait_ge(s_kh, key_order.index(t - 2) + 1)
            done(A(lat[:R, t % 2], ps[:R, 0:LAT], ACT.Copy), b1.free(("lat", t)))
            act.wait_ge(b1.free(("lat", t)), b1.at[("lat", t)][2] + 1)
            act.sem_inc(s_lat, 1)
            if t:
                act.wait_ge(s_latn, t)
            do(A(junk[:R, 0:QL], lat[:R, t % 2, 0:QL], ACT.Square, scale=QL ** -0.5, accum_out=st[:R, 12:13]))
            do(A(junk[:R, 0:KVL], lat[:R, t % 2, QL:QL + KVL], ACT.Square, scale=KVL ** -0.5, accum_out=st[:R, 13:14]))
            act.sem_inc(s_lss, 1)
            if t < NT:
                x_squares(t + 1)
            for kt in kvs(t):
                kv(kt)
            ps = b1.read(act, ("u", t))
            if t >= 2:
                act.wait_ge(s_gm, t - 1)
            done(A(u_sb[:R, t % 2], ps[:R, :], ACT.Gelu_apprx_tanh), b1.free(("u", t)))
            act.wait_ge(b1.free(("u", t)), b1.at[("u", t)][2] + 1)
            act.sem_inc(s_u, 1)
            if t < NT:
                hT_half(t + 1)
            ps = b1.read(act, ("gv", t))
            if t:
                act.wait_ge(s_vr, t)
            done(A(gv[:R], ps[:R, :], ACT.Gelu_apprx_tanh), b1.free(("gv", t)))
            act.wait_ge(b1.free(("gv", t)), b1.at[("gv", t)][2] + 1)
            act.sem_inc(s_gv, 1)
            if t < NT:
                for j in loop_ada(t)[:-1]:
                    ada(j)
            if t:
                act.wait_ge(s_qh, t)
            for half in range(2):
                ps = b1.read(act, (f"q{half}", t))
                done(A(sq_q[:R, 4 * half:4 * half + 4], ps[:R, 0:384].rearrange("p (h n) -> p h n", n=QK), ACT.Square), b1.free((f"q{half}", t)))
            for half in range(2):
                act.wait_ge(b1.free((f"q{half}", t)), b1.at[(f"q{half}", t)][2] + 1)
            act.sem_inc(s_sqq, 1)
        for j in END_ADA[:2]:
            ada(j)
        kv(NT)
        for j in END_ADA[2:]:
            ada(j)
        act.sem_inc(s_end1, 1)
        act.wait_ge(s_end1, 4)

        nk = 0

        def turn(tag, half, dst, r, par=0):
            ps = b2.read(act, tag)
            src = ps[:QK, :].rearrange("p (h n) -> p h n", n=P)[:, :, :r]
            if dst is None:
                ins = A(qT[:, par, 4 * half:4 * half + 4, :r], src, ACT.Copy, scale=gqk[0:QK, 0:1])
            else:
                ins = A(kT[:, 4 * half:4 * half + 4, dst:dst + r], src, ACT.Copy)
            ins.then_inc(b2.free(tag), 1)
            act.wait_ge(b2.free(tag), b2.at[tag][2] + 1)

        act.wait_ge(s_fold, 1)
        def prep(s):
            t = seq[s]
            for kt in key_tiles[t]:
                r = P if kt != SAMPLE else DEC
                turn(("kT0", kt), 0, kslot(t, kt) * P, r)
                turn(("kT1", kt), 1, kslot(t, kt) * P, r)
                act.sem_inc(s_keys, 1)
            if s >= 2:
                act.wait_ge(s_heads, s - 1)
            turn(("qT0", t), 0, None, ROWS[t], s % 2)
            turn(("qT1", t), 1, None, ROWS[t], s % 2)
            act.sem_inc(s_qkT, 1)

        def exps(s, h):
            t = seq[s]
            R, n, u, c = ROWS[t], nkeys(t), s * H + h, sums(s) + h
            act.wait_ge(s_nmax, u + 1)
            if u >= 2:
                act.wait_ge(s_PT, u - 1)
            bank = scores(u)
            if n > 512:
                do(A(prob[:R, u % 2, 0:512], psum[bank][:R, :], ACT.Exp, bias=st2[:R, h:h + 1], accum_out=st2[:R, c:c + 1]))
                do(A(prob[:R, u % 2, 512:n], psum[bank + 1][:R, 0:n - 512], ACT.Exp, bias=st2[:R, h:h + 1], accum_out=st2[:R, c + 8:c + 9]), sig[id(s_prob)])
            else:
                do(A(prob[:R, u % 2, 0:n], psum[bank][:R, 0:n], ACT.Exp, bias=st2[:R, h:h + 1], accum_out=st2[:R, c:c + 1]), sig[id(s_prob)])

        prep(0)
        for s in range(len(seq)):
            for h in range(H):
                exps(s, h)
                if s >= 2 and h == 3:
                    x2_squares(act, s - 2, do, sig)
                for name, of, _ in beside(s, h):
                    if name == "prep":
                        prep(of)
        for s in (LAST - 1, LAST):
            x2_squares(act, s, do, sig)
        act.sem_inc(s_end2, 1)
        act.wait_ge(s_end2, 4)

        for v in range(2):
            act.wait_ge(s_gmp, v + 1)
            for half in range(2):
                do(A(gate_m[:, v, half * 512:(half + 1) * 512], psum[4 + half][:], ACT.Copy))
            act.sem_inc(s_gmr, 1)
        act.wait_ge(s_rx, 1)
        do(A(rt[:, 1, :, 0:NG], rt[:, 0, :, 0:NG], ACT.Exp))
        do(A(rt[:, 3, :, 0:1], rt[:, 2, :, 0:1], ACT.Exp))
        act.sem_inc(s_ry, 1)
        do(A(sg[0:1, 0:1], ident[0:1, 0:1], ACT.Silu))
        act.wait_ge(s_tab, 1)

        def xT_half(b):
            act.wait_ge(s_xTp, b + 1)
            A(xT[:, 4:8, :], psum[1][:].rearrange("p (k n) -> p k n", n=P), ACT.Copy).then_inc(s_xTa, 1)
            act.wait_ge(s_xTa, b + 1)

        def silu(b):
            act.wait_ge(s_gu, b + 1)
            if not isinstance(b, int) or b >= 1:
                act.wait_ge(s_hid, b)
            A(sg[:], psum[2][:, 0:DE], ACT.Silu).then_inc(s_sg, 1)
            act.wait_ge(s_sg, b + 1)

        def y_half(b, par, nth):
            act.wait_ge(s_down, b + 1)
            if nth is not None:
                act.wait_ge(s_yst[par], nth)
            ww = roww[:, b:b + 1] if isinstance(b, int) else roww[:, bass.ds(b, 1)]
            A(yb[:, par, 0:512], psum[5][:], ACT.Copy, scale=ww).then_inc(s_ya, 1)

        xT_half(0)
        silu(0)
        xT_half(1)
        for b in range(2):
            silu(b + 1)
            xT_half(b + 2)
            y_half(b, b % 2, None)
        with act.Fori(0, (NE - SLOTS) // 2) as i:
            for u in range(2):
                b = i * 2 + (2 + u)
                silu(b + 1)
                xT_half(b + 2)
                y_half(b, u, i * 16 + 16)
        for b in range(NE - 2, NE):
            if b + 1 < NE:
                silu(b + 1)
            y_half(b, b % 2, 16 * (b // 2))
        n_ov = act.value_load(ovf_i[0:1, MAXOV:MAXOV + 1], min_val=0, max_val=MAXOV)
        def overflow(j):
            b = j + NE
            xT_half(b)
            silu(b)
            y_half(b, 0, j * 16 + 16 * (NE // 2))

        overflow_blocks(act, n_ov, overflow)

    @block.vector
    def _(dve):
        do = Serial(dve, dve_step)
        V = nc.vector

        def signal(s):
            dve.sem_inc(s, 1)

        def rstd(beside=0, n=[0]):
            n[0] += 1
            dve.sem_inc(s_ms, 1)
            ada_products(beside)
            dve.wait_ge(s_rs, n[0])

        def last_read(ins, tag, banks=b1):
            ins.then_inc(banks.free(tag), 1)
            b, _, before = banks.at[tag]
            nread[tag] = nread.get(tag, 0) + 1
            dve.wait_ge(banks.free(tag), before + nread[tag] + (others.get(tag[0] if isinstance(tag, tuple) else tag, 0)))

        nread = {}
        others = {"kv0": 2, "kv1": 2, "q0": 1, "q1": 1}

        def lat_norm(R, lat_ap, dst_q, dst_c, sq, sc):
            do(V.tensor_scalar(dst_q, lat_ap[:, 0:QL], sq, None, ALU.mult))
            do(V.tensor_scalar(dst_c, lat_ap[:, QL:QL + KVL], sc, None, ALU.mult))

        dve.wait_ge(s_cact, 1)
        ps = b1.read(dve, "vec")
        last_read(V.tensor_copy(vT[:, 0:NVEC], ps[:, 0:NVEC]), "vec")
        def ada(js):
            tag = ("adaT", js[0])
            n = 2 * len(js)
            c = 2 * js[0]
            ps = b1.read(dve, tag)
            last_read(V.tensor_tensor(modT[:, c:c + n, :], ps[:, 0:2 * n].rearrange("p (n v) -> p n v", v=2),
                                      bcast(vT[:, R_BADA + c:R_BADA + c + n].unsqueeze(2), [P, n, 2]), ALU.add), tag)
            dve.sem_inc(s_modT, len(js))

        ada_at = [0, 0, 0, 0]

        def ada_products(n):
            for _ in range(n):
                t, i = ada_at[0] // (2 * KD), ada_at[0] % (2 * KD)
                if t >= ada_at[3]:
                    return
                j, k, v = DVE_ADA[t], i // 2, i % 2
                if i == 0:
                    dve.wait_ge(s_ada[j % 3], 16 * (j // 3 + 1))
                chunk, c = ada_w[:, j % 3, k, :], c_act[:, k, v:v + 1]
                if k == 0:
                    ins = V.tensor_scalar(ada_acc[:, v], chunk, c, None, ALU.mult)
                else:
                    dve.wait_ge(dve_step.sem, ada_at[1 + v])
                    ins = V.scalar_tensor_tensor(ada_acc[:, v], chunk, c, ada_acc[:, v], ALU.mult, ALU.add)
                ins.then_inc(dve_step.sem, 1)
                dve_step.n += 1
                ada_at[1 + v] = dve_step.n
                ada_at[0] += 1
                if i == 2 * KD - 1:
                    dve.wait_ge(dve_step.sem, dve_step.n)
                    dve.sem_inc(s_aused[j % 3], 1)

        def x_norm(t):
            R = ROWS[t]
            dve.wait_ge(s_ss, t + 1)
            rstd(2)
            do(V.tensor_scalar(xn[:R], xbuf[:R, t % 2], st[:R, 2 + t % 2:3 + t % 2], None, ALU.mult))
            signal(s_xn)

        def hT_half(t):
            R = ROWS[t]
            v = prompt_or_sample(t)
            ps = b1.read(dve, ("xT0", t))
            for k in range(4):
                ins = V.tensor_scalar(hT[:, t % 2, k, :R], ps[:, k * P:k * P + R], A1[:, k, v:v + 1], modT[:, k, v:v + 1], ALU.mult, ALU.add)
                if k < 3:
                    do(ins)
                else:
                    last_read(ins, ("xT0", t))
            signal(s_hTv)

        def turn(dst, src, table, pt, R, n):
            C = bcast(table[:R, pt:pt + 1, 0:RD], [R, n, RD])
            half = RD // 2
            do(V.tensor_tensor(rot[:R, 0:n], src, C, ALU.mult))
            for i in range(2):
                Sn = bcast(table[:R, pt:pt + 1, RD + half * i:RD + half * (i + 1)], [R, n, half])
                do(V.tensor_tensor(rot2[:R, 0:n, half * i:half * (i + 1)], src[:, :, half * (1 - i):half * (2 - i)], Sn, ALU.mult))
            do(V.tensor_tensor(dst, rot[:R, 0:n], rot2[:R, 0:n], ALU.add))

        def kv(kt):
            R = P if kt != SAMPLE else DEC
            n = key_order.index(kt)
            if kt >= 9:
                kr = cck[:R, kt - 9:kt - 8, KVL:KVL + RD]
                pt = kt - 9
            else:
                kr = lat[:R, kt % 2:kt % 2 + 1, QL + KVL:LAT]
                pt = kt if kt < NT else NC_
            turn(krot[:R].unsqueeze(1), kr, rope_k, pt, R, 1)
            do(V.tensor_tensor_reduce(ctmp[:R], kr[:, 0, :], kr[:, 0, :], 1.0, 0.0, ALU.mult, ALU.add, st[:R, 30:31]))
            dve.wait_ge(s_sqk, n + 1)
            do(V.tensor_reduce(st[:R, 32:40], sq_k[:R], AXX, ALU.add))
            do(V.tensor_scalar(st[:R, 32:40], st[:R, 32:40], st[:R, 30:31], 1.0 / QK, ALU.add, ALU.mult))
            rstd(4)
            if n >= 2:
                dve.wait_ge(s_out1[f"k{n % 2}"], 16 * (n // 2))
            for half in range(2):
                ps = b1.read(dve, (f"kv{half}", kt))
                v = ps[:R].rearrange("p (h n) -> p h n", n=ND + VD)[:, :, 0:ND]
                last_read(V.tensor_tensor(kh[:R, n % 2, 4 * half:4 * half + 4, 0:ND], v,
                                          bcast(st[:R, 32 + 4 * half:36 + 4 * half].unsqueeze(2), [R, 4, ND]), ALU.mult), (f"kv{half}", kt))
            do(V.tensor_tensor(kh[:R, n % 2, :, ND:], bcast(krot[:R].unsqueeze(1), [R, H, RD]), bcast(st[:R, 32:40].unsqueeze(2), [R, H, RD]), ALU.mult))
            signal(s_kh)

        for j in range(SETUP_ADA):
            ada([j])
            if j == 1:
                dve.wait_ge(s_css, 1)
                rstd()
                for c in range(NC_):
                    do(V.tensor_scalar(cn[:, c, :], cck[:, c, 0:KVL], st[:, 16 + c:17 + c], None, ALU.mult))
                signal(s_cn)
            if j == 3:
                x_norm(0)
        do(V.tensor_scalar(A1[:], modT[:, 8:16, :], 1.0, None, ALU.add))
        do(V.tensor_tensor(A1[:], A1[:], bcast(vT[:, R_G1:R_G1 + 8].unsqueeze(2), [P, KD, 2]), ALU.mult))
        signal(s_A1)
        hT_half(0)
        ps = b1.read(dve, "cT")
        last_read(V.tensor_copy(latT_c[:], ps[:].rearrange("p (h n) -> p h n", n=P)), "cT")
        signal(s_cT)
        dve.wait_ge(s_wkv, 16)
        do(V.tensor_scalar(W_ukv[:], W_ukv[:], vT[:, R_GKV:R_GKV + 1], None, ALU.mult))
        signal(s_fold1)
        dve.wait_ge(s_rope, 16 * 7)
        do(V.tensor_tensor(rope_k[:], rope_q[:], bcast(grope[:, 1:2, :], [P, NT, 2 * RD]), ALU.mult))
        do(V.tensor_tensor(rope_q[:], rope_q[:], bcast(grope[:, 0:1, :], [P, NT, 2 * RD]), ALU.mult))

        def late_constants():
            dve.wait_ge(s_params, 16 * 3)
            for half in range(2):
                ps = b1.read(dve, f"wsp{half}")
                last_read(V.tensor_copy(wspT[:, 4 * half:4 * half + 4, :], ps[:].rearrange("p (h n) -> p h n", n=P)), f"wsp{half}")
            do(V.memset(wspT[DEC:P, :, 0:DEC], 0.0))
            signal(s_wsp)
            dve.wait_ge(s_wuq, 16)
            for k in range(2):
                do(V.tensor_scalar(W_uq[:, k], W_uq[:, k], vT[:, R_GQL + k:R_GQL + k + 1], None, ALU.mult))
            signal(s_fold1)

        def mix(t):
            R = ROWS[t]
            ps = b1.read(dve, ("mix", t))
            if t:
                dve.wait_ge(s_out1["gm"], 16 * t)
            last_read(V.tensor_tensor(gm[:R].rearrange("p (h n) -> p h n", n=64), ps[:R].rearrange("p (h n) -> p h n", n=64),
                                      bcast(vT[:R, R_BSP:R_BSP + 8].unsqueeze(2), [R, H, 64]), ALU.add), ("mix", t))
            do(V.tensor_tensor(gm[:R], gm[:R], u_sb[:R, t % 2], ALU.mult))
            do(V.tensor_tensor_reduce(u_sb[:R, t % 2], gm[:R], gm[:R], 1.0 / GW, 0.0, ALU.mult, ALU.add, st[:R, 41:42]))
            rstd(2)
            do(V.tensor_scalar(gm[:R], gm[:R], st[:R, 41:42], None, ALU.mult))
            signal(s_gm)

        for t in range(NT + 1):
            R = ROWS[t]
            dve.wait_ge(s_lss, t + 1)
            rstd(2)
            lat_norm(R, lat[:R, t % 2], latn[:R, 0:QL], latn[:R, QL:], st[:R, 14:15], st[:R, 15:16])
            signal(s_latn)
            if t < NT:
                x_norm(t + 1)
            for kt in kvs(t):
                kv(kt)
            if t == 0:
                late_constants()
            ps = b1.read(dve, ("latT", t))
            last_read(V.tensor_copy(latT[:, :, :R], ps[:, 0:3 * P].rearrange("p (k n) -> p k n", n=P)[:, :, :R]), ("latT", t))
            signal(s_latT)
            if t < NT:
                hT_half(t + 1)
            if t:
                ada_products(2 * KD)
                mix(t - 1)
                ada(loop_ada(t - 1))
            ada_at[3] = min(t + 1, NT)
            dve.wait_ge(s_gv, t + 1)
            do(V.bn_stats(st[:R, 42:48], gv[:R]))
            do(V.bn_aggr(st[:R, 48:50], st[:R, 42:48]))
            rstd(2)
            do(V.tensor_scalar(gv[:R], gv[:R], st[:R, 48:49], st[:R, 50:51], ALU.subtract, ALU.mult))
            do(V.tensor_tensor(vrows[:R], gv[:R], ln_g[:R], ALU.mult))
            do(V.tensor_tensor(vrows[:R], vrows[:R], ln_b[:R], ALU.add))
            signal(s_vr)
            dve.wait_ge(s_sqq, t + 1)
            do(V.tensor_reduce(st[:R, 52:60], sq_q[:R], AXX, ALU.add))
            do(V.tensor_scalar(st[:R, 52:60], st[:R, 52:60], 1.0 / QK, None, ALU.mult))
            rstd(4)
            if t:
                dve.wait_ge(s_out1["q"], 16 * t)
            for half in range(2):
                ps = b1.read(dve, (f"q{half}", t))
                last_read(V.tensor_tensor(qh[:R, 4 * half:4 * half + 4], ps[:R, 0:384].rearrange("p (h n) -> p h n", n=QK),
                                          bcast(st[:R, 52 + 4 * half:56 + 4 * half].unsqueeze(2), [R, 4, QK]), ALU.mult), (f"q{half}", t))
            turn(qh[:R, :, ND:], qh[:R, :, ND:], rope_q, t if t < NT else NC_, R, H)
            signal(s_qh)
            ada_products(4)
            if t:
                k = t - 1
                if k == 0:
                    dve.wait_ge(s_wout, 16)
                do(V.tensor_scalar(W_out[:, k], W_out[:, k], vT[:, R_GOA + k:R_GOA + k + 1], None, ALU.mult))
        kv(NT)
        mix(NT)
        ada(END_ADA)
        signal(s_end1)
        dve.wait_ge(s_end1, 4)

        do(V.tensor_tensor(gqk[0:ND], vT[0:ND, R_GQ:R_GQ + 1], vT[0:ND, R_GK:R_GK + 1], ALU.mult))
        do(V.memset(gqk[ND:QK], 1.0))
        do(V.tensor_scalar(gqk[0:QK], gqk[0:QK], QK ** -0.5, None, ALU.mult))
        do(V.tensor_scalar(A2T[:], modT[:, 32:40, :], 1.0, None, ALU.add))
        do(V.tensor_tensor(A2T[:], A2T[:], bcast(vT[:, R_G2:R_G2 + 8].unsqueeze(2), [P, KD, 2]), ALU.mult))
        signal(s_fold)
        perm = lambda ap: ap.rearrange("p (k q) -> p q k", q=P)

        rows_a = [(gate_a, A2, B2), [bc_next[:, j] for j in range(3)]]
        rows_of = lambda s: rows_a[0 if seq[s] == SAMPLE else 1]

        def residual(s, half):
            R = ROWS[seq[s]]
            c = slice(half * 512, (half + 1) * 512)
            dve.wait_ge(s_y, 2 * s + half + 1)
            do(V.tensor_tensor(tmp2[:R, c], psum[6][:R], rows_of(s)[0][:R, c], ALU.mult))
            signal(s_yfree)
            if half:
                dve.wait_ge(s_ld2["x"][s % 2], 16 * (s // 2 + 1))
                do(V.tensor_tensor(x_att[:R, s % 2], x_att[:R, s % 2], tmp2[:R], ALU.add))
                signal(s_x2)

        def tail_norm(s):
            R = ROWS[seq[s]]
            dve.wait_ge(s_x2sq, s + 1)
            rstd()
            do(V.scalar_tensor_tensor(tmp2[:R], x_att[:R, s % 2], st2[:R, 41:42], rows_of(s)[1][:R], ALU.mult, ALU.mult))
            if s:
                dve.wait_ge(s_st2["h2"], 16 * s)
            do(V.tensor_tensor(perm(h2[:R]), tmp2[:R].rearrange("p (q k) -> p q k", k=KD), rows_of(s)[2][:R].rearrange("p (q k) -> p q k", k=KD), ALU.add))
            signal(s_h2)

        def h2T_(s):
            t = seq[s]
            R = ROWS[t]
            for half in range(2):
                tag = (f"h2T{half}", t)
                ps = b2.read(dve, tag)
                last_read(V.tensor_copy(h2T[:, 4 * half:4 * half + 4, :R], ps[:].rearrange("p (k n) -> p k n", n=P)[:, :, :R]), tag, b2)
            signal(s_h2T)

        def router(s):
            t = seq[s]
            R = ROWS[t]
            if s == 0:
                dve.wait_ge(s_wr, 64)
            ps = b2.read(dve, ("rt", t))
            last_read(V.tensor_tensor(logits[:R, t, :], ps[:R, 0:NG + NE], b_r[:R], ALU.add), ("rt", t), b2)

        def mT_(s):
            t = seq[s]
            R = ROWS[t]
            for half in range(2):
                tag = (f"mT{half}", t)
                ps = b2.read(dve, tag)
                last_read(V.tensor_copy(mT[:, 4 * half:4 * half + 4, :R], ps[:].rearrange("p (k n) -> p k n", n=P)[:, :, :R]), tag, b2)
            signal(s_mT)

        def row_max(s, h):
            t = seq[s]
            u = s * H + h
            R, n, bank = ROWS[t], nkeys(t), scores(u)
            dve.wait_ge(s_S[u % 2], u // 2 + 1)
            if n > 512:
                do(V.tensor_reduce(st2[:R, 8:9], psum[bank][:R, :], AXX, ALU.max))
                do(V.tensor_reduce(st2[:R, 9:10], psum[bank + 1][:R, 0:n - 512], AXX, ALU.max))
                do(V.tensor_scalar(st2[:R, h:h + 1], st2[:R, 8:9], st2[:R, 9:10], -1.0, ALU.max, ALU.mult))
            else:
                do(V.tensor_reduce(st2[:R, 8:9], psum[bank][:R, 0:n], AXX, ALU.max))
                do(V.tensor_scalar(st2[:R, h:h + 1], st2[:R, 8:9], -1.0, None, ALU.mult))
            signal(s_nmax)

        def PT(s, h):
            t = seq[s]
            R, u = ROWS[t], s * H + h
            for j in range((len(blocks(t)) + 3) // 4):
                tag = ("PT", t, h, j)
                ps = b2.read(dve, tag)
                bl = blocks(t)[4 * j:4 * j + 4]
                full = [b for b in bl if b[1] == P]
                part = [b for b in bl if b[1] < P]
                src = ps[:].rearrange("p (k n) -> p k n", n=P)
                ops = []
                if full:
                    ops.append(V.tensor_copy(probT[:, u % 2, 4 * j:4 * j + len(full), :R], src[:, 0:len(full), :R]))
                    if part:
                        do(ops.pop())
                for b, r in part:
                    ops.append(V.tensor_copy(probT[:r, u % 2, b, :R], src[:r, b % 4, :R]))
                last_read(ops[-1], tag, b2)
            signal(s_PT)

        def attention_rows(s):
            t = seq[s]
            R, c = ROWS[t], sums(s)
            if nkeys(t) > 512:
                do(V.tensor_tensor(st2[:R, c:c + 8], st2[:R, c:c + 8], st2[:R, c + 8:c + 16], ALU.add))
            do(V.reciprocal(st2[:R, c:c + 8], st2[:R, c:c + 8]))
            dve.wait_ge(s_heads, s + 1)
            do(V.tensor_tensor(attn[:R].rearrange("p (h n) -> p h n", n=VD), psum[7][:R].rearrange("p (h n) -> p h n", n=VD),
                               bcast(st2[:R, c:c + 8].unsqueeze(2), [R, H, VD]), ALU.mult))
            signal(s_Ofree)
            do(V.tensor_tensor_reduce(junk_v2[:R], attn[:R], attn[:R], 1.0 / GW, 0.0, ALU.mult, ALU.add, st2[:R, 42:43]))
            rstd()
            do(V.tensor_scalar(merged[:R, s % 2, 0:GW], attn[:R], st2[:R, 42:43], None, ALU.mult))
            dve.wait_ge(s_ld2["gm"][s % 2], 16 * (s // 2 + 1))
            signal(s_mrg)

        def rows_of_vectors(s):
            for j in range(6):
                ps = b2.read(dve, ("bc", s, j))
                last_read(V.tensor_copy(rows_a[s][j // 2][:, (j % 2) * 512:(j % 2 + 1) * 512], ps[:]), ("bc", s, j), b2)

        def work(name, of, part):
            if name == "vectors":
                rows_of_vectors(of)
            if name == "mT":
                mT_(of)
            if name == "W_out" and OUT_PARTS[part][2] == KD:
                residual(of, OUT_PARTS[part][0])
            if name == "h2T":
                h2T_(of)
            if name == "router":
                router(of)

        row_max(0, 0)
        row_max(0, 1)
        for s in range(len(seq)):
            for h in range(H):
                PT(s, h)
                if s * H + h + 2 < len(seq) * H:
                    row_max(s + (h + 2) // H, (h + 2) % H)
                for job in beside(s, h):
                    work(*job)
                if s and h == 0:
                    attention_rows(s - 1)
                if s >= 2 and h == 4:
                    tail_norm(s - 2)
        attention_rows(LAST)
        for i, job in enumerate(closing):
            if i == 4:
                tail_norm(LAST - 1)
            if job == ("h2T", LAST, 0):
                tail_norm(LAST)
            work(*job)
        dve.sem_inc(s_end2, 2)
        dve.wait_ge(s_end2, 4)

        NTT = NT + 1
        T = lambda i, n=EG: rt[:, i, :, 0:n]
        col = lambda i: rt[:, i, :, 0:1]
        TT, TS = V.tensor_tensor, V.tensor_scalar

        def first_max(dst, vals, m, n, desc):
            do(V.tensor_reduce(m, vals, AXX, ALU.max))
            do(TT(T(20, n), vals, bcast(m, [P, NTT, n]), ALU.is_equal))
            do(TT(T(20, n), T(20, n), desc, ALU.mult))
            do(V.tensor_reduce(col(21), T(20, n), AXX, ALU.max))
            do(TT(dst, T(20, n), bcast(col(21), [P, NTT, n]), ALU.is_equal))

        do(TS(rt[:, 19, 0, :], iota_f[:, 0:EG], -1.0, float(EG), ALU.mult, ALU.add))
        desc = lambda n: bcast(rt[:, 19, 0:1, 0:n], [P, NTT, n])
        lg = logits[:, :, 0:NG]
        first_max(T(4, NG), lg, col(5), NG, desc(NG))
        do(TT(T(0, NG), lg, bcast(col(5), [P, NTT, NG]), ALU.subtract))
        le = logits[:, :, NG:].rearrange("p t (g e) -> p t g e", e=EG)
        do(TT(big[:].rearrange("p t (e g) -> p t g e", g=NG), le, bcast(T(4, NG).unsqueeze(3), [P, NTT, NG, EG]), ALU.mult))
        do(V.tensor_reduce(T(6), big[:].rearrange("p t (e g) -> p t e g", g=NG), AXX, ALU.add))
        first_max(T(7), T(6), col(8), EG, desc(EG))
        do(TS(T(9), T(7), NEG, None, ALU.mult))
        do(TT(T(9), T(9), T(6), ALU.add))
        first_max(T(10), T(9), col(11), EG, desc(EG))
        do(TT(col(2), col(11), col(8), ALU.subtract))
        signal(s_rx)
        g4 = bcast(T(4, NG).unsqueeze(3), [P, NTT, NG, EG])
        for dst, src in ((E1, 7), (E2, 10)):
            do(TT(dst[:].rearrange("p t (g e) -> p t g e", e=EG), g4, bcast(T(src).unsqueeze(2), [P, NTT, NG, EG]), ALU.mult))
            do(V.memset(dst[DEC:P, NT, :], 0.0))
        do(TT(E[:], E1[:], E2[:], ALU.add))
        signal(s_E)
        dve.wait_ge(s_ry, 1)
        do(V.tensor_reduce(col(12), T(1, NG), AXX, ALU.add))
        do(TS(col(13), col(3), 1.0, None, ALU.add))
        do(TT(col(13), col(13), col(12), ALU.mult))
        do(V.reciprocal(col(14), col(13)))
        do(TT(col(15), col(14), col(3), ALU.mult))
        dve.wait_ge(s_rank, 1)
        do(V.tensor_copy(big2[:], psum[1][:, 0:NTT * NE].rearrange("p (t e) -> p t e", e=NE)))
        do(V.memset(base[:, 0, :], 0.0))
        for t in range(1, NTT):
            do(TT(base[:, t, :], base[:, t - 1, :], big2[:, t - 1, :], ALU.add))
        do(TT(cnt[:, 0, :], base[:, NT, :], big2[:, NT, :], ALU.add))
        do(TT(base[:], base[:], psum[0][:, 0:NTT * NE].rearrange("p (t e) -> p t e", e=NE), ALU.add))
        do(TS(cmp_[:, 0, 0:MAXOV], iota_f[:, 0:MAXOV], float(P), float(P), ALU.mult, ALU.add))
        do(V.tensor_copy(thr[:], cmp_[:, 0, 0:MAXOV]))
        do(TT(cmp_[:], bcast(cnt[:, 0, :].unsqueeze(2), [P, NE, MAXOV]), bcast(thr[:].unsqueeze(1), [P, NE, MAXOV]), ALU.is_gt))
        do(V.tensor_reduce(cnt[:, 1, :], cmp_[:], AXX, ALU.add))
        src, dst = 1, 2
        k = 1
        do(V.tensor_copy(cnt[:, 2, :], cnt[:, 1, :]))
        src, dst = 2, 3
        while k < NE:
            do(V.tensor_copy(cnt[:, dst, 0:k], cnt[:, src, 0:k]))
            do(TT(cnt[:, dst, k:], cnt[:, src, k:], cnt[:, src, 0:NE - k], ALU.add))
            src, dst = dst, src
            k *= 2
        incl = src
        do(TT(cnt[:, 4, :], cnt[:, incl, :], cnt[:, 1, :], ALU.subtract))
        do(TS(cnt[:, 5, :], iota_f[:, 0:NE], float(P), None, ALU.mult))
        do(TS(cnt[:, 6, :], cnt[:, 4, :], float(NE - 1), float(P), ALU.add, ALU.mult))
        do(TT(cnt[:, 6, :], cnt[:, 6, :], cnt[:, 5, :], ALU.subtract))
        do(TS(big[:], base[:], float(P), None, ALU.is_ge))
        do(TT(big[:], big[:], bcast(cnt[:, 6:7, :], [P, NTT, NE]), ALU.mult))
        do(TT(big[:], big[:], base[:], ALU.add))
        do(TT(big[:], big[:], bcast(cnt[:, 5:6, :], [P, NTT, NE]), ALU.add))
        for kk, Ek in enumerate((E1, E2)):
            do(TT(big2[:], big[:], Ek[:], ALU.mult))
            do(V.tensor_reduce(posf[:, kk, :], big2[:], AXX, ALU.add))
        do(V.tensor_copy(pos_i2[:], posf[:]))
        do(TS(ri[:], pos_i2[:], P - 1, None, ALU.bitwise_and))
        do(TS(bi[:], pos_i2[:], 7, None, ALU.logical_shift_right))
        do(V.tensor_copy(rf[:], ri[:]))
        do(V.tensor_copy(bf[:], bi[:]))
        for kk in range(2):
            do(TT(onehot[:, kk], bcast(iota_f[:].unsqueeze(1), [P, NTT, P]), bcast(rf[:, kk, :].unsqueeze(2), [P, NTT, P]), ALU.is_equal))
            hot = bhot[:, kk, :, 0, :]
            do(TT(hot, bcast(iota_f[:, 0:NB].unsqueeze(1), [P, NTT, NB]), bcast(bf[:, kk, :].unsqueeze(2), [P, NTT, NB]), ALU.is_equal))
            do(TT(bhot[:, kk, :, 1, :], hot, bcast(rt[:, 14 + kk, :, 0:1], [P, NTT, NB]), ALU.mult))
            do(TT(hot, hot, bcast(tok_id[:].unsqueeze(2), [P, NTT, NB]), ALU.mult))
            signal(s_hot)
        do(TT(cmp_[:].rearrange("p e j -> p j e"), bcast(cnt[:, incl, :].unsqueeze(1), [P, MAXOV, NE]),
              bcast(iota_f[:, 0:MAXOV].unsqueeze(2), [P, MAXOV, NE]), ALU.is_le))
        do(V.tensor_reduce(ovf[:, 0:MAXOV], cmp_[:].rearrange("p e j -> p j e"), AXX, ALU.add))
        do(V.tensor_copy(ovf[:, MAXOV:MAXOV + 1], cnt[:, incl, NE - 1:NE]))
        do(V.tensor_copy(ovf_i[:], ovf[:]))
        dve.wait_ge(s_tabp, 1)
        do(V.tensor_copy(rowtok_i[:], psum[2][:, 0:NB]))
        do(V.tensor_copy(roww[:], psum[2][:, NB:2 * NB]))
        signal(s_tab)

        def xT_half(b):
            dve.wait_ge(s_xTp, b + 1)
            V.tensor_copy(xT[:, 0:4, :], psum[0][:].rearrange("p (k n) -> p k n", n=P)).then_inc(s_xTv, 1)
            dve.wait_ge(s_xTv, b + 1)

        def hidden(b):
            dve.wait_ge(s_sg, b + 1)
            if not isinstance(b, int) or b >= 1:
                dve.wait_ge(s_hTp, b)
            V.tensor_tensor(hid[:].rearrange("p (k q) -> p q k", q=P), sg[:].rearrange("p (q k) -> p q k", k=2),
                            psum[3][:, 0:DE].rearrange("p (q k) -> p q k", k=2), ALU.mult).then_inc(s_hid, 1)
            dve.wait_ge(s_hid, b + 1)

        def hidT_(b):
            dve.wait_ge(s_hTp, b + 1)
            if not isinstance(b, int) or b >= 1:
                dve.wait_ge(s_down, b)
            V.tensor_copy(hidT[:], psum[4][:, 0:DE].rearrange("p (k n) -> p k n", n=P)).then_inc(s_hTc, 1)
            dve.wait_ge(s_hTc, b + 1)

        def y_half(b, par, nth):
            dve.wait_ge(s_down, b + 1)
            if nth is not None:
                dve.wait_ge(s_yst[par], nth)
            ww = roww[:, b:b + 1] if isinstance(b, int) else roww[:, bass.ds(b, 1)]
            V.tensor_scalar(yb[:, par, 512:], psum[6][:], ww, None, ALU.mult).then_inc(s_yv, 1)

        xT_half(0)
        hidden(0)
        xT_half(1)
        for b in range(2):
            hidT_(b)
            hidden(b + 1)
            xT_half(b + 2)
            y_half(b, b % 2, None)
        with dve.Fori(0, (NE - SLOTS) // 2) as i:
            for u in range(2):
                b = i * 2 + (2 + u)
                hidT_(b)
                hidden(b + 1)
                xT_half(b + 2)
                y_half(b, u, i * 16 + 16)
        for b in range(NE - 2, NE):
            hidT_(b)
            if b + 1 < NE:
                hidden(b + 1)
            y_half(b, b % 2, 16 * (b // 2))
        n_ov = dve.value_load(ovf_i[0:1, MAXOV:MAXOV + 1], min_val=0, max_val=MAXOV)
        def overflow(j):
            b = j + NE
            xT_half(b)
            hidden(b)
            hidT_(b)
            y_half(b, 0, j * 16 + 16 * (NE // 2))

        overflow_blocks(dve, n_ov, overflow)
        for t in range(NT + 1):
            R = ROWS[t]
            v = prompt_or_sample(t)
            p = t % YBUF
            if t == 0:
                dve.wait_ge(s_x2l, 16 * (NT + 1))
            dve.wait_ge(s_g1[p], 32 * (t // YBUF + 1))
            do(V.tensor_tensor(y1b[:R, p], y1b[:R, p], y2b[:R, p], ALU.add))
            do(V.tensor_tensor(y1b[:R, p], y1b[:R, p], gate_m[:R, v], ALU.mult))
            do(V.tensor_tensor(x2_all[:R, t], y1b[:R, p], x2_all[:R, t], ALU.add))
            signal(s_yo)


_INS = ["x_prompt", "x_sample", "cache_ckv", "cache_krope", "c_prompt", "c_sample", "w_ada", "b_ada", "g_norm_mix", "w_in",
        "g_q_lat", "w_uq", "g_kv_lat", "w_ukv", "g_qnorm", "g_knorm", "g_ln_v", "b_ln_v", "w_spatial", "b_spatial",
        "g_out_attn", "g_out_gmlp", "w_out", "g_norm_ffn", "w_router_group", "b_router_group", "w_router_expert",
        "b_router_expert", "w_gate_e", "w_up_e", "w_down_e"]
_OUTS = [(1, SEQ, D), (1, DEC, D), (1, 1, SEQ, KVL), (1, 1, SEQ, RD), (1, 1, DEC, KVL), (1, 1, DEC, RD), (1, 1, DEC, GW)]


def rope_table():
    half = RD // 2
    inv = (np.float32(1.0) / (np.float32(10000.0) ** (np.arange(half, dtype=np.float32) / np.float32(half)))).astype(np.float32)
    ang = np.arange(SEQ, dtype=np.float32)[:, None] * inv[None, :]
    c, s = np.cos(ang).astype(np.float32), np.sin(ang).astype(np.float32)
    return np.concatenate([c, c, -s, s], axis=1)


def kernel(**inputs):
    import concourse.bacc as bacc
    from concourse.bass_utils import run_bass_kernel_spmd

    nc = bacc.Bacc("TRN2", target_bir_lowering=False, num_devices=1)
    arrays, aps = {}, {}
    for name in _INS:
        x = np.ascontiguousarray(inputs[name])
        arrays[f"in_{name}"] = x
        aps[name] = nc.dram_tensor(f"in_{name}", x.shape, F32, kind="ExternalInput").ap()
    arrays["rope_table"] = rope_table()
    aps["rope_table"] = nc.dram_tensor("rope_table", (SEQ, 2 * RD), F32, kind="ExternalInput").ap()
    outs = [nc.dram_tensor(f"out_{i}", shape, F32, kind="ExternalOutput").ap() for i, shape in enumerate(_OUTS)]
    build(nc, aps, outs)
    r = run_bass_kernel_spmd(nc, [arrays], core_ids=[0])
    return tuple(r.results[0][f"out_{i}"] for i in range(len(_OUTS)))
```
